# Optimizing a Trainium2 kernel written in Bass

```python
import math
import jax, jax.numpy as jnp
from jax import lax
import numpy as np

D_MODEL = 1024
BATCH = 1
SEQ = 256
DEPTH = 2

N_MIXERS = 3
CHUNK = 64
D_FF = 2816
LN_EPS = 1e-5
NORM_EPS = 1e-6
DN_ALPHA = (2 * DEPTH) ** 0.25
DN_BETA = (8 * DEPTH) ** -0.25

GLA_HEADS = 4
GLA_DK = D_MODEL // (2 * GLA_HEADS)
GLA_DV = D_MODEL // GLA_HEADS
GLA_KEY = GLA_HEADS * GLA_DK
GLA_VAL = GLA_HEADS * GLA_DV
GLA_RANK = 16
GLA_TAU = 16.0
GLA_SPLITS = (GLA_KEY, GLA_KEY, GLA_VAL, GLA_VAL, GLA_RANK)

RET_HEADS = 4
RET_DK = D_MODEL // RET_HEADS
RET_DV = 2 * D_MODEL // RET_HEADS
RET_KEY = RET_HEADS * RET_DK
RET_VAL = RET_HEADS * RET_DV
RET_SPLITS = (RET_KEY, RET_KEY, RET_VAL, RET_VAL)
ROPE_BASE = 10000.0

SSD_INNER = 2 * D_MODEL
SSD_HEADDIM = 64
SSD_HEADS = SSD_INNER // SSD_HEADDIM
SSD_GROUPS = 4
SSD_HPG = SSD_HEADS // SSD_GROUPS
SSD_STATE = 128
SSD_CONV = 4
SSD_CONV_DIM = SSD_INNER + 2 * SSD_GROUPS * SSD_STATE
SSD_SPLITS = (SSD_INNER, SSD_CONV_DIM, SSD_HEADS)

N_LAYERS_A = len(range(0, DEPTH, N_MIXERS))
N_LAYERS_B = len(range(1, DEPTH, N_MIXERS))
N_LAYERS_C = len(range(2, DEPTH, N_MIXERS))


def split_cols(t, sizes):
    return jnp.split(t, np.cumsum(sizes)[:-1].tolist(), axis=-1)

def layer_norm(x, g, b):
    xf = x.astype(jnp.float32)
    mu = xf.mean(-1, keepdims=True)
    var = jnp.square(xf - mu).mean(-1, keepdims=True)
    return ((xf - mu) * lax.rsqrt(var + LN_EPS)).astype(x.dtype) * g + b

def rms_norm(x, g):
    xf = x.astype(jnp.float32)
    ms = jnp.square(xf).mean(-1, keepdims=True)
    return (xf * lax.rsqrt(ms + NORM_EPS)).astype(x.dtype) * g

def head_group_norm(x, g):
    xf = x.astype(jnp.float32)
    mu = xf.mean(-1, keepdims=True)
    var = jnp.square(xf - mu).mean(-1, keepdims=True)
    return ((xf - mu) * lax.rsqrt(var + NORM_EPS)).astype(x.dtype) * g

def swiglu(x, w_in, w_out):
    gate, up = jnp.split(x @ w_in, 2, axis=-1)
    return (jax.nn.silu(gate) * up) @ w_out

def to_chunks(t):
    b, l = t.shape[:2]
    t = t.reshape((b, l // CHUNK, CHUNK) + t.shape[2:])
    return jnp.moveaxis(t, 1, 0)

def from_chunks(t):
    t = jnp.moveaxis(t, 0, 1)
    return t.reshape((t.shape[0], t.shape[1] * t.shape[2]) + t.shape[3:])

def rotary(t):
    l, dh = t.shape[1], t.shape[-1]
    inv = ROPE_BASE ** (-jnp.arange(0, dh, 2, dtype=jnp.float32) / dh)
    ang = jnp.arange(l, dtype=jnp.float32)[:, None] * inv[None, :]
    cos = jnp.cos(ang)[None, :, None, :].astype(t.dtype)
    sin = jnp.sin(ang)[None, :, None, :].astype(t.dtype)
    t1, t2 = jnp.split(t, 2, axis=-1)
    return jnp.concatenate([t1 * cos - t2 * sin, t1 * sin + t2 * cos], axis=-1)

def gla_chunked(q, k, v, log_a):
    bsz = q.shape[0]
    mask = jnp.tril(jnp.ones((CHUNK, CHUNK), dtype=bool))

    def step(state, inp):
        qc, kc, vc, ac = inp
        cum = jnp.cumsum(ac, axis=1)
        tot = cum[:, -1]
        q_dec = qc * jnp.exp(cum)
        k_inv = kc * jnp.exp(-cum)
        k_end = kc * jnp.exp(tot[:, None] - cum)
        s = jnp.where(mask, jnp.einsum('bihd,bjhd->bhij', q_dec, k_inv), 0.0)
        o = jnp.einsum('bhij,bjhv->bihv', s, vc) + jnp.einsum('bihd,bhdv->bihv', q_dec, state)
        state = jnp.exp(tot)[..., None] * state + jnp.einsum('bjhd,bjhv->bhdv', k_end, vc)
        return state, o

    state0 = jnp.zeros((bsz, GLA_HEADS, GLA_DK, GLA_DV), jnp.float32)
    _, o = lax.scan(step, state0, (to_chunks(q), to_chunks(k), to_chunks(v), to_chunks(log_a)))
    return from_chunks(o).astype(v.dtype)

def gla_mixer(x, w_in, w_gate, b_gate, norm_g, w_out):
    bsz, l, _ = x.shape
    q, k, v, r, g_low = split_cols(x @ w_in, GLA_SPLITS)
    q = q.reshape(bsz, l, GLA_HEADS, GLA_DK) * GLA_DK ** -0.5
    k = k.reshape(bsz, l, GLA_HEADS, GLA_DK)
    v = v.reshape(bsz, l, GLA_HEADS, GLA_DV)
    log_a = jax.nn.log_sigmoid((g_low @ w_gate + b_gate).astype(jnp.float32)) / GLA_TAU
    log_a = log_a.reshape(bsz, l, GLA_HEADS, GLA_DK)
    o = rms_norm(gla_chunked(q, k, v, log_a), norm_g)
    return (o.reshape(bsz, l, GLA_VAL) * jax.nn.silu(r)) @ w_out

def retention_chunked(q, k, v):
    bsz = q.shape[0]
    log_g = jnp.log(1.0 - 2.0 ** (-5.0 - jnp.arange(RET_HEADS, dtype=jnp.float32)))
    idx = jnp.arange(CHUNK, dtype=jnp.float32)
    mask = jnp.tril(jnp.ones((CHUNK, CHUNK), dtype=bool))
    decay_intra = jnp.where(mask[None], jnp.exp((idx[:, None] - idx[None, :])[None] * log_g[:, None, None]), 0.0)
    decay_q = jnp.exp((idx + 1.0)[:, None] * log_g[None, :])[None, :, :, None]
    decay_k = jnp.exp((CHUNK - 1.0 - idx)[:, None] * log_g[None, :])[None, :, :, None]
    decay_chunk = jnp.exp(CHUNK * log_g)[None, :, None, None]

    def step(state, inp):
        qc, kc, vc = inp
        s = jnp.einsum('bihd,bjhd->bhij', qc, kc) * decay_intra
        o = jnp.einsum('bhij,bjhv->bihv', s, vc) + jnp.einsum('bihd,bhdv->bihv', qc, state) * decay_q
        state = decay_chunk * state + jnp.einsum('bjhd,bjhv->bhdv', kc * decay_k, vc)
        return state, o

    state0 = jnp.zeros((bsz, RET_HEADS, RET_DK, RET_DV), jnp.float32)
    _, o = lax.scan(step, state0, (to_chunks(q), to_chunks(k), to_chunks(v)))
    return from_chunks(o).astype(v.dtype)

def retention_mixer(x, w_in, norm_g, w_out):
    bsz, l, _ = x.shape
    q, k, v, g = split_cols(x @ w_in, RET_SPLITS)
    q = rotary(q.reshape(bsz, l, RET_HEADS, RET_DK))
    k = rotary(k.reshape(bsz, l, RET_HEADS, RET_DK)) * RET_DK ** -0.5
    v = v.reshape(bsz, l, RET_HEADS, RET_DV)
    o = head_group_norm(retention_chunked(q, k, v), norm_g)
    return (o.reshape(bsz, l, RET_VAL) * jax.nn.silu(g)) @ w_out

def causal_dwconv(t, w, b):
    ch = t.shape[-1]
    y = lax.conv_general_dilated(t, w[:, None, :].astype(t.dtype), window_strides=(1,),
                                 padding=[(SSD_CONV - 1, 0)],
                                 dimension_numbers=('NWC', 'WIO', 'NWC'),
                                 feature_group_count=ch)
    return y + b

def ssd_chunked(xs, dt, a, bm, cm):
    bsz = xs.shape[0]
    mask = jnp.tril(jnp.ones((CHUNK, CHUNK), dtype=bool))[None, :, :, None, None]

    def step(state, inp):
        xc, dtc, bc, cc = inp
        cum = jnp.cumsum(dtc * a, axis=1)
        seg = jnp.exp(jnp.where(mask, cum[:, :, None] - cum[:, None, :], -jnp.inf))
        cb = jnp.einsum('bign,bjgn->bijg', cc, bc)
        w = seg * cb[..., None] * dtc[:, None]
        y = jnp.einsum('bijge,bjgep->bigep', w, xc)
        y = y + jnp.einsum('bign,bgepn->bigep', cc, state) * jnp.exp(cum)[..., None]
        to_end = jnp.exp(cum[:, -1:] - cum) * dtc
        state = jnp.exp(cum[:, -1])[..., None, None] * state + jnp.einsum('bjgn,bjge,bjgep->bgepn', bc, to_end, xc)
        return state, y

    state0 = jnp.zeros((bsz, SSD_GROUPS, SSD_HPG, SSD_HEADDIM, SSD_STATE), jnp.float32)
    _, y = lax.scan(step, state0, (to_chunks(xs), to_chunks(dt), to_chunks(bm), to_chunks(cm)))
    return from_chunks(y).astype(xs.dtype)

def ssd_mixer(x, w_in, conv_w, conv_b, dt_bias, a_log, d_skip, norm_g, w_out):
    bsz, l, _ = x.shape
    z, xbc, dt_raw = split_cols(x @ w_in, SSD_SPLITS)
    xbc = jax.nn.silu(causal_dwconv(xbc, conv_w, conv_b))
    xs, bm, cm = split_cols(xbc, (SSD_INNER, SSD_GROUPS * SSD_STATE, SSD_GROUPS * SSD_STATE))
    xs = xs.reshape(bsz, l, SSD_GROUPS, SSD_HPG, SSD_HEADDIM)
    bm = bm.reshape(bsz, l, SSD_GROUPS, SSD_STATE)
    cm = cm.reshape(bsz, l, SSD_GROUPS, SSD_STATE)
    dt = jax.nn.softplus((dt_raw + dt_bias).astype(jnp.float32)).reshape(bsz, l, SSD_GROUPS, SSD_HPG)
    a = -jnp.exp(a_log.astype(jnp.float32)).reshape(SSD_GROUPS, SSD_HPG)
    y = ssd_chunked(xs, dt, a, bm, cm) + xs * d_skip.reshape(SSD_GROUPS, SSD_HPG)[..., None]
    y = y.reshape(bsz, l, SSD_INNER) * jax.nn.silu(z)
    y = rms_norm(y.reshape(bsz, l, SSD_GROUPS, SSD_INNER // SSD_GROUPS), norm_g.reshape(SSD_GROUPS, -1))
    return y.reshape(bsz, l, SSD_INNER) @ w_out

def _col_scale(sizes, scaled):
    return jnp.concatenate([jnp.full((s,), DN_BETA if i in scaled else 1.0, jnp.float32)
                            for i, s in enumerate(sizes)])

def first_inputs(seed: int = 0) -> dict:
    key = jax.random.key(seed)
    ks = list(jax.random.split(key, 24))

    def nrm(i, shape, scale):
        return jax.random.normal(ks[i], shape, jnp.float32) * scale

    x = nrm(0, (BATCH, SEQ, D_MODEL), 1.0)
    ffn_w_in = nrm(1, (DEPTH, 2, D_MODEL, 2 * D_FF), DN_BETA * D_MODEL ** -0.5)
    ffn_w_out = nrm(2, (DEPTH, 2, D_FF, D_MODEL), DN_BETA * D_FF ** -0.5)
    ln_g = 1.0 + nrm(3, (DEPTH, 3, D_MODEL), 0.02)
    ln_b = nrm(4, (DEPTH, 3, D_MODEL), 0.02)
    gla_w_in = nrm(5, (N_LAYERS_A, D_MODEL, sum(GLA_SPLITS)), D_MODEL ** -0.5) * _col_scale(GLA_SPLITS, (2,))
    gla_w_gate = nrm(6, (N_LAYERS_A, GLA_RANK, GLA_KEY), GLA_RANK ** -0.5)
    gla_b_gate = nrm(7, (N_LAYERS_A, GLA_KEY), 0.1)
    gla_norm_g = 1.0 + nrm(8, (N_LAYERS_A, GLA_DV), 0.02)
    gla_w_out = nrm(9, (N_LAYERS_A, GLA_VAL, D_MODEL), DN_BETA * GLA_VAL ** -0.5)
    ret_w_in = nrm(10, (N_LAYERS_B, D_MODEL, sum(RET_SPLITS)), D_MODEL ** -0.5) * _col_scale(RET_SPLITS, (2,))
    ret_norm_g = 1.0 + nrm(11, (N_LAYERS_B, RET_DV), 0.02)
    ret_w_out = nrm(12, (N_LAYERS_B, RET_VAL, D_MODEL), DN_BETA * RET_VAL ** -0.5)
    ssd_cols = (SSD_INNER, SSD_INNER, SSD_CONV_DIM - SSD_INNER, SSD_HEADS)
    ssd_w_in = nrm(13, (N_LAYERS_C, D_MODEL, sum(SSD_SPLITS)), D_MODEL ** -0.5) * _col_scale(ssd_cols, (1,))
    ssd_conv_w = nrm(14, (N_LAYERS_C, SSD_CONV, SSD_CONV_DIM), SSD_CONV ** -0.5)
    ssd_conv_b = nrm(15, (N_LAYERS_C, SSD_CONV_DIM), 0.02)
    dt0 = jnp.exp(jax.random.uniform(ks[16], (N_LAYERS_C, SSD_HEADS), jnp.float32,
                                     math.log(1e-3), math.log(1e-1)))
    ssd_dt_bias = dt0 + jnp.log(-jnp.expm1(-dt0))
    ssd_a_log = jnp.log(jax.random.uniform(ks[17], (N_LAYERS_C, SSD_HEADS), jnp.float32, 1.0, 16.0))
    ssd_d = 1.0 + nrm(18, (N_LAYERS_C, SSD_HEADS), 0.02)
    ssd_norm_g = 1.0 + nrm(19, (N_LAYERS_C, SSD_INNER), 0.02)
    ssd_w_out = nrm(20, (N_LAYERS_C, SSD_INNER, D_MODEL), DN_BETA * SSD_INNER ** -0.5)
    return {'x': x, 'ffn_w_in': ffn_w_in, 'ffn_w_out': ffn_w_out, 'ln_g': ln_g, 'ln_b': ln_b,
            'gla_w_in': gla_w_in, 'gla_w_gate': gla_w_gate, 'gla_b_gate': gla_b_gate,
            'gla_norm_g': gla_norm_g, 'gla_w_out': gla_w_out,
            'ret_w_in': ret_w_in, 'ret_norm_g': ret_norm_g, 'ret_w_out': ret_w_out,
            'ssd_w_in': ssd_w_in, 'ssd_conv_w': ssd_conv_w, 'ssd_conv_b': ssd_conv_b,
            'ssd_dt_bias': ssd_dt_bias, 'ssd_a_log': ssd_a_log, 'ssd_d': ssd_d,
            'ssd_norm_g': ssd_norm_g, 'ssd_w_out': ssd_w_out}

def first_block(x, ffn_w_in, ffn_w_out, ln_g, ln_b,
              gla_w_in, gla_w_gate, gla_b_gate, gla_norm_g, gla_w_out,
              ret_w_in, ret_norm_g, ret_w_out,
              ssd_w_in, ssd_conv_w, ssd_conv_b, ssd_dt_bias, ssd_a_log, ssd_d, ssd_norm_g, ssd_w_out):
    h = x
    for i in range(DEPTH):
        h = layer_norm(DN_ALPHA * h + 0.5 * swiglu(h, ffn_w_in[i, 0], ffn_w_out[i, 0]), ln_g[i, 0], ln_b[i, 0])
        kind, j = i % N_MIXERS, i // N_MIXERS
        if kind == 0:
            m = gla_mixer(h, gla_w_in[j], gla_w_gate[j], gla_b_gate[j], gla_norm_g[j], gla_w_out[j])
        elif kind == 1:
            m = retention_mixer(h, ret_w_in[j], ret_norm_g[j], ret_w_out[j])
        else:
            m = ssd_mixer(h, ssd_w_in[j], ssd_conv_w[j], ssd_conv_b[j], ssd_dt_bias[j],
                          ssd_a_log[j], ssd_d[j], ssd_norm_g[j], ssd_w_out[j])
        h = layer_norm(DN_ALPHA * h + m, ln_g[i, 1], ln_b[i, 1])
        h = layer_norm(DN_ALPHA * h + 0.5 * swiglu(h, ffn_w_in[i, 1], ffn_w_out[i, 1]), ln_g[i, 2], ln_b[i, 2])
    return h


DEPTH_2 = 1

HEAD_DIM = 64
N_HEADS_MIX = 8
BRANCH_WIDTH = N_HEADS_MIX * HEAD_DIM
N_BRANCHES = 3
IDX_HEADS = 16
IDX_DIM = 64
TOPK_MAX = 256
Q_BLOCK = 128
D_FF_2 = 4 * D_MODEL
DEEPNORM_ALPHA = (2.0 * DEPTH_2) ** 0.25
DEEPNORM_BETA = (8.0 * DEPTH_2) ** -0.25
FORGET_BIAS_MEAN = 3.0

IN_SIZES = (
    BRANCH_WIDTH, BRANCH_WIDTH, BRANCH_WIDTH,
    IDX_HEADS * IDX_DIM, IDX_DIM, IDX_HEADS,
    BRANCH_WIDTH, BRANCH_WIDTH, BRANCH_WIDTH,
    N_HEADS_MIX,
    BRANCH_WIDTH, BRANCH_WIDTH, BRANCH_WIDTH,
    N_BRANCHES * D_MODEL,
)
V_SECTIONS = (2, 8, 12)
IN_COLS = sum(IN_SIZES)


def _layer_norm(x, g, b):
    xf = x.astype(jnp.float32)
    mu = jnp.mean(xf, axis=-1, keepdims=True)
    xc = xf - mu
    var = jnp.mean(xc * xc, axis=-1, keepdims=True)
    y = xc * lax.rsqrt(var + LN_EPS) * g.astype(jnp.float32) + b.astype(jnp.float32)
    return y.astype(x.dtype)

def _alibi_slopes(n):
    return 2.0 ** (-8.0 * jnp.arange(1, n + 1, dtype=jnp.float32) / n)

def _to_blocks(a):
    b, s = a.shape[:2]
    a = a.reshape((b, s // Q_BLOCK, Q_BLOCK) + a.shape[2:])
    return jnp.moveaxis(a, 1, 0)

def _from_blocks(a):
    a = jnp.moveaxis(a, 0, 1)
    b, nb, qb = a.shape[:3]
    return a.reshape(b, nb * qb, -1)

def _dsa_attention(q, k, v, q_idx, k_idx, w_idx, slopes):
    s_len = q.shape[1]
    topk = min(TOPK_MAX, s_len // 4)
    pos = jnp.arange(s_len)
    scale = HEAD_DIM ** -0.5

    def block(args):
        qb, qib, wb, tq = args
        dots = jnp.einsum('bqhd,bkd->bqhk', qib, k_idx, preferred_element_type=jnp.float32)
        score = jnp.einsum('bqhk,bqh->bqk', jax.nn.relu(dots), wb.astype(jnp.float32))
        causal = pos[None, :] <= tq[:, None]
        score = jnp.where(causal[None], score, -jnp.inf)
        _, idx = lax.top_k(score, topk)
        valid = idx <= tq[None, :, None]
        k_sel = jax.vmap(lambda kb, ib: kb[ib])(k, idx)
        v_sel = jax.vmap(lambda vb, ib: vb[ib])(v, idx)
        logits = jnp.einsum('bqhd,bqkhd->bhqk', qb, k_sel, preferred_element_type=jnp.float32) * scale
        dist = (tq[None, :, None] - idx).astype(jnp.float32)
        logits = logits - slopes[None, :, None, None] * dist[:, None]
        logits = jnp.where(valid[:, None], logits, -jnp.inf)
        p = jax.nn.softmax(logits, axis=-1).astype(v.dtype)
        return jnp.einsum('bhqk,bqkhd->bqhd', p, v_sel)

    out = lax.map(block, (_to_blocks(q), _to_blocks(q_idx), _to_blocks(w_idx), pos.reshape(-1, Q_BLOCK)))
    return _from_blocks(out)

def _forgetting_attention(q, k, v, log_f):
    s_len = q.shape[1]
    pos = jnp.arange(s_len)
    scale = HEAD_DIM ** -0.5
    c = jnp.cumsum(log_f, axis=1)
    c_k = jnp.transpose(c, (0, 2, 1))[:, :, None, :]

    def block(args):
        qb, cq, tq = args
        logits = jnp.einsum('bqhd,bkhd->bhqk', qb, k, preferred_element_type=jnp.float32) * scale
        logits = logits + jnp.transpose(cq, (0, 2, 1))[..., None] - c_k
        causal = pos[None, :] <= tq[:, None]
        logits = jnp.where(causal[None, None], logits, -jnp.inf)
        p = jax.nn.softmax(logits, axis=-1).astype(v.dtype)
        return jnp.einsum('bhqk,bkhd->bqhd', p, v)

    out = lax.map(block, (_to_blocks(q), _to_blocks(c), pos.reshape(-1, Q_BLOCK)))
    return _from_blocks(out)

def _stick_breaking_attention(q, k, v):
    s_len = q.shape[1]
    pos = jnp.arange(s_len)
    scale = HEAD_DIM ** -0.5

    def block(args):
        qb, tq = args
        z = jnp.einsum('bqhd,bkhd->bhqk', qb, k, preferred_element_type=jnp.float32) * scale
        strict = (pos[None, :] < tq[:, None])[None, None]
        log_beta = jax.nn.log_sigmoid(z)
        log_one_minus = jnp.where(strict, jax.nn.log_sigmoid(-z), 0.0)
        later = lax.cumsum(log_one_minus, axis=3, reverse=True) - log_one_minus
        a = jnp.where(strict, jnp.exp(log_beta + later), 0.0).astype(v.dtype)
        return jnp.einsum('bhqk,bkhd->bqhd', a, v)

    out = lax.map(block, (_to_blocks(q), pos.reshape(-1, Q_BLOCK)))
    return _from_blocks(out)

def second_inputs(seed: int = 0) -> dict:
    key = jax.random.key(seed)
    ks = jax.random.split(key, 12)
    x = jax.random.normal(ks[0], (BATCH, SEQ, D_MODEL), jnp.float32)
    sec_keys = jax.random.split(ks[1], len(IN_SIZES))
    secs = []
    for i, size in enumerate(IN_SIZES):
        sc = D_MODEL ** -0.5 * (DEEPNORM_BETA if i in V_SECTIONS else 1.0)
        secs.append(jax.random.normal(sec_keys[i], (DEPTH_2, D_MODEL, size), jnp.float32) * sc)
    w_in = jnp.concatenate(secs, axis=-1)
    b_forget = FORGET_BIAS_MEAN + 0.5 * jax.random.normal(ks[2], (DEPTH_2, N_HEADS_MIX), jnp.float32)
    w_branch = jax.random.normal(ks[3], (DEPTH_2, N_BRANCHES, BRANCH_WIDTH, D_MODEL), jnp.float32) * (BRANCH_WIDTH ** -0.5 * DEEPNORM_BETA)
    w_out = jax.random.normal(ks[4], (DEPTH_2, D_MODEL, D_MODEL), jnp.float32) * (D_MODEL ** -0.5 * DEEPNORM_BETA)
    ln1_g = 1.0 + 0.05 * jax.random.normal(ks[5], (DEPTH_2, D_MODEL), jnp.float32)
    ln1_b = 0.02 * jax.random.normal(ks[6], (DEPTH_2, D_MODEL), jnp.float32)
    w_ff1 = jax.random.normal(ks[7], (DEPTH_2, D_MODEL, D_FF_2), jnp.float32) * (D_MODEL ** -0.5 * DEEPNORM_BETA)
    w_ff2 = jax.random.normal(ks[8], (DEPTH_2, D_FF_2, D_MODEL), jnp.float32) * (D_FF_2 ** -0.5 * DEEPNORM_BETA)
    ln2_g = 1.0 + 0.05 * jax.random.normal(ks[9], (DEPTH_2, D_MODEL), jnp.float32)
    ln2_b = 0.02 * jax.random.normal(ks[10], (DEPTH_2, D_MODEL), jnp.float32)
    return {'x': x, 'w_in': w_in, 'b_forget': b_forget, 'w_branch': w_branch, 'w_out': w_out,
            'ln1_g': ln1_g, 'ln1_b': ln1_b, 'w_ff1': w_ff1, 'w_ff2': w_ff2,
            'ln2_g': ln2_g, 'ln2_b': ln2_b}

def second_block(x, w_in, b_forget, w_branch, w_out, ln1_g, ln1_b, w_ff1, w_ff2, ln2_g, ln2_b):
    b, s, _ = x.shape
    slopes = _alibi_slopes(N_HEADS_MIX)
    split_at = [int(v) for v in np.cumsum(IN_SIZES)[:-1]]

    def heads(a):
        return a.reshape(b, s, N_HEADS_MIX, HEAD_DIM)

    for layer in range(DEPTH_2):
        proj = jnp.einsum('bsd,dc->bsc', x, w_in[layer])
        (qa, ka, va, qi, ki, wi, qf, kf, vf, fg, qs, ks_, vs, gates) = jnp.split(proj, split_at, axis=-1)
        o_a = _dsa_attention(heads(qa), heads(ka), heads(va),
                             qi.reshape(b, s, IDX_HEADS, IDX_DIM), ki, wi, slopes)
        log_f = jax.nn.log_sigmoid((fg + b_forget[layer]).astype(jnp.float32))
        o_b = _forgetting_attention(heads(qf), heads(kf), heads(vf), log_f)
        o_c = _stick_breaking_attention(heads(qs), heads(ks_), heads(vs))
        branches = jnp.stack([o_a, o_b, o_c], axis=0)
        up = jnp.einsum('ibsw,iwd->bsid', branches, w_branch[layer])
        g = jax.nn.sigmoid(gates.reshape(b, s, N_BRANCHES, D_MODEL))
        merged = jnp.sum(up * g, axis=2)
        y = jnp.einsum('bsd,de->bse', merged, w_out[layer])
        x = _layer_norm(DEEPNORM_ALPHA * x + y, ln1_g[layer], ln1_b[layer])
        h = jnp.square(jax.nn.relu(jnp.einsum('bsd,df->bsf', x, w_ff1[layer])))
        y = jnp.einsum('bsf,fd->bsd', h, w_ff2[layer])
        x = _layer_norm(DEEPNORM_ALPHA * x + y, ln2_g[layer], ln2_b[layer])
    return x


def setup_inputs(seed=0):
    out = dict(first_inputs(seed))
    for name, value in second_inputs(seed + 1).items():
        if name != "x":
            out[name + "_2"] = value
    return out


def reference(
    x, ffn_w_in, ffn_w_out, ln_g, ln_b, gla_w_in, gla_w_gate, gla_b_gate, gla_norm_g, gla_w_out,
    ret_w_in, ret_norm_g, ret_w_out, ssd_w_in, ssd_conv_w, ssd_conv_b, ssd_dt_bias, ssd_a_log,
    ssd_d, ssd_norm_g, ssd_w_out, w_in_2, b_forget_2, w_branch_2, w_out_2, ln1_g_2, ln1_b_2,
    w_ff1_2, w_ff2_2, ln2_g_2, ln2_b_2,
):
    x = first_block(
        x, ffn_w_in, ffn_w_out, ln_g, ln_b, gla_w_in, gla_w_gate, gla_b_gate, gla_norm_g,
        gla_w_out, ret_w_in, ret_norm_g, ret_w_out, ssd_w_in, ssd_conv_w, ssd_conv_b,
        ssd_dt_bias, ssd_a_log, ssd_d, ssd_norm_g, ssd_w_out,
    )
    return second_block(
        x, w_in_2, b_forget_2, w_branch_2, w_out_2, ln1_g_2, ln1_b_2, w_ff1_2, w_ff2_2, ln2_g_2,
        ln2_b_2,
    )


_drawn_inputs = setup_inputs


def setup_inputs(seed=0):
    import zlib

    import numpy as np

    out = dict(_drawn_inputs(seed))
    spreads = {}
    factors = {'gla_b_gate': 5.616,
     'gla_norm_g': 8.0,
     'ret_norm_g': 24.624,
     'b_forget_2': 64.0,
     'ln1_b_2': 2.925,
     'ln2_b_2': 2.869}
    for name, (base, spread) in spreads.items():
        noise = np.random.default_rng([zlib.crc32(name.encode()), seed]).standard_normal(out[name].shape)
        drawn = base * np.exp(spread * noise) if base else spread * noise
        out[name] = __import__('jax').numpy.asarray(drawn.astype(out[name].dtype))
    for name, factor in factors.items():
        out[name] = (out[name] * factor).astype(out[name].dtype)
    return out
```

```python
from contextlib import ExitStack

import concourse.bass as bass
import numpy as np
from concourse import mybir

F32 = mybir.dt.float32
F32R = mybir.dt.float32r
U32 = mybir.dt.uint32
ALU = mybir.AluOpType
ACT = mybir.ActivationFunctionType
AX_X = mybir.AxisListType.X

P = 128
D = 1024
TOK = 256
TB = TOK // P
KC = D // P
NCOL = 512
TILE = 2048
RING = 3

D_FF = 2816
FFN_STEPS = D_FF // 256
GLA_HEADS, GLA_DK, GLA_DV, GLA_RANK, GLA_TAU = 4, 128, 256, 16, 16.0
CHUNK = 64
RET_HEADS, RET_DK, RET_DV = 4, 256, 512
HEADS, HEAD_DIM = 8, 64
IDX_HEADS = 16
TOPK = 64
FF2 = 4096
FF2_STEPS = FF2 // 512
ALPHA = 4.0 ** 0.25
ALPHA_2 = 2.0 ** 0.25
LN_EPS, NORM_EPS = 1e-5, 1e-6
NEG = -3.0e38
TAKEN = -3.4e38
CAUSAL = P + TOK

FFN_TILES = 3 * FFN_STEPS
GLA_UNITS, RET_UNITS, SEC_UNITS = 6, 12, 11
N_FFN0 = 0
N_GLA = N_FFN0 + FFN_TILES
N_GLA_OUT = N_GLA + 2 * GLA_UNITS
N_FFN1 = N_GLA_OUT + 4
N_FFN2 = N_FFN1 + FFN_TILES
N_RET = N_FFN2 + FFN_TILES
N_RET_OUT = N_RET + 2 * RET_UNITS
N_FFN3 = N_RET_OUT + 8
N_SEC = N_FFN3 + FFN_TILES
N_MERGE = N_SEC + 2 * SEC_UNITS
N_SEC_OUT = N_MERGE + 18
N_FF2 = N_SEC_OUT + 4
N_TILES = N_FF2 + 4 * FF2_STEPS


def build(nc, io):
    ctx = ExitStack()
    with ctx:
        def sb(name, shape, dt=F32, where=ctx):
            return where.enter_context(nc.sbuf_tensor(name, shape, dt))

        def sem(name):
            return ctx.enter_context(nc.semaphore(name))

        raw = sb("weights_raw", [P, RING, TILE])
        w_hi = sb("weights_hi", [P, RING, TILE], F32R)
        w_lo = sb("weights_lo", [P, RING, TILE], F32R)
        x_hi = sb("operand_hi", [P, KC, TOK], F32R)
        x_lo = sb("operand_lo", [P, KC, TOK], F32R)
        xn = sb("normalised", [P, TB, D])
        resid = sb("residual", [P, TB, D])
        ln_rows = sb("ln_rows", [P, 2, D])
        ln_cols = sb("ln_cols", [P, 9, 2, KC])
        cst = sb("constants", [P, 4, P])
        ident, tri, later_of, ones = (cst[:, i, :] for i in range(4))
        affine_tmp = sb("affine_tmp", [P, 2, 2 * TOK])
        stats = sb("stats", [P, 8, 6])
        mv = sb("mean_var", [P, 8, 2])
        rstd = sb("rstd", [P, 8])
        minus_half = sb("minus_half", [P, 8])
        bank = ctx.enter_context(nc.psum_tensor("psum", [P, 8, NCOL], F32))
        acc = bank[:, 0:4, :]
        work = bank[:, 4:8, :]

        with ExitStack() as ph:
            silu_g = sb("silu_gate", [P, TB, 256], F32, ph)
            hid = sb("hidden", [P, TB, 512], F32, ph)
            hid_hi = sb("hidden_hi", [P, 4, TOK], F32R, ph)
            hid_lo = sb("hidden_lo", [P, 4, TOK], F32R, ph)
        with ExitStack() as ph:
            g_qT = sb("gla_qT", [P, GLA_HEADS, TOK], F32, ph)
            g_kT = sb("gla_kT", [P, GLA_HEADS, TOK], F32, ph)
            g_v = sb("gla_v", [P, TB, D], F32, ph)
            g_r = sb("gla_r", [P, TB, D], F32, ph)
            g_z = sb("gla_z", [P, GLA_HEADS, TOK], F32, ph)
            g_t = sb("gla_t", [P, GLA_HEADS, TOK], F32, ph)
            g_cum = sb("gla_cum", [P, GLA_HEADS, TOK], F32, ph)
            g_up = sb("gla_exp_cum", [P, GLA_HEADS, TOK], F32, ph)
            g_dn = sb("gla_exp_minus_cum", [P, GLA_HEADS, TOK], F32, ph)
            g_end = sb("gla_exp_to_end", [P, GLA_HEADS, TOK], F32, ph)
            g_kend = sb("gla_k_end", [P, TB, GLA_HEADS * GLA_DK], F32, ph)
            g_s = sb("gla_scores", [P, TB, GLA_HEADS, P], F32, ph)
            g_state = sb("gla_state", [P, 3, GLA_HEADS, GLA_DV], F32, ph)
            g_low = sb("gla_low", [GLA_RANK, TOK], F32, ph)
            g_tail = sb("gla_w_low", [P, KC, GLA_RANK], F32, ph)
            g_wg = sb("gla_w_gate", [GLA_RANK, GLA_HEADS * GLA_DK], F32, ph)
            g_bg = sb("gla_b_gate", [P, GLA_HEADS], F32, ph)
            g_gain = sb("gla_gain", [P, GLA_DV], F32, ph)
            g_cst = sb("gla_constants", [P, TOK + GLA_HEADS * P], F32, ph)
            g_ss = sb("gla_sumsq", [P, 8], F32, ph)
            g_junk = sb("gla_junk", [P, GLA_DV], F32, ph)
            chunk_keep = g_cst[:, 0:TOK]
            chunk_mask = g_cst[:, TOK:TOK + GLA_HEADS * P]
        with ExitStack() as ph:
            r_qk = sb("ret_qkT", [P, 2, KC, TOK], F32, ph)
            r_v = sb("ret_v", [P, TB, 2 * D], F32, ph)
            r_g = sb("ret_g", [P, TB, 2 * D], F32, ph)
            r_rot = sb("ret_rot", [P, 2, 2, 2, TOK], F32, ph)
            r_after = r_rot[:, :, :, :, :].rearrange("p a b c t -> p (a b c t)")
            r_s = r_after[:, 0:RET_HEADS * CAUSAL].rearrange("p (h c) -> p h c", h=RET_HEADS)
            r_gain = r_after[:, RET_HEADS * CAUSAL:RET_HEADS * CAUSAL + RET_DV]
            r_lo = sb("ret_out_lo", [P, 2 * KC, TOK], F32R, ph)
            r_hi2 = sb("ret_out_hi", [P, KC, TOK], F32R, ph)
            r_cst = sb("ret_constants", [P, 2 * TOK + RET_HEADS * CAUSAL], F32, ph)
            r_o = r_qk[:, :, :, :].rearrange("p a c t -> p a (c t)")
            cos, sin = r_cst[:, 0:TOK], r_cst[:, TOK:2 * TOK]
            decay = r_cst[:, 2 * TOK:].rearrange("p (h c) -> p h c", h=RET_HEADS)
        with ExitStack() as ph:
            a_q = sb("att_qT", [P, 2, 4, TOK], F32, ph)
            a_k = sb("att_kT", [P, 2, 4, TOK], F32, ph)
            a_v = sb("att_v", [P, 3, TB, HEADS * HEAD_DIM], F32, ph)
            a_ki = sb("att_kiT", [P, TOK], F32, ph)
            a_wf = sb("att_wi_fg", [P, TB, IDX_HEADS + HEADS], F32, ph)
            a_bf = sb("att_b_forget", [P, HEADS], F32, ph)
            a_lf = sb("att_log_f", [P, 3, TB, HEADS], F32, ph)
            a_cT = sb("att_cT", [HEADS, 2, TOK], F32, ph)
            a_cst = sb("att_constants", [P, 3, CAUSAL], F32, ph)
            a_sc = sb("att_score", [P, 2, CAUSAL], F32, ph)
            a_top = sb("att_top8", [P, 8], F32, ph)
            a_max = sb("att_max", [P, 2, TB, HEADS], F32, ph)
            a_sum = sb("att_sum", [P, TB, HEADS], F32, ph)
            a_p = sb("att_p", [P, HEADS, CAUSAL], F32, ph)
            a_pt = sb("att_pT", [P, HEADS, CAUSAL], F32, ph)
            causal, negdist, strict = (a_cst[:, i, :] for i in range(3))
            with ExitStack() as sub:
                a_tail = sb("att_w_small", [P, KC, P + IDX_HEADS + HEADS], F32, sub)
                a_qi = sb("att_qiT", [P, 8, TOK], F32, sub)
            a_oh = sb("att_out_hi", [P, 12, TOK], F32R, ph)
            a_ol = sb("att_out_lo", [P, 12, TOK], F32R, ph)
            relu = a_pt[:, :, :].rearrange("p h c -> p (h c)")[:, 0:2048].rearrange("p (b c) -> p b c", b=2)
            sig = a_p[:, :, :].rearrange("p h c -> p (h c)")[:, 0:2048].rearrange("p (b t c) -> p b t c", b=2, t=TB)
            upg = a_pt[:, :, :].rearrange("p h c -> p (h c)")[:, 0:2048].rearrange("p (b t c) -> p b t c", b=2, t=TB)
            merged = xn

        weight_loaded = [sem(f"weight_loaded{i}") for i in range(RING)]
        hi_split = sem("hi_split")
        lo_split = sem("lo_split")
        weights_used = sem("weights_used")
        pair_free = [sem("pair_free0"), sem("pair_free1")]
        x_loaded, consts_loaded = sem("x_loaded"), sem("consts_loaded")
        eps_ready = sem("eps_ready")
        var_ready, rstd_ready = sem("var_ready"), sem("rstd_ready")
        xn_ready, resid_ready = sem("xn_ready"), sem("resid_ready")
        rows_loaded = sem("rows_loaded")
        turned, turned_hi, operand_ready = sem("turned"), sem("turned_hi"), sem("operand_ready")
        affine_done = sem("affine_done")
        silu_done, hid_done = sem("silu_done"), sem("hid_done")
        hid_turned, hid_hi_done, hid_ready = sem("hid_turned"), sem("hid_hi_done"), sem("hid_ready")
        dve_step, pool_step, act_step = sem("dve_step"), sem("pool_step"), sem("act_step")
        out_ready, out_stored = sem("out_ready"), sem("out_stored")
        gla_loaded, ret_loaded, att_loaded = sem("gla_loaded"), sem("ret_loaded"), sem("att_loaded")
        low_ready, low_copied, z_ready = sem("low_ready"), sem("low_copied"), sem("z_ready")
        naz_ready, ln1p_ready, cum_ready = sem("naz_ready"), sem("ln1p_ready"), sem("cum_ready")
        exp_ready, dec_ready = sem("exp_ready"), sem("dec_ready")
        kend_turned, kend_copied = sem("kend_turned"), sem("kend_copied")
        gs_ready, gs_masked = sem("gs_ready"), sem("gs_masked")
        upd_ready, state_ready, gla_o = sem("upd_ready"), sem("state_ready"), sem("gla_o")
        ss_ready, gate_ready, mixed = sem("ss_ready"), sem("gate_ready"), sem("mixed")
        rot_ready, rope_done = sem("rot_ready"), sem("rope_done")
        rs_ready, rs_decayed, ret_o = sem("rs_ready"), sem("rs_decayed"), sem("ret_o")
        unit_copied = sem("unit_copied")
        small_ready, small_copied = sem("small_ready"), sem("small_copied")
        dots_ready, relu_done, dots_used = sem("dots_ready"), sem("relu_done"), sem("dots_used")
        lf_exp, lf_ln, lf_ready, cum_f, cT_copied = sem("lf_exp"), sem("lf_ln"), sem("lf_ready"), sem("cum_f"), sem("cT_copied")
        lf_in = sem("lf_in")
        logits_ready, max_ready, exp_done, p_ready = sem("logits_ready"), sem("max_ready"), sem("exp_done"), sem("p_ready")
        p_turned, pt_act, pt_dve = sem("p_turned"), sem("pt_act"), sem("pt_dve")
        o_ready, o_hi_done, o_done = sem("o_ready"), sem("o_hi_done"), sem("o_done")
        sb_z, sb_ln, sb_l, sb_later, sb_t, sb_exp, sb_a = (
            sem(n) for n in ("sb_z", "sb_ln", "sb_l", "sb_later", "sb_t", "sb_exp", "sb_a"))
        sig_done, up_used, merged_ready = sem("sig_done"), sem("up_used"), sem("merged_ready")

        pairs = [work[:, 0:2, :], work[:, 2:4, :]]
        slot_of = lambda n: n % RING

        order = ["ln1", "gla", "ln2", "ln3", "ln4", "ret", "ln5", "ln6", "mrg", "ln7"]
        turns, at = {"x": 0}, KC // 2
        for what in order:
            turns[what] = at
            at += KC if what == "ret" else KC // 2

        affine_base = {w: (KC // 2) * i for i, w in enumerate(["x"] + [w for w in order if w[0:2] == "ln"])}

        block = ctx.enter_context(nc.Block())

        @block.sync
        def _(sp):
            def load(n, i=0):
                s = slot_of(n)
                src = io["weights"][n + RING * i] if isinstance(i, int) else io["weights"][bass.ds(n + RING * i, 1)]
                if not isinstance(i, int):
                    src = src.rearrange("a p n -> (a p) n")
                return src

            for n in range(RING):
                sp.dma_start(raw[:, n, :], io["weights"][n]).then_inc(weight_loaded[n], 16)
            rounds = (N_TILES - RING) // RING
            with sp.Fori(0, rounds) as i:
                for n in range(RING, 2 * RING):
                    src = io["weights"][bass.ds(sp.snap(i * RING + n), 1)].rearrange("a p n -> (a p) n")
                    sp.wait_ge(lo_split, i * RING + (n - RING + 1))
                    sp.dma_start(raw[:, n % RING, :], src).then_inc(weight_loaded[n % RING], 16)
            for n in range(RING * (rounds + 1), N_TILES):
                sp.wait_ge(lo_split, n - RING + 1)
                sp.dma_start(raw[:, n % RING, :], io["weights"][n]).then_inc(weight_loaded[n % RING], 16)
            for tb in range(TB):
                sp.wait_ge(out_ready, tb + 1)
                sp.dma_start(io["out"][tb], resid[:, tb, :]).then_inc(out_stored, 16)
            sp.wait_ge(out_stored, 16 * TB)

        @block.gpsimd
        def _(pool):
            step = [0]

            def link(ins):
                step[0] += 1
                ins.then_inc(pool_step, 1)
                pool.wait_ge(pool_step, step[0])

            powers = [0]

            def inverse_root(out, var, scale, eps, n):
                powers[0] += 1
                pool.wait_ge(var_ready, powers[0])
                link(nc.gpsimd.tensor_scalar(out, var, scale, eps, ALU.mult, ALU.add))
                nc.gpsimd.tensor_tensor(out, out, minus_half[:, 0:n], ALU.pow).then_inc(rstd_ready, 1)

            link(nc.gpsimd.memset(minus_half[:, :], -0.5))
            pool.wait_ge(x_loaded, 16 * TB)
            nc.gpsimd.tensor_scalar(resid[:, :, :], xn[:, :, :], ALPHA, 0.0, ALU.mult, ALU.add).then_inc(resid_ready, 1)

            def layer_norm(ln):
                for tb in range(TB):
                    inverse_root(rstd[:, tb:tb + 1], mv[:, tb, 1:2], 1.0, LN_EPS, 1)
                for j in range(2):
                    pool.dma_start(ln_rows[:, j, :], io["ln_rows"][2 * (ln - 1) + j:2 * (ln - 1) + j + 1, :]
                                   .to_broadcast([P, D])).then_inc(rows_loaded, 16)
                if ln == 8:
                    return
                pool.wait_ge(rows_loaded, 32 * ln)
                pool.wait_ge(xn_ready, TB * ln)
                for tb in range(TB):
                    link(nc.gpsimd.tensor_tensor(resid[:, tb, :], xn[:, tb, :], ln_rows[:, 0, :], ALU.mult))
                    link(nc.gpsimd.tensor_tensor(resid[:, tb, :], resid[:, tb, :], ln_rows[:, 1, :], ALU.add))
                last = nc.gpsimd.tensor_scalar(resid[:, :, :], resid[:, :, :], ALPHA if ln < 6 else ALPHA_2, 0.0,
                                               ALU.mult, ALU.add)
                last.then_inc(resid_ready, 1)
                pool.wait_ge(resid_ready, ln + 1)

            layer_norm(1)
            pool.wait_ge(gla_loaded, 16 * 5)
            pool.wait_ge(unit_copied, 1)
            for tb in range(TB):
                for h in range(GLA_HEADS):
                    cols = slice(h * GLA_DV, (h + 1) * GLA_DV)
                    last = nc.gpsimd.tensor_tensor(g_r[:, tb, cols], g_r[:, tb, cols], g_gain[:, :], ALU.mult)
            last.then_inc(gate_ready, 1)
            inverse_root(rstd[:, 0:8], g_ss[:, :], 1.0 / GLA_DV, NORM_EPS, 8)
            layer_norm(2)
            layer_norm(3)
            layer_norm(4)
            for u in range(4):
                for j in range(2):
                    pool.wait_ge(rot_ready, 2 * u + j + 1)
                    head = 2 * (u % 2) + j
                    qk = r_qk[:, u // 2, 2 * head:2 * head + 2, :]
                    by_cos, by_sin = r_rot[:, j, 0], r_rot[:, j, 1]
                    nc.gpsimd.tensor_tensor(qk[:, 0, :], by_cos[:, 0, :], by_sin[:, 1, :], ALU.subtract)
                    nc.gpsimd.tensor_tensor(qk[:, 1, :], by_sin[:, 0, :], by_cos[:, 1, :], ALU.add).then_inc(rope_done, 1)
            pool.wait_ge(ret_loaded, 32)
            pool.wait_ge(unit_copied, 2)
            for tb in range(TB):
                for h in range(RET_HEADS):
                    cols = slice(h * RET_DV, (h + 1) * RET_DV)
                    last = nc.gpsimd.tensor_tensor(r_g[:, tb, cols], r_g[:, tb, cols], r_gain, ALU.mult)
            last.then_inc(gate_ready, 1)
            for tb in range(TB):
                inverse_root(rstd[:, 4 * tb:4 * tb + 4], mv[:, 4 * tb:4 * tb + 4, 1], 1.0, NORM_EPS, 4)
            layer_norm(5)
            layer_norm(6)
            layer_norm(7)
            layer_norm(8)

        @block.scalar
        def _(act):
            step = [0]

            def link(ins):
                step[0] += 1
                ins.then_inc(act_step, 1)
                act.wait_ge(act_step, step[0])

            def split_hi(n, i=0):
                if n >= N_TILES:
                    return
                s = slot_of(n)
                act.wait_ge(weight_loaded[s], i * 16 + 16 * (n // RING + 1))
                if n >= RING:
                    act.wait_ge(weights_used, i * RING + (n - RING + 1))
                nc.scalar.activation(w_hi[:, s, :], raw[:, s, :], ACT.Copy).then_inc(hi_split, 1)

            def turn_hi(what, affine, hi, first=0):
                base = turns[what] + first
                for b in range(KC // 2):
                    if affine:
                        act.wait_ge(affine_done, affine_base[what] + b + 1)
                        src = affine_tmp[:, b % 2, :]
                    else:
                        act.wait_ge(turned, base + b + 1)
                        src = work[:, b, :]
                    nc.scalar.activation(hi[:, 2 * b:2 * b + 2, :].rearrange("p c t -> p (c t)"), src,
                                         ACT.Copy).then_inc(turned_hi, 1)

            def ffn(n0, f):
                def silu(n, i=0):
                    act.wait_ge(weights_used, i * RING + n + 2)
                    nc.scalar.activation(silu_g[:, :, :], work[:, 0:2, 0:256], ACT.Silu).then_inc(silu_done, 1)

                def hidden_hi(j, i=0):
                    act.wait_ge(hid_turned, i + j + 1)
                    nc.scalar.activation(hid_hi[:, 0:2, :], work[:, 2, :].rearrange("p (c t) -> p c t", c=2), ACT.Copy).then_inc(hid_hi_done, 1)

                j0 = f * FFN_STEPS
                split_hi(n0 + 3)
                silu(n0)
                split_hi(n0 + 4)
                with act.Fori(0, FFN_STEPS - 1) as i:
                    hidden_hi(j0, i)
                    split_hi(n0 + 5, i)
                    silu(n0 + 2, i)
                    split_hi(n0 + 6, i)
                    split_hi(n0 + 7, i)
                hidden_hi(j0 + FFN_STEPS - 1)
                split_hi(n0 + FFN_TILES + 2)

            def unit(n, u, out, func=ACT.Copy, scale=1.0):
                split_hi(n + 3)
                act.wait_ge(weights_used, n + 2)
                src = pairs[u % 2]
                ins = nc.scalar.activation(out, src, func, scale=scale)
                ins.then_inc(pair_free[u % 2], 1)
                split_hi(n + 4)

            for tb in range(TB):
                act.dma_start(xn[:, tb, :], io["x"][tb]).then_inc(x_loaded, 16)
            act.dma_start(cst[:, :, :], io["constants"]).then_inc(consts_loaded, 16)
            act.dma_start(ln_cols[:, :, :, :], io["ln_cols"]).then_inc(consts_loaded, 16)
            act.wait_ge(consts_loaded, 32)
            turn_hi("x", True, x_hi)
            for n in range(RING):
                split_hi(n)
            ffn(N_FFN0, 0)
            turn_hi("ln1", True, x_hi)

            for dst, name in ((g_tail, "gla_w_low"), (g_wg, "gla_w_gate"), (g_bg, "gla_b_gate"),
                              (g_cst, "gla_constants")):
                act.dma_start(dst[tuple([slice(None)] * len(dst.shape))], io[name]).then_inc(gla_loaded, 16)
            act.dma_start(g_gain[:, :], io["gla_gain"].to_broadcast([P, GLA_DV])).then_inc(gla_loaded, 16)
            n = N_GLA
            act.wait_ge(low_ready, 1)
            nc.scalar.activation(g_low[:, :], acc[0:GLA_RANK, 0, 0:TOK], ACT.Copy).then_inc(low_copied, 1)
            flat = lambda t: t.rearrange("p h t -> p (h t)")
            as_pair = lambda t: t.rearrange("p (a b) t -> p a (b t)", a=2)
            unit(n, 0, as_pair(g_qT[:, :, :]), scale=GLA_DK ** -0.5)
            act.wait_ge(naz_ready, 1)
            link(nc.scalar.activation(g_t[:, :, :], g_t[:, :, :], ACT.Exp))
            nc.scalar.activation(g_t[:, :, :], g_t[:, :, :], ACT.Ln, bias=1.0).then_inc(ln1p_ready, 1)
            unit(n + 2, 1, as_pair(g_kT[:, :, :]))
            act.wait_ge(cum_ready, 1)
            nc.scalar.activation(g_up[:, :, :], g_cum[:, :, :], ACT.Exp, scale=1.0 / GLA_TAU)
            nc.scalar.activation(g_dn[:, :, :], g_cum[:, :, :], ACT.Exp, scale=-1.0 / GLA_TAU)
            nc.scalar.activation(g_end[:, :, :], g_end[:, :, :], ACT.Exp, scale=1.0 / GLA_TAU).then_inc(exp_ready, 1)
            unit(n + 4, 2, g_v[:, :, 0:512])
            unit(n + 6, 3, g_v[:, :, 512:1024])
            for tb in range(TB):
                act.wait_ge(kend_turned, tb + 1)
                nc.scalar.activation(g_kend[:, tb, :], acc[:, 3 * tb, :], ACT.Copy).then_inc(kend_copied, 1)
            unit(n + 8, 4, g_r[:, :, 0:512], ACT.Silu)
            unit(n + 10, 5, g_r[:, :, 512:1024], ACT.Silu)
            act.wait_ge(pair_free[1], 3)
            act.sem_inc(unit_copied, 1)
            for tb in range(TB):
                act.wait_ge(gla_o, tb + 1)
                for h in range(GLA_HEADS):
                    src = acc[:, 2 * tb + h // 2, (h % 2) * GLA_DV:(h % 2 + 1) * GLA_DV]
                    link(nc.scalar.activation(g_junk[:, :], src, ACT.Square,
                                              accum_out=g_ss[:, 4 * tb + h:4 * tb + h + 1]))
            act.sem_inc(var_ready, 1)
            turn_hi("gla", False, x_hi)
            for j in range(4):
                split_hi(N_GLA_OUT + j + 3)
            turn_hi("ln2", True, x_hi)
            ffn(N_FFN1, 1)
            turn_hi("ln3", True, x_hi)
            ffn(N_FFN2, 2)
            turn_hi("ln4", True, x_hi)

            act.dma_start(r_cst[:, :], io["ret_constants"]).then_inc(ret_loaded, 16)
            n = N_RET
            for u in range(4):
                split_hi(n + 3)
                split_hi(n + 4)
                n += 2
            act.wait_ge(rope_done, 8)
            act.dma_start(r_gain, io["ret_gain"].to_broadcast([P, RET_DV])).then_inc(ret_loaded, 16)
            for u in range(4, 8):
                unit(n, u, r_v[:, :, (u - 4) * 512:(u - 3) * 512])
                n += 2
            for u in range(8, 12):
                unit(n, u, r_g[:, :, (u - 8) * 512:(u - 7) * 512], ACT.Silu)
                n += 2
            act.wait_ge(pair_free[1], 9)
            act.sem_inc(unit_copied, 1)
            turn_hi("ret", False, x_hi)
            turn_hi("ret", False, r_hi2, KC // 2)
            for j in range(8):
                split_hi(N_RET_OUT + j + 3)
            turn_hi("ln5", True, x_hi)
            ffn(N_FFN3, 3)
            turn_hi("ln6", True, x_hi)

            act.dma_start(a_tail[:, :, :], io["att_w_small"]).then_inc(att_loaded, 16)
            act.dma_start(a_cst[:, :, :], io["att_constants"]).then_inc(att_loaded, 16)
            act.dma_start(a_bf[:, :], io["b_forget"].to_broadcast([P, HEADS])).then_inc(att_loaded, 16)
            n = N_SEC
            unit(n, 0, as_pair(a_qi[:, 0:4, :]))
            unit(n + 2, 1, as_pair(a_qi[:, 4:8, :]))
            act.wait_ge(small_ready, 1)
            nc.scalar.activation(a_ki[:, :], acc[:, 0, 0:TOK], ACT.Copy)
            nc.scalar.activation(a_wf[:, :, :], acc[:, 1, 0:64].rearrange("p (t c) -> p t c", t=TB)[:, :, 0:24],
                                 ACT.Copy).then_inc(small_copied, 1)
            unit(n + 4, 2, as_pair(a_q[:, 0]), scale=HEAD_DIM ** -0.5)
            unit(n + 6, 3, as_pair(a_k[:, 0]))
            act.wait_ge(lf_in, 1)
            link(nc.scalar.activation(a_lf[:, 1], a_lf[:, 1], ACT.Exp))
            nc.scalar.activation(a_lf[:, 1], a_lf[:, 1], ACT.Ln, bias=1.0).then_inc(lf_ln, 1)
            for p in range(6):
                act.wait_ge(dots_ready, p + 1)
                if p >= 2:
                    act.wait_ge(dots_used, p - 1)
                nc.scalar.activation(relu[:, p % 2, :].rearrange("p (b c) -> p b c", b=2),
                                     acc[:, 2 * (p % 2):2 * (p % 2) + 2, :], ACT.Relu).then_inc(relu_done, 1)
            unit(n + 8, 4, a_v[:, 0])
            unit(n + 10, 5, as_pair(a_q[:, 1]), scale=HEAD_DIM ** -0.5)
            act.wait_ge(cum_f, 1)
            nc.scalar.activation(a_cT[:, 0, :], acc[0:HEADS, 0, 0:TOK], ACT.Copy)
            nc.scalar.activation(a_cT[:, 1, :], acc[0:HEADS, 0, 0:TOK], ACT.Copy, scale=-1.0).then_inc(cT_copied, 1)
            unit(n + 12, 6, as_pair(a_k[:, 1]))
            unit(n + 14, 7, a_v[:, 1])

            def softmax_exp(br):
                for g, (tb, heads) in enumerate(((1, range(0, 4)), (1, range(4, 8)), (0, range(8)))):
                    act.wait_ge(max_ready, 3 * br + g + 1)
                    cols = slice(P, CAUSAL) if tb else slice(0, P)
                    for h in heads:
                        ins = nc.scalar.activation(a_p[:, h, cols], a_p[:, h, cols], ACT.Exp,
                                                   bias=a_max[:, 1, tb, h:h + 1],
                                                   accum_out=a_sum[:, tb, h:h + 1])
                    ins.then_inc(exp_done, 1)

            def pt_copy(br):
                for h in range(0, HEADS, 2):
                    act.wait_ge(p_turned, 8 * br + h + 1)
                    nc.scalar.activation(a_pt[:, h, :], acc[:, h % 4, 0:CAUSAL], ACT.Copy).then_inc(pt_act, 1)

            def out_hi(br):
                act.wait_ge(o_ready, br + 1)
                nc.scalar.activation(a_oh[:, 4 * br:4 * br + 4, :].rearrange("p (a b) t -> p a (b t)", a=2),
                                     acc[:, 0:2, :], ACT.Copy).then_inc(o_hi_done, 1)

            softmax_exp(0)
            unit(n + 16, 8, as_pair(a_q[:, 0]), scale=HEAD_DIM ** -0.5)
            pt_copy(0)
            out_hi(0)
            unit(n + 18, 9, as_pair(a_k[:, 0]))
            softmax_exp(1)
            unit(n + 20, 10, a_v[:, 2])
            pt_copy(1)
            out_hi(1)
            for r in range(2):
                rows = slice(4 * r, 4 * r + 4)
                act.wait_ge(sb_z, r + 1)
                link(nc.scalar.activation(a_pt[:, rows, :], acc[:, 0:4, 0:CAUSAL], ACT.Abs))
                link(nc.scalar.activation(a_pt[:, rows, :], a_pt[:, rows, :], ACT.Exp, scale=-1.0))
                nc.scalar.activation(a_pt[:, rows, :], a_pt[:, rows, :], ACT.Ln, bias=1.0).then_inc(sb_ln, 1)
                act.wait_ge(sb_t, r + 1)
                nc.scalar.activation(a_p[:, rows, :], a_p[:, rows, :], ACT.Exp).then_inc(sb_exp, 1)
            out_hi(2)

            with act.Fori(0, 2) as half:
                for b in range(3):
                    m = N_MERGE + 3 * b
                    split_hi(m + 3, 3 * half)
                    act.wait_ge(weights_used, half * 9 + m + 2)
                    if b == 2:
                        act.wait_ge(up_used, half * 3 + 1)
                    nc.scalar.activation(sig[:, b % 2, :, :], pairs[(b + 1) % 2], ACT.Sigmoid).then_inc(sig_done, 1)
                    split_hi(m + 4, 3 * half)
                    split_hi(m + 5, 3 * half)
            turn_hi("mrg", False, x_hi)
            for j in range(4):
                split_hi(N_SEC_OUT + j + 3)
            turn_hi("ln7", True, x_hi)

            j0 = 4 * FFN_STEPS

            def relu_up(n, i=0):
                act.wait_ge(weights_used, i * 12 + n + 2)
                nc.scalar.activation(hid[:, :, :], work[:, 0:2, :], ACT.Relu).then_inc(silu_done, 1)

            def hidden2_hi(j, i=0):
                act.wait_ge(hid_turned, i * 3 + j + 1)
                nc.scalar.activation(hid_hi[:, :, :].rearrange("p (a b) t -> p a (b t)", a=2), work[:, 2:4, :],
                                     ACT.Copy).then_inc(hid_hi_done, 1)

            def ff2_step(n, j, i=0):
                hidden2_hi(j, i)
                split_hi(n + 3, 4 * i)
                relu_up(n, i)
                split_hi(n + 4, 4 * i)
                split_hi(n + 5, 4 * i)
                split_hi(n + 6, 4 * i)

            split_hi(N_FF2 + 3)
            relu_up(N_FF2)
            split_hi(N_FF2 + 4)
            with act.Fori(0, 2) as i:
                for s in range(3):
                    ff2_step(N_FF2 + 2 + 4 * s, j0 + s, i)
            ff2_step(N_FF2 + 26, j0 + 6)
            hidden2_hi(j0 + 7)

        @block.vector
        def _(dve):
            step = [0]

            def mark(ins):
                step[0] += 1
                ins.then_inc(dve_step, 1)
                return step[0]

            def link(ins):
                dve.wait_ge(dve_step, mark(ins))

            def split_lo(n, i=0):
                if n >= N_TILES:
                    return
                s = slot_of(n)
                dve.wait_ge(hi_split, i * RING + (n + 1))
                nc.vector.tensor_tensor(w_lo[:, s, :], raw[:, s, :], w_hi[:, s, :].bitcast(F32),
                                        ALU.subtract).then_inc(lo_split, 1)

            def turn_lo(what, ln, hi, lo, first=0):
                base = turns[what] + first

                def affine(b):
                    dve.wait_ge(turned, base + b + 1)
                    for c in (2 * b, 2 * b + 1):
                        at = (c % 2) * TOK
                        last = nc.vector.tensor_scalar(affine_tmp[:, b % 2, at:at + TOK], work[:, b, at:at + TOK],
                                                       ln_cols[:, ln, 0, c:c + 1], ln_cols[:, ln, 1, c:c + 1],
                                                       ALU.mult, ALU.add)
                    last.then_inc(affine_done, 1)

                if ln is not None:
                    affine(0)
                for b in range(KC // 2):
                    if ln is not None and b + 1 < KC // 2:
                        if b >= 1:
                            dve.wait_ge(operand_ready, base + b)
                        affine(b + 1)
                    dve.wait_ge(turned_hi, base + b + 1)
                    pair = lambda t: t[:, 2 * b:2 * b + 2, :].rearrange("p c t -> p (c t)")
                    nc.vector.tensor_tensor(pair(lo), work[:, b, :] if ln is None else affine_tmp[:, b % 2, :],
                                            pair(hi).bitcast(F32), ALU.subtract).then_inc(operand_ready, 1)

            def layer_norm(ln, used, scale):
                dve.wait_ge(weights_used, used)
                dve.wait_ge(resid_ready, ln)
                sums = []
                for tb in range(TB):
                    sums.append(mark(nc.vector.scalar_tensor_tensor(
                        out=xn[:, tb, :], in0=acc[:, 2 * tb:2 * tb + 2, :].rearrange("p a b -> p (a b)"), scalar=scale,
                        in1=resid[:, tb, :], op0=ALU.mult, op1=ALU.add)))
                for tb in range(TB):
                    dve.wait_ge(dve_step, sums[tb])
                    nc.vector.bn_stats(stats[:, 2 * tb, :], xn[:, tb, 0:512])
                    link(nc.vector.bn_stats(stats[:, 2 * tb + 1, :], xn[:, tb, 512:1024]))
                    nc.vector.bn_aggr(mv[:, tb, :], stats[:, 2 * tb:2 * tb + 2, :]).then_inc(var_ready, 1)
                for tb in range(TB):
                    count[0] += 1
                    dve.wait_ge(rstd_ready, count[0])
                    nc.vector.tensor_scalar(xn[:, tb, :], xn[:, tb, :], mv[:, tb, 0:1], rstd[:, tb:tb + 1],
                                            ALU.subtract, ALU.mult).then_inc(xn_ready, 1)

            count = [0]

            def ffn(n0, f):
                j0 = f * FFN_STEPS

                def hidden(j, i=0):
                    dve.wait_ge(silu_done, i + j + 1)
                    nc.vector.tensor_tensor(hid[:, :, 0:256], silu_g[:, :, :], work[:, 0:2, 256:512],
                                            ALU.mult).then_inc(hid_done, 1)

                def hidden_lo(j, i=0):
                    dve.wait_ge(hid_hi_done, i + j + 1)
                    nc.vector.tensor_tensor(hid_lo[:, 0:2, :], work[:, 2, :].rearrange("p (c t) -> p c t", c=2), hid_hi[:, 0:2, :].bitcast(F32),
                                            ALU.subtract).then_inc(hid_ready, 1)

                split_lo(n0 + 3)
                hidden(j0)
                split_lo(n0 + 4)
                with dve.Fori(0, FFN_STEPS - 1) as i:
                    hidden_lo(j0, i)
                    split_lo(n0 + 5, i)
                    hidden(j0 + 1, i)
                    split_lo(n0 + 6, i)
                    split_lo(n0 + 7, i)
                hidden_lo(j0 + FFN_STEPS - 1)
                split_lo(n0 + FFN_TILES + 2)

            dve.wait_ge(consts_loaded, 32)
            turn_lo("x", 0, x_hi, x_lo)
            for n in range(RING):
                split_lo(n)
            ffn(N_FFN0, 0)
            layer_norm(1, N_GLA, 0.5)
            turn_lo("ln1", 1, x_hi, x_lo)

            n = N_GLA
            dve.wait_ge(gla_loaded, 16 * 5)
            link(nc.vector.memset(g_s[:, :, :, :], 0.0))
            split_lo(n + 3)
            split_lo(n + 4)
            dve.wait_ge(z_ready, 1)
            for h in range(GLA_HEADS):
                last = nc.vector.tensor_scalar(g_z[:, h, :], acc[:, 1 + h // 2, (h % 2) * TOK:(h % 2 + 1) * TOK],
                                               g_bg[:, h:h + 1], None, ALU.add)
            link(last)
            nc.vector.scalar_tensor_tensor(out=g_t[:, :, :], in0=g_z[:, :, :], scalar=-1.0, in1=g_z[:, :, :],
                                           op0=ALU.mult, op1=ALU.min).then_inc(naz_ready, 1)
            split_lo(n + 5)
            dve.wait_ge(ln1p_ready, 1)
            link(nc.vector.scalar_tensor_tensor(out=g_z[:, :, :], in0=g_z[:, :, :], scalar=0.0, in1=g_t[:, :, :],
                                                op0=ALU.min, op1=ALU.subtract))
            for h in range(GLA_HEADS):
                last = nc.vector.tensor_tensor_scan(g_cum[:, h, :], chunk_keep, g_z[:, h, :], 0.0, ALU.mult, ALU.add)
            link(last)
            cum_c = g_cum[:, :, :].rearrange("p h (c t) -> p (h c) t", t=CHUNK)
            nc.vector.tensor_tensor(g_end[:, :, :].rearrange("p h (c t) -> p (h c) t", t=CHUNK),
                                    cum_c[:, :, CHUNK - 1:CHUNK].to_broadcast([P, 16, CHUNK]), cum_c,
                                    ALU.subtract).then_inc(cum_ready, 1)
            split_lo(n + 6)
            dve.wait_ge(exp_ready, 1)
            nc.vector.tensor_tensor(g_qT[:, :, :], g_qT[:, :, :], g_up[:, :, :], ALU.mult)
            nc.vector.tensor_tensor(g_end[:, :, :], g_kT[:, :, :], g_end[:, :, :], ALU.mult)
            nc.vector.tensor_tensor(g_dn[:, :, :], g_kT[:, :, :], g_dn[:, :, :], ALU.mult).then_inc(dec_ready, 1)
            for j in range(7, 12):
                split_lo(n + j)
                if j == 10:
                    for tb in range(TB):
                        dve.wait_ge(gs_ready, tb + 1)
                        nc.vector.copy_predicated(g_s[:, tb].rearrange("p h i -> p (h i)"), chunk_mask.bitcast(U32),
                                                  acc[:, 1 + tb, :]).then_inc(gs_masked, 1)
            for j in range(12, 15):
                split_lo(n + j)
            for c in range(3):
                dve.wait_ge(upd_ready, c + 1)
                src = pairs[c % 2].rearrange("p a (b v) -> p (a b) v", b=2)
                if c == 0:
                    link(nc.vector.tensor_copy(g_state[:, 0], src))
                else:
                    for h in range(GLA_HEADS):
                        end = c * CHUNK + CHUNK - 1
                        last = nc.vector.scalar_tensor_tensor(out=g_state[:, c, h, :], in0=g_state[:, c - 1, h, :],
                                                              scalar=g_up[:, h, end:end + 1], in1=src[:, h, :],
                                                              op0=ALU.mult, op1=ALU.add)
                    link(last)
                dve.sem_inc(state_ready, 1)
            count[0] += 1
            dve.wait_ge(rstd_ready, count[0])
            dve.wait_ge(gate_ready, 1)
            for tb in range(TB):
                for h in range(GLA_HEADS):
                    cols = slice(h * GLA_DV, (h + 1) * GLA_DV)
                    last = nc.vector.scalar_tensor_tensor(
                        out=g_v[:, tb, cols], in0=acc[:, 2 * tb + h // 2, (h % 2) * GLA_DV:(h % 2 + 1) * GLA_DV],
                        scalar=rstd[:, 4 * tb + h:4 * tb + h + 1], in1=g_r[:, tb, cols], op0=ALU.mult, op1=ALU.mult)
                last.then_inc(mixed, 1)
            turn_lo("gla", None, x_hi, x_lo)
            for j in range(4):
                split_lo(N_GLA_OUT + j + 3)
            layer_norm(2, N_FFN1, 1.0)
            turn_lo("ln2", 2, x_hi, x_lo)
            ffn(N_FFN1, 1)
            layer_norm(3, N_FFN2, 0.5)
            turn_lo("ln3", 3, x_hi, x_lo)
            ffn(N_FFN2, 2)
            layer_norm(4, N_RET, 0.5)
            turn_lo("ln4", 4, x_hi, x_lo)

            n = N_RET
            dve.wait_ge(ret_loaded, 16)
            for u in range(4):
                split_lo(n + 3)
                dve.wait_ge(weights_used, n + 2)
                for j in range(2):
                    if u:
                        dve.wait_ge(rope_done, 2 * (u - 1) + j + 1)
                    src = pairs[u % 2][:, j, :].rearrange("p (b t) -> p b t", b=2)
                    nc.vector.tensor_tensor(r_rot[:, j, 0], src, cos.rearrange("p (b t) -> p b t", b=1)
                                            .to_broadcast([P, 2, TOK]), ALU.mult)
                    last = nc.vector.tensor_tensor(r_rot[:, j, 1], src, sin.rearrange("p (b t) -> p b t", b=1)
                                                   .to_broadcast([P, 2, TOK]), ALU.mult)
                    last.then_inc(rot_ready, 1)
                dve.wait_ge(rot_ready, 2 * u + 2)
                dve.sem_inc(pair_free[u % 2], 1)
                split_lo(n + 4)
                n += 2
            for u in range(4, 12):
                split_lo(n + 3)
                split_lo(n + 4)
                n += 2
                if u == 4:
                    for h in range(RET_HEADS):
                        dve.wait_ge(rs_ready, h + 1)
                        nc.vector.tensor_tensor(r_s[:, h, :], acc[:, h, 0:CAUSAL], decay[:, h, :],
                                                ALU.mult).then_inc(rs_decayed, 1)
            for tb in range(TB):
                dve.wait_ge(ret_o, tb + 1)
                o = work if tb == 0 else acc
                for h in range(RET_HEADS):
                    last = nc.vector.bn_stats(stats[:, 4 * tb + h, :], o[:, h, :])
                link(last)
                for h in range(RET_HEADS):
                    last = nc.vector.bn_aggr(mv[:, 4 * tb + h, :], stats[:, 4 * tb + h, :])
                last.then_inc(var_ready, 1)
            dve.wait_ge(gate_ready, 2)
            for tb in range(TB):
                o = work if tb == 0 else acc
                count[0] += 1
                dve.wait_ge(rstd_ready, count[0])
                for h in range(RET_HEADS):
                    i = 4 * tb + h
                    cols = slice(h * RET_DV, (h + 1) * RET_DV)
                    last = nc.vector.tensor_scalar(r_o[:, tb, cols], o[:, h, :], mv[:, i, 0:1], rstd[:, i:i + 1],
                                                   ALU.subtract, ALU.mult)
                link(last)
                nc.vector.tensor_tensor(r_o[:, tb, :], r_o[:, tb, :], r_g[:, tb, :], ALU.mult).then_inc(mixed, 1)
            turn_lo("ret", None, x_hi, r_lo[:, 0:KC, :])
            turn_lo("ret", None, r_hi2, r_lo[:, KC:2 * KC, :], KC // 2)
            for j in range(8):
                split_lo(N_RET_OUT + j + 3)
            layer_norm(5, N_FFN3, 1.0)
            turn_lo("ln5", 5, x_hi, x_lo)
            ffn(N_FFN3, 3)
            layer_norm(6, N_SEC, 0.5)
            turn_lo("ln6", 6, x_hi, x_lo)

            n = N_SEC
            dve.wait_ge(att_loaded, 48)
            for j in range(3, 11):
                split_lo(n + j)
            dve.wait_ge(small_copied, 1)
            link(nc.vector.tensor_tensor(a_lf[:, 0], a_wf[:, :, IDX_HEADS:],
                                         a_bf[:, :].rearrange("p (t h) -> p t h", t=1).to_broadcast([P, TB, HEADS]), ALU.add))
            nc.vector.scalar_tensor_tensor(out=a_lf[:, 1], in0=a_lf[:, 0], scalar=-1.0, in1=a_lf[:, 0],
                                           op0=ALU.mult, op1=ALU.min).then_inc(lf_in, 1)
            for p in range(6):
                dve.wait_ge(relu_done, p + 1)
                tb = 1 if p < 4 else 0
                width = TOK if tb else P
                per = NCOL // width
                cols = slice(P, CAUSAL) if tb else slice(0, P)
                for b in range(2):
                    for s in range(per):
                        h = (4 * p if tb else 8 * (p - 4)) + 2 * s + b
                        src = relu[:, p % 2, b * NCOL + s * width:b * NCOL + (s + 1) * width]
                        if h == 0:
                            link(nc.vector.tensor_scalar(a_sc[:, 0, cols], src, a_wf[:, tb, h:h + 1], None, ALU.mult))
                        else:
                            link(nc.vector.scalar_tensor_tensor(out=a_sc[:, 0, cols], in0=src, scalar=a_wf[:, tb, h:h + 1],
                                                                in1=a_sc[:, 0, cols], op0=ALU.mult, op1=ALU.add))
                dve.sem_inc(dots_used, 1)
                if p == 0:
                    dve.wait_ge(lf_ln, 1)
                    nc.vector.scalar_tensor_tensor(out=a_lf[:, 2], in0=a_lf[:, 0], scalar=0.0, in1=a_lf[:, 1],
                                                   op0=ALU.min, op1=ALU.subtract).then_inc(lf_ready, 1)
            link(nc.vector.tensor_tensor(a_sc[:, 0, :], a_sc[:, 0, :], causal, ALU.add))
            split_lo(n + 11)
            for tb, cols in ((1, slice(P, CAUSAL)), (0, slice(0, P))):
                for r in range(TOPK // 8):
                    link(nc.vector.max(out=a_top[:, :], in_=a_sc[:, 0, cols]))
                    link(nc.vector.match_replace(out=a_sc[:, 0, cols], in_to_replace=a_top[:, :],
                                                 in_values=a_sc[:, 0, cols], imm_value=TAKEN))
                    if r == 3:
                        split_lo(n + 12 + 2 * (1 - tb))
                split_lo(n + 13 + 2 * (1 - tb))
            link(nc.vector.tensor_scalar(a_sc[:, 0, :], a_sc[:, 0, :], TAKEN, NEG, ALU.not_equal, ALU.mult))
            link(nc.vector.tensor_tensor(a_sc[:, 0, :], a_sc[:, 0, :], causal, ALU.min))
            for j in range(16, 19):
                split_lo(n + j)

            groups = ((1, range(0, 4)), (1, range(4, 8)), (0, range(8)))

            def logits(br):
                for g, (tb, heads) in enumerate(groups):
                    dve.wait_ge(logits_ready, 3 * br + g + 1)
                    width = TOK if tb else P
                    cols = slice(P, CAUSAL) if tb else slice(0, P)
                    if br == 0:
                        for h in heads:
                            last = nc.vector.scalar_tensor_tensor(
                                out=a_p[:, h, cols], in0=negdist[:, cols], scalar=2.0 ** -(h + 1), in1=a_sc[:, 0, cols],
                                op0=ALU.mult, op1=ALU.add)
                        link(last)
                    for h in heads:
                        b, s = h % 2, (h - heads[0]) // 2
                        src = acc[:, 2 * (g % 2) + b, s * width:(s + 1) * width]
                        last = nc.vector.tensor_tensor_reduce(
                            out=a_p[:, h, cols], in0=src, in1=a_p[:, h, cols] if br == 0 else causal[:, cols],
                            scale=1.0, scalar=-3.4e38, op0=ALU.add, op1=ALU.max, accum_out=a_max[:, 0, tb, h:h + 1])
                    link(last)
                    nc.vector.tensor_scalar(a_max[:, 1, tb, heads[0]:heads[-1] + 1], a_max[:, 0, tb, heads[0]:heads[-1] + 1],
                                            -1.0, None, ALU.mult).then_inc(max_ready, 1)

            def normalise(br):
                for g, (tb, heads) in enumerate(groups):
                    dve.wait_ge(exp_done, 3 * br + g + 1)
                    cols = slice(P, CAUSAL) if tb else slice(0, P)
                    hs = slice(heads[0], heads[-1] + 1)
                    link(nc.vector.reciprocal(a_sum[:, tb, hs], a_sum[:, tb, hs]))
                    for h in heads:
                        last = nc.vector.tensor_scalar(a_p[:, h, cols], a_p[:, h, cols], a_sum[:, tb, h:h + 1], None, ALU.mult)
                    last.then_inc(p_ready, 1)

            def pt_copy(br):
                for h in range(1, HEADS, 2):
                    dve.wait_ge(p_turned, 8 * br + h + 1)
                    nc.vector.tensor_copy(a_pt[:, h, :], acc[:, h % 4, 0:CAUSAL]).then_inc(pt_dve, 1)

            def out_lo(br):
                dve.wait_ge(o_hi_done, br + 1)
                nc.vector.tensor_tensor(a_ol[:, 4 * br:4 * br + 4, :].rearrange("p (a b) t -> p a (b t)", a=2),
                                        acc[:, 0:2, :],
                                        a_oh[:, 4 * br:4 * br + 4, :].rearrange("p (a b) t -> p a (b t)", a=2).bitcast(F32),
                                        ALU.subtract).then_inc(o_done, 1)

            logits(0)
            normalise(0)
            split_lo(n + 19)
            split_lo(n + 20)
            pt_copy(0)
            out_lo(0)
            split_lo(n + 21)
            split_lo(n + 22)
            logits(1)
            normalise(1)
            split_lo(n + 23)
            split_lo(n + 24)
            pt_copy(1)
            out_lo(1)
            for r in range(2):
                rows = slice(4 * r, 4 * r + 4)
                z = acc[:, 0:4, 0:CAUSAL]
                dve.wait_ge(sb_ln, r + 1)
                link(nc.vector.scalar_tensor_tensor(out=a_p[:, rows, :], in0=z, scalar=0.0, in1=a_pt[:, rows, :],
                                                    op0=ALU.min, op1=ALU.subtract))
                link(nc.vector.tensor_tensor(a_pt[:, rows, :], a_p[:, rows, :], z, ALU.subtract))
                mask = strict.rearrange("p (h c) -> p h c", h=1).to_broadcast([P, 4, CAUSAL])
                nc.vector.tensor_tensor(a_pt[:, rows, :], a_pt[:, rows, :], mask, ALU.mult).then_inc(sb_l, 1)
                dve.wait_ge(sb_later, r + 1)
                nc.vector.tensor_tensor(a_p[:, rows, :], a_p[:, rows, :], z, ALU.add).then_inc(sb_t, 1)
                dve.wait_ge(sb_exp, r + 1)
                nc.vector.tensor_tensor(a_p[:, rows, :], a_p[:, rows, :], mask, ALU.mult).then_inc(sb_a, 1)
            out_lo(2)

            dve.wait_ge(resid_ready, 7)
            with dve.Fori(0, 2) as half:
                for b in range(3):
                    m = N_MERGE + 3 * b
                    split_lo(m + 3, 3 * half)
                    split_lo(m + 4, 3 * half)
                    dve.wait_ge(sig_done, half * 3 + b + 1)
                    dve.wait_ge(weights_used, half * 9 + m + 3)
                    dst = merged[:, :, bass.ds(half * NCOL, NCOL)]
                    up = acc[:, 2 * (b % 2):2 * (b % 2) + 2, :]
                    nc.vector.tensor_tensor(dst if b == 0 else upg[:, b % 2], sig[:, b % 2], up, ALU.mult).then_inc(up_used, 1)
                    if b:
                        dve.wait_ge(up_used, half * 3 + b + 1)
                        if b == 2:
                            dve.wait_ge(merged_ready, half * 2 + 1)
                        nc.vector.tensor_tensor(dst, dst, upg[:, b % 2], ALU.add).then_inc(merged_ready, 1)
                    split_lo(m + 5, 3 * half)
            turn_lo("mrg", None, x_hi, x_lo)
            for j in range(4):
                split_lo(N_SEC_OUT + j + 3)
            layer_norm(7, N_FF2, 1.0)
            turn_lo("ln7", 7, x_hi, x_lo)

            j0 = 4 * FFN_STEPS

            def square(j, i=0):
                dve.wait_ge(silu_done, i * 3 + j + 1)
                nc.vector.tensor_tensor(hid[:, :, :], hid[:, :, :], hid[:, :, :], ALU.mult).then_inc(hid_done, 1)

            def hidden2_lo(j, i=0):
                dve.wait_ge(hid_hi_done, i * 3 + j + 1)
                pair = lambda t: t[:, :, :].rearrange("p (a b) t -> p a (b t)", a=2)
                nc.vector.tensor_tensor(pair(hid_lo), work[:, 2:4, :], pair(hid_hi).bitcast(F32),
                                        ALU.subtract).then_inc(hid_ready, 1)

            def ff2_step(n, j, i=0):
                hidden2_lo(j, i)
                split_lo(n + 3, 4 * i)
                square(j + 1, i)
                split_lo(n + 4, 4 * i)
                split_lo(n + 5, 4 * i)
                split_lo(n + 6, 4 * i)

            split_lo(N_FF2 + 3)
            square(j0)
            split_lo(N_FF2 + 4)
            with dve.Fori(0, 2) as i:
                for s in range(3):
                    ff2_step(N_FF2 + 2 + 4 * s, j0 + s, i)
            ff2_step(N_FF2 + 26, j0 + 6)
            hidden2_lo(j0 + 7)
            layer_norm(8, N_TILES, 1.0)
            dve.wait_ge(rows_loaded, 32 * 8)
            for tb in range(TB):
                dve.wait_ge(xn_ready, TB * 7 + tb + 1)
                link(nc.vector.tensor_tensor(xn[:, tb, :], xn[:, tb, :], ln_rows[:, 0, :], ALU.mult))
                nc.vector.tensor_tensor(resid[:, tb, :], xn[:, tb, :], ln_rows[:, 1, :], ALU.add).then_inc(out_ready, 1)

        @block.tensor
        def _(pe):
            mm = nc.tensor.matmul

            def three(out, a_hi, a_lo, b_hi, b_lo, start, stop):
                mm(out, a_hi, b_hi, start=start, stop=False, skip_group_check=True)
                mm(out, a_hi, b_lo, start=False, stop=False, skip_group_check=True)
                return mm(out, a_lo, b_hi, start=False, stop=stop, skip_group_check=True)

            def turn(what, src, ready, values, c0=0):
                for tb in range(TB):
                    pe.wait_ge(ready, values[tb])
                    for c in range(KC):
                        at = (c % 2) * TOK + tb * P
                        ins = nc.tensor.transpose(work[:, c // 2, at:at + P], src[:, tb, (c0 + c) * P:(c0 + c + 1) * P],
                                                  ident)
                        if tb == TB - 1 and c % 2:
                            ins.then_inc(turned, 1)

            def tokens_unit(n, out, base=None, i=0):
                for s in range(2):
                    slot = slot_of(n + s)
                    pe.wait_ge(lo_split, i + (n + s + 1))
                    for k in range(4):
                        c = 4 * s + k
                        if base is not None:
                            pe.wait_ge(operand_ready, base + c // 2 + 1)
                        cols = slice(k * NCOL, (k + 1) * NCOL)
                        for tb in range(TB):
                            t = slice(tb * P, (tb + 1) * P)
                            last = three(out[:, tb, :], x_hi[:, c, t], x_lo[:, c, t], w_hi[:, slot, cols], w_lo[:, slot, cols],
                                         c == 0, c == KC - 1)
                    last.then_inc(weights_used, 1)

            def features_unit(n, out, base=None):
                for s in range(2):
                    slot = slot_of(n + s)
                    pe.wait_ge(lo_split, n + s + 1)
                    for k in range(4):
                        c = 4 * s + k
                        if base is not None:
                            pe.wait_ge(operand_ready, base + c // 2 + 1)
                        for b in range(4):
                            cols = slice(k * NCOL + b * P, k * NCOL + (b + 1) * P)
                            last = three(out[:, b // 2, (b % 2) * TOK:(b % 2 + 1) * TOK], w_hi[:, slot, cols], w_lo[:, slot, cols],
                                         x_hi[:, c, :], x_lo[:, c, :], c == 0 and b % 2 == 0, c == KC - 1)
                    last.then_inc(weights_used, 1)

            def down(n, h_hi, h_lo, chunks, first, final, i=0, ready=None):
                slot = slot_of(n)
                pe.wait_ge(lo_split, i + (n + 1))
                for k, c in enumerate(chunks):
                    if ready is not None:
                        pe.wait_ge(operand_ready, ready + c // 2 + 1)
                    for tb in range(TB):
                        t = slice(tb * P, (tb + 1) * P)
                        for half in range(2):
                            cols = slice(k * D + half * NCOL, k * D + (half + 1) * NCOL)
                            last = three(acc[:, 2 * tb + half, :], h_hi[:, c, t], h_lo[:, c, t], w_hi[:, slot, cols],
                                         w_lo[:, slot, cols], first and k == 0, final and k == len(chunks) - 1)
                last.then_inc(weights_used, 1)

            def turn_hidden(j, i=0, cols=256):
                pe.wait_ge(hid_done, i + (j + 1))
                for c in range(cols // P):
                    for tb in range(TB):
                        at = (c % 2) * TOK + tb * P
                        ins = nc.tensor.transpose(work[:, 2 + c // 2, at:at + P], hid[:, tb, c * P:(c + 1) * P], ident)
                ins.then_inc(hid_turned, 1)

            def ffn(n0, f, base):
                j0 = f * FFN_STEPS
                gate_up = work[:, 0:2, :]
                tokens_unit(n0, gate_up, base)
                turn_hidden(j0)
                tokens_unit(n0 + 2, gate_up)
                pe.wait_ge(hid_ready, j0 + 1)
                down(n0 + 4, hid_hi, hid_lo, range(2), True, False)
                turn_hidden(j0 + 1)
                with pe.Fori(0, FFN_STEPS - 2) as i:
                    tokens_unit(n0 + 5, gate_up, i=3 * i)
                    pe.wait_ge(hid_ready, i + (j0 + 2))
                    down(n0 + 7, hid_hi, hid_lo, range(2), False, False, 3 * i)
                    turn_hidden(j0 + 2, i)
                pe.wait_ge(hid_ready, j0 + FFN_STEPS)
                down(n0 + FFN_TILES - 1, hid_hi, hid_lo, range(2), False, True)

            pe.wait_ge(consts_loaded, 32)
            turn("x", xn, x_loaded, [32, 32])
            ffn(N_FFN0, 0, turns["x"])
            turn("ln1", xn, xn_ready, [1, 2])

            base = turns["ln1"]
            pe.wait_ge(gla_loaded, 16 * 5)
            pe.wait_ge(operand_ready, base + KC // 2)
            for c in range(KC):
                for part in (x_hi, x_lo):
                    last = mm(acc[0:GLA_RANK, 0, 0:TOK], g_tail[:, c, :], part[:, c, :].bitcast(F32),
                              start=(c == 0 and part is x_hi), stop=(c == KC - 1 and part is x_lo))
            last.then_inc(low_ready, 1)
            n = N_GLA
            features_unit(n, pairs[0])
            pe.wait_ge(low_copied, 1)
            for h in range(GLA_HEADS):
                last = mm(acc[:, 1 + h // 2, (h % 2) * TOK:(h % 2 + 1) * TOK], g_wg[:, h * GLA_DK:(h + 1) * GLA_DK],
                          g_low[:, :], start=(h % 2 == 0), stop=True, skip_group_check=True)
            last.then_inc(z_ready, 1)
            features_unit(n + 2, pairs[1])
            for u in range(2, 4):
                pe.wait_ge(pair_free[u % 2], u // 2)
                tokens_unit(n + 2 * u, pairs[u % 2])
            pe.wait_ge(dec_ready, 1)
            for tb in range(TB):
                for h in range(GLA_HEADS):
                    last = nc.tensor.transpose(acc[:, 3 * tb, h * P:(h + 1) * P], g_end[:, h, tb * P:(tb + 1) * P], ident)
                last.then_inc(kend_turned, 1)
            for tb in range(TB):
                for h in range(GLA_HEADS):
                    t = slice(tb * P, (tb + 1) * P)
                    last = mm(acc[:, 1 + tb, h * P:(h + 1) * P], g_dn[:, h, t], g_qT[:, h, t],
                              start=(h == 0), stop=True, skip_group_check=True)
                last.then_inc(gs_ready, 1)
            for u in range(4, 6):
                pe.wait_ge(pair_free[u % 2], u // 2)
                tokens_unit(n + 2 * u, pairs[u % 2])
            pe.wait_ge(kend_copied, TB)
            pe.wait_ge(gs_masked, TB)

            def update(c):
                rows, tb = slice((c % 2) * CHUNK, (c % 2 + 1) * CHUNK), c // 2
                for h in range(GLA_HEADS):
                    last = mm(pairs[c % 2][:, h // 2, (h % 2) * GLA_DV:(h % 2 + 1) * GLA_DV],
                              g_kend[rows, tb, h * GLA_DK:(h + 1) * GLA_DK], g_v[rows, tb, h * GLA_DV:(h + 1) * GLA_DV],
                              start=(h % 2 == 0), stop=True, skip_group_check=True)
                last.then_inc(upd_ready, 1)

            def gla_out(tb, h):
                return acc[:, 2 * tb + h // 2, (h % 2) * GLA_DV:(h % 2 + 1) * GLA_DV]

            def from_state(c):
                rows, tb = slice((c % 2) * CHUNK, (c % 2 + 1) * CHUNK), c // 2
                pe.wait_ge(state_ready, c)
                for h in range(GLA_HEADS):
                    last = mm(gla_out(tb, h)[rows], g_qT[:, h, c * CHUNK:(c + 1) * CHUNK], g_state[:, c - 1, h, :],
                              start=False, stop=True, skip_group_check=True)
                return last

            for c in range(2):
                pe.wait_ge(pair_free[c], 3)
                update(c)
            for tb in range(TB):
                for h in range(GLA_HEADS):
                    mm(gla_out(tb, h), g_s[:, tb, h, :], g_v[:, tb, h * GLA_DV:(h + 1) * GLA_DV],
                       start=(h % 2 == 0), stop=False, skip_group_check=True)
            from_state(1).then_inc(gla_o, 1)
            update(2)
            from_state(2)
            from_state(3).then_inc(gla_o, 1)
            turn("gla", g_v, mixed, [1, 2])
            for j in range(4):
                down(N_GLA_OUT + j, x_hi, x_lo, range(2 * j, 2 * j + 2), j == 0, j == 3, ready=turns["gla"])
            turn("ln2", xn, xn_ready, [3, 4])
            ffn(N_FFN1, 1, turns["ln2"])
            turn("ln3", xn, xn_ready, [5, 6])
            ffn(N_FFN2, 2, turns["ln3"])
            turn("ln4", xn, xn_ready, [7, 8])

            n = N_RET
            free = [3, 3]
            pe.wait_ge(operand_ready, turns["ln4"] + KC // 2)
            for u in range(RET_UNITS):
                if u >= 2:
                    free[u % 2] += 1
                    pe.wait_ge(pair_free[u % 2], free[u % 2])
                (features_unit if u < 4 else tokens_unit)(n + 2 * u, pairs[u % 2])
                if u == 4:
                    pe.wait_ge(rope_done, 8)
                    for h in range(RET_HEADS):
                        for kb, cols in ((0, slice(0, TOK)), (1, slice(TOK, CAUSAL))):
                            for c in range(2):
                                last = mm(acc[:, h, cols], r_qk[:, 1, 2 * h + c, kb * P:(kb + 1) * P],
                                          r_qk[:, 0, 2 * h + c, kb * P:TOK], start=(c == 0), stop=(c == 1))
                        last.then_inc(rs_ready, 1)
            pe.wait_ge(rs_decayed, RET_HEADS)
            for u in range(2):
                pe.wait_ge(pair_free[u], free[u] + 1)
            for tb in range(TB):
                o = work if tb == 0 else acc
                for h in range(RET_HEADS):
                    for kb in range(tb + 1):
                        cols = slice(tb * P, (tb + 1) * P) if kb == 0 else slice(TOK, CAUSAL)
                        last = mm(o[:, h, :], r_s[:, h, cols], r_v[:, kb, h * RET_DV:(h + 1) * RET_DV],
                                  start=(kb == 0), stop=(kb == tb))
                last.then_inc(ret_o, 1)
            turn("ret", r_o, mixed, [3, 4])
            pe.wait_ge(operand_ready, turns["ret"] + KC // 2)
            turn("ret", r_o, mixed, [3, 4], KC)
            for j in range(8):
                hi, c = (x_hi, 2 * j) if j < 4 else (r_hi2, 2 * j - KC)
                lo = r_lo[:, 0:KC, :] if j < 4 else r_lo[:, KC:2 * KC, :]
                down(N_RET_OUT + j, hi, lo, range(c, c + 2), j == 0, j == 7, ready=turns["ret"] + (0 if j < 4 else KC // 2))
            turn("ln5", xn, xn_ready, [9, 10])
            ffn(N_FFN3, 3, turns["ln5"])
            turn("ln6", xn, xn_ready, [11, 12])

            n = N_SEC
            free = [9, 9]
            pe.wait_ge(operand_ready, turns["ln6"] + KC // 2)

            def unit(u, kind):
                if u >= 2:
                    free[u % 2] += 1
                    pe.wait_ge(pair_free[u % 2], free[u % 2])
                kind(n + 2 * u, pairs[u % 2])

            unit(0, features_unit)
            unit(1, features_unit)
            pe.wait_ge(att_loaded, 48)
            for c in range(KC):
                for part in (x_hi, x_lo):
                    mm(acc[:, 0, 0:TOK], a_tail[:, c, 0:P], part[:, c, :].bitcast(F32),
                       start=(c == 0 and part is x_hi), stop=(c == KC - 1 and part is x_lo))
            for tb in range(TB):
                for c in range(KC):
                    for part in (x_hi, x_lo):
                        last = mm(acc[:, 1, 32 * tb:32 * tb + 24], part[:, c, tb * P:(tb + 1) * P].bitcast(F32), a_tail[:, c, P:],
                                  start=(c == 0 and part is x_hi), stop=(c == KC - 1 and part is x_lo))
            last.then_inc(small_ready, 1)
            unit(2, features_unit)
            unit(3, features_unit)
            pe.wait_ge(small_copied, 1)
            pe.wait_ge(pair_free[1], free[1])
            for p in range(6):
                if p >= 2:
                    pe.wait_ge(relu_done, p - 1)
                tb = 1 if p < 4 else 0
                width = TOK if tb else P
                per = NCOL // width
                for s in range(per):
                    for b in range(2):
                        h = (4 * p if tb else 8 * (p - 4)) + 2 * s + b
                        rows = slice(HEAD_DIM * b, HEAD_DIM * (b + 1))
                        last = mm(acc[:, 2 * (p % 2) + b, s * width:(s + 1) * width], a_qi[rows, h // 2, tb * P:(tb + 1) * P],
                                  a_ki[rows, 0:width], start=(s == 0), stop=True, skip_group_check=True)
                last.then_inc(dots_ready, 1)
            unit(4, tokens_unit)
            pe.wait_ge(lf_ready, 1)
            pe.wait_ge(relu_done, 6)
            mm(acc[0:HEADS, 0, 0:P], a_lf[:, 2, 0, :], tri, start=True, stop=True, skip_group_check=True)
            mm(acc[0:HEADS, 0, P:TOK], a_lf[:, 2, 0, :], ones, start=False, stop=False, skip_group_check=True)
            mm(acc[0:HEADS, 0, P:TOK], a_lf[:, 2, 1, :], tri, start=False, stop=True, skip_group_check=True).then_inc(cum_f, 1)
            unit(5, features_unit)
            unit(6, features_unit)
            unit(7, tokens_unit)

            def logits(br, st):
                for g, (tb, heads) in enumerate(((1, range(0, 4)), (1, range(4, 8)), (0, range(8)))):
                    if g == 2:
                        pe.wait_ge(max_ready, 3 * br + 1)
                    width = TOK if tb else P
                    for h in heads:
                        b, s = h % 2, (h - heads[0]) // 2
                        rows = slice(HEAD_DIM * b, HEAD_DIM * (b + 1))
                        out = acc[:, 2 * (g % 2) + b, s * width:(s + 1) * width]
                        last = mm(out, a_q[rows, st, h // 2, tb * P:(tb + 1) * P], a_k[rows, st, h // 2, 0:width],
                                  start=(s == 0), stop=(br == 0), skip_group_check=True)
                    if br == 1:
                        for h in heads:
                            b, s = h % 2, (h - heads[0]) // 2
                            out = acc[:, 2 * (g % 2) + b, s * width:(s + 1) * width]
                            pick = ident[0:HEADS, h:h + 1]
                            mm(out, a_cT[:, 0, tb * P:(tb + 1) * P], pick.to_broadcast([HEADS, width]),
                               start=False, stop=False, skip_group_check=True)
                            last = mm(out, pick.to_broadcast([HEADS, P]), a_cT[:, 1, 0:width],
                                      start=False, stop=True, skip_group_check=True)
                    last.then_inc(logits_ready, 1)

            def turn_p(br):
                pe.wait_ge(p_ready, 3 * br + 3)
                for h in range(HEADS):
                    if h >= 4:
                        pe.wait_ge(pt_act if h % 2 == 0 else pt_dve, 4 * br + (h - 4) // 2 + 1)
                    nc.tensor.transpose(acc[:, h % 4, 0:P], a_p[:, h, 0:P], ident)
                    nc.tensor.transpose(acc[:, h % 4, P:TOK], a_p[:, h, P:TOK], ident)
                    nc.tensor.transpose(acc[:, h % 4, TOK:CAUSAL], a_p[:, h, TOK:CAUSAL], ident).then_inc(p_turned, 1)

            def values(br, pt):
                for h in range(HEADS):
                    rows = slice(HEAD_DIM * (h % 2), HEAD_DIM * (h % 2 + 1))
                    c = h // 2
                    out = acc[rows, c // 2, (c % 2) * TOK:(c % 2 + 1) * TOK]
                    cols = slice(h * HEAD_DIM, (h + 1) * HEAD_DIM)
                    mm(out, a_v[:, br, 0, cols], pt[:, h, 0:TOK], start=(c % 2 == 0), stop=False, skip_group_check=True)
                    last = mm(out[:, P:TOK], a_v[:, br, 1, cols], pt[:, h, TOK:CAUSAL], start=False, stop=True,
                              skip_group_check=True)
                last.then_inc(o_ready, 1)

            pe.wait_ge(cT_copied, 1)
            logits(0, 0)
            unit(8, features_unit)
            turn_p(0)
            pe.wait_ge(pt_act, 4)
            pe.wait_ge(pt_dve, 4)
            values(0, a_pt)
            unit(9, features_unit)
            pe.wait_ge(o_done, 1)
            logits(1, 1)
            unit(10, tokens_unit)
            turn_p(1)
            pe.wait_ge(pt_act, 8)
            pe.wait_ge(pt_dve, 8)
            values(1, a_pt)
            pe.wait_ge(o_done, 2)
            pe.wait_ge(pair_free[0], free[0] + 1)
            for r in range(2):
                if r:
                    pe.wait_ge(sb_t, r)
                for i in range(4):
                    h = 4 * r + i
                    rows = slice(HEAD_DIM * (h % 2), HEAD_DIM * (h % 2 + 1))
                    for kb, cols in ((0, slice(0, TOK)), (1, slice(TOK, CAUSAL))):
                        last = mm(acc[:, i, cols], a_k[rows, 0, h // 2, kb * P:(kb + 1) * P], a_q[rows, 0, h // 2, kb * P:TOK],
                                  start=True, stop=True, skip_group_check=True)
                last.then_inc(sb_z, 1)
                pe.wait_ge(sb_l, r + 1)
                for i in range(4):
                    h = 4 * r + i
                    mm(acc[:, i, 0:TOK], later_of, a_pt[:, h, 0:TOK], start=True, stop=False, skip_group_check=True)
                    mm(acc[:, i, P:TOK], ones, a_pt[:, h, TOK:CAUSAL], start=False, stop=False, skip_group_check=True)
                    last = mm(acc[:, i, TOK:CAUSAL], later_of, a_pt[:, h, TOK:CAUSAL], start=False, stop=True,
                              skip_group_check=True)
                last.then_inc(sb_later, 1)
            pe.wait_ge(sb_a, 2)
            values(2, a_p)
            pe.wait_ge(o_done, 3)
            for u in range(2):
                pe.wait_ge(pair_free[u], free[u] + (1 if u == 0 else 0))
            with pe.Fori(0, 2) as half:
                for b in range(3):
                    m = N_MERGE + 3 * b
                    if b == 2:
                        pe.wait_ge(sig_done, half * 3 + 1)
                    tokens_unit(m, pairs[(b + 1) % 2], i=9 * half)
                    slot = slot_of(m + 2)
                    pe.wait_ge(lo_split, half * 9 + (m + 3))
                    if b == 2:
                        pe.wait_ge(up_used, half * 3 + 1)
                    for k in range(4):
                        cols = slice(k * NCOL, (k + 1) * NCOL)
                        for tb in range(TB):
                            t = slice(tb * P, (tb + 1) * P)
                            last = three(acc[:, 2 * (b % 2) + tb, :], a_oh[:, 4 * b + k, t], a_ol[:, 4 * b + k, t],
                                         w_hi[:, slot, cols], w_lo[:, slot, cols], k == 0, k == 3)
                    last.then_inc(weights_used, 1)
                pe.wait_ge(up_used, half * 3 + 3)
            turn("mrg", merged, merged_ready, [4, 4])
            for j in range(4):
                down(N_SEC_OUT + j, x_hi, x_lo, range(2 * j, 2 * j + 2), j == 0, j == 3, ready=turns["mrg"])
            turn("ln7", xn, xn_ready, [13, 14])

            j0 = 4 * FFN_STEPS
            gate_up = work[:, 0:2, :]

            def ff2_step(n, j, i=0, first=False):
                tokens_unit(n, gate_up, i=12 * i)
                pe.wait_ge(hid_ready, i * 3 + j + 1)
                down(n + 2, hid_hi, hid_lo, range(0, 2), first, False, 12 * i)
                down(n + 3, hid_hi, hid_lo, range(2, 4), False, False, 12 * i)
                turn_hidden(j + 1, 3 * i, 512)

            tokens_unit(N_FF2, gate_up, turns["ln7"])
            turn_hidden(j0, 0, 512)
            ff2_step(N_FF2 + 2, j0, first=True)
            with pe.Fori(0, 2) as i:
                for s in range(3):
                    ff2_step(N_FF2 + 6 + 4 * s, j0 + 1 + s, i)
            pe.wait_ge(hid_ready, j0 + 8)
            down(N_TILES - 2, hid_hi, hid_lo, range(0, 2), False, False)
            down(N_TILES - 1, hid_hi, hid_lo, range(2, 4), False, True)


def _column_tiles(w):
    return [w[r:r + 512].reshape(4, P, NCOL).transpose(1, 0, 2).reshape(P, TILE) for r in (0, 512)]


def _row_tiles(w):
    return [w[r:r + 256].reshape(2, P, D).transpose(1, 0, 2).reshape(P, TILE) for r in range(0, w.shape[0], 256)]


def _weight_stream(a):
    def units(w, columns):
        return [t for c in columns for t in _column_tiles(w[:, c:c + NCOL])]

    def ffn(i, j):
        w_in, down = a["ffn_w_in"][i, j], _row_tiles(a["ffn_w_out"][i, j])
        up = [_column_tiles(np.concatenate([w_in[:, 256 * s:256 * s + 256], w_in[:, D_FF + 256 * s:D_FF + 256 * s + 256]], 1))
              for s in range(FFN_STEPS)]
        tiles = list(up[0])
        for s in range(1, FFN_STEPS):
            tiles += up[s] + [down[s - 1]]
        return tiles + [down[-1]]

    tiles = ffn(0, 0)
    tiles += units(a["gla_w_in"][0], range(0, 3072, NCOL)) + _row_tiles(a["gla_w_out"][0])
    tiles += ffn(0, 1) + ffn(1, 0)
    tiles += units(a["ret_w_in"][0], range(0, 6144, NCOL)) + _row_tiles(a["ret_w_out"][0])
    tiles += ffn(1, 1)
    w = a["w_in_2"][0]
    at = dict(zip("qa ka va qi ki wi qf kf vf fg qs ks vs gates".split(),
                  np.cumsum([0, 512, 512, 512, 1024, 64, 16, 512, 512, 512, 8, 512, 512, 512])))
    tiles += units(w, [at["qi"], at["qi"] + NCOL] + [at[s] for s in "qa ka va qf kf vf qs ks vs".split()])
    for half in range(2):
        for b in range(3):
            tiles += units(w, [at["gates"] + b * D + half * NCOL])
            tiles += _column_tiles(np.concatenate([a["w_branch_2"][0, b][:, half * NCOL:(half + 1) * NCOL]] * 2))[:1]
    tiles += _row_tiles(a["w_out_2"][0])
    up = [_column_tiles(a["w_ff1_2"][0][:, 512 * s:512 * s + 512]) for s in range(FF2_STEPS)]
    down = _row_tiles(a["w_ff2_2"][0])
    tiles += up[0]
    for s in range(1, FF2_STEPS):
        tiles += up[s] + down[2 * s - 2:2 * s]
    tiles += down[-2:]
    small = np.concatenate([w[:, at["ki"]:at["ki"] + 64]] * 2 + [w[:, at["wi"]:at["wi"] + 16], w[:, at["fg"]:at["fg"] + 8]], 1)
    return np.stack(tiles), small


def _constants():
    f = np.float32
    i = np.arange(P)
    square = np.stack([np.eye(P), i[:, None] <= i[None, :], i[:, None] > i[None, :], np.ones((P, P))], 1).astype(f)
    t = np.arange(TOK)
    keep = np.broadcast_to(t % CHUNK != 0, (P, TOK))
    same = (i[:, None] // CHUNK == i[None, :] // CHUNK) & (i[:, None] <= i[None, :])
    gla = np.concatenate([keep] + [same] * GLA_HEADS, 1).astype(f)
    inv = (np.float32(10000.0) ** (-np.arange(0, RET_DK, 2, dtype=f) / f(RET_DK))).astype(f)
    angle = (t.astype(f)[None, :] * inv[:, None]).astype(np.float64)
    log_g = np.log(1.0 - 2.0 ** (-5.0 - np.arange(RET_HEADS)))
    decays = []
    for h in range(RET_HEADS):
        gap = t[None, :] - t[:, None]
        d = np.where(gap >= 0, np.exp(np.maximum(gap, 0) * log_g[h]), 0.0) * RET_DK ** -0.5
        decays += [d[0:P, :], d[P:, P:]]
    ret = np.concatenate([np.cos(angle), np.sin(angle)] + decays, 1).astype(f)
    gap = np.concatenate([i[:, None] - i[None, :], P + i[:, None] - t[None, :]], 1)
    before = np.concatenate([i[:, None] < t[None, :], i[:, None] < i[None, :]], 1)
    att = np.stack([np.where(gap >= 0, 0.0, NEG), -gap, before], 1).astype(f)
    return square, gla, ret, att


def kernel(**inputs):
    import concourse.bacc as _bacc
    from concourse.bass_utils import run_bass_kernel_spmd as _run

    a = {k: np.asarray(v) for k, v in inputs.items()}
    weights, small = _weight_stream(a)
    square, gla, ret, att = _constants()
    gains = [a["ln_g"][i, j] for i in range(2) for j in range(3)] + [a["ln1_g_2"][0], a["ln2_g_2"][0]]
    shifts = [a["ln_b"][i, j] for i in range(2) for j in range(3)] + [a["ln1_b_2"][0], a["ln2_b_2"][0]]
    cols = [np.stack([np.ones((KC, P), np.float32), np.zeros((KC, P), np.float32)])]
    cols += [np.stack([g.reshape(KC, P), b.reshape(KC, P)]) for g, b in zip(gains, shifts)]
    by_chunk = lambda w: w.reshape(KC, P, -1).transpose(1, 0, 2)
    arrays = {
        "weights": weights,
        "x": a["x"][0].reshape(TB, P, D),
        "constants": square,
        "ln_cols": np.stack(cols).transpose(3, 0, 1, 2),
        "ln_rows": np.stack([r for g, b in zip(gains, shifts) for r in (g, b)]),
        "gla_w_low": by_chunk(a["gla_w_in"][0][:, 3072:]),
        "gla_w_gate": a["gla_w_gate"][0],
        "gla_b_gate": a["gla_b_gate"][0].reshape(GLA_HEADS, P).T,
        "gla_constants": gla,
        "gla_gain": a["gla_norm_g"],
        "ret_constants": ret,
        "ret_gain": a["ret_norm_g"],
        "att_w_small": by_chunk(small),
        "att_constants": att,
        "b_forget": a["b_forget_2"],
    }
    nc = _bacc.Bacc("TRN2", target_bir_lowering=False, num_devices=1)
    io, data = {}, {}
    for name, v in arrays.items():
        data[f"in_{name}"] = np.ascontiguousarray(v)
        io[name] = nc.dram_tensor(f"in_{name}", v.shape, F32, kind="ExternalInput").ap()
    io["out"] = nc.dram_tensor("out_0", (TB, P, D), F32, kind="ExternalOutput").ap()
    build(nc, io)
    r = _run(nc, [data], core_ids=[0])
    return r.results[0]["out_0"].reshape(1, TOK, D)
```

```python
from contextlib import ExitStack

import concourse.bass as bass
import numpy as np
from concourse import mybir

F32 = mybir.dt.float32
F32R = mybir.dt.float32r
U32 = mybir.dt.uint32
ALU = mybir.AluOpType
ACT = mybir.ActivationFunctionType
AX_X = mybir.AxisListType.X

P = 128
D = 1024
TOK = 256
TB = TOK // P
KC = D // P
NCOL = 512
TILE = 2048
RING = 3

D_FF = 2816
FFN_STEPS = D_FF // 256
GLA_HEADS, GLA_DK, GLA_DV, GLA_RANK, GLA_TAU = 4, 128, 256, 16, 16.0
CHUNK = 64
RET_HEADS, RET_DK, RET_DV = 4, 256, 512
HEADS, HEAD_DIM = 8, 64
IDX_HEADS = 16
TOPK = 64
FF2 = 4096
FF2_STEPS = FF2 // 512
ALPHA = 4.0 ** 0.25
ALPHA_2 = 2.0 ** 0.25
LN_EPS, NORM_EPS = 1e-5, 1e-6
NEG = -3.0e38
TAKEN = -3.4e38
CAUSAL = P + TOK

FFN_TILES = 3 * FFN_STEPS
GLA_UNITS, RET_UNITS, SEC_UNITS = 6, 12, 11
N_FFN0 = 0
N_GLA = N_FFN0 + FFN_TILES
N_GLA_OUT = N_GLA + 2 * GLA_UNITS
N_FFN1 = N_GLA_OUT + 4
N_FFN2 = N_FFN1 + FFN_TILES
N_RET = N_FFN2 + FFN_TILES
N_RET_OUT = N_RET + 2 * RET_UNITS
N_FFN3 = N_RET_OUT + 8
N_SEC = N_FFN3 + FFN_TILES
N_MERGE = N_SEC + 2 * SEC_UNITS
N_SEC_OUT = N_MERGE + 18
N_FF2 = N_SEC_OUT + 4
N_TILES = N_FF2 + 4 * FF2_STEPS


def build(nc, io):
    ctx = ExitStack()
    with ctx:
        def sb(name, shape, dt=F32, where=ctx):
            return where.enter_context(nc.sbuf_tensor(name, shape, dt))

        def sem(name):
            return ctx.enter_context(nc.semaphore(name))

        raw = sb("weights_raw", [P, RING, TILE])
        w_hi = sb("weights_hi", [P, RING, TILE], F32R)
        w_lo = sb("weights_lo", [P, RING, TILE], F32R)
        x_hi = sb("operand_hi", [P, KC, TOK], F32R)
        x_lo = sb("operand_lo", [P, KC, TOK], F32R)
        xn = sb("normalised", [P, TB, D])
        resid = sb("residual", [P, TB, D])
        ln_rows = sb("ln_rows", [P, 2, D])
        cst = sb("constants", [P, 4, P])
        ident, tri, later_of, ones = (cst[:, i, :] for i in range(4))
        squares = sb("squares", [P, D])
        row_sum = sb("row_sum", [P, TB])
        minus_mean = sb("minus_mean", [P, TB])
        square_sum = sb("square_sum", [P, TB])
        ln_rstd = sb("ln_rstd", [P, TB])
        stats = sb("stats", [P, 8, 6])
        mv = sb("mean_var", [P, 8, 2])
        rstd = sb("rstd", [P, 8])
        minus_half = sb("minus_half", [P, 8])
        bank = ctx.enter_context(nc.psum_tensor("psum", [P, 8, NCOL], F32))
        acc = bank[:, 0:4, :]
        work = bank[:, 4:8, :]

        with ExitStack() as ph:
            silu_g = sb("silu_gate", [P, 2, TOK], F32, ph)
            hid = sb("hidden", [P, 4, TOK], F32, ph)
            hid_hi = sb("hidden_hi", [P, 12, TOK], F32R, ph)
            hid_lo = sb("hidden_lo", [P, 12, TOK], F32R, ph)
        with ExitStack() as ph:
            g_qT = sb("gla_qT", [P, GLA_HEADS, TOK], F32, ph)
            g_kT = sb("gla_kT", [P, GLA_HEADS, TOK], F32, ph)
            g_v = sb("gla_v", [P, TB, D], F32, ph)
            g_r = sb("gla_r", [P, TB, D], F32, ph)
            g_z = sb("gla_z", [P, GLA_HEADS, TOK], F32, ph)
            g_t = sb("gla_t", [P, GLA_HEADS, TOK], F32, ph)
            g_cum = sb("gla_cum", [P, GLA_HEADS, TOK], F32, ph)
            g_up = sb("gla_exp_cum", [P, GLA_HEADS, TOK], F32, ph)
            g_dn = sb("gla_exp_minus_cum", [P, GLA_HEADS, TOK], F32, ph)
            g_end = sb("gla_exp_to_end", [P, GLA_HEADS, TOK], F32, ph)
            g_kend = sb("gla_k_end", [P, TB, GLA_HEADS * GLA_DK], F32, ph)
            g_s = sb("gla_scores", [P, TB, GLA_HEADS, P], F32, ph)
            g_state = sb("gla_state", [P, 3, GLA_HEADS, GLA_DV], F32, ph)
            g_low = sb("gla_low", [GLA_RANK, TOK], F32, ph)
            g_tail = sb("gla_w_low", [P, KC, GLA_RANK], F32, ph)
            g_wg = sb("gla_w_gate", [GLA_RANK, GLA_HEADS * GLA_DK], F32, ph)
            g_bg = sb("gla_b_gate", [P, GLA_HEADS], F32, ph)
            g_gain = sb("gla_gain", [P, GLA_DV], F32, ph)
            g_cst = sb("gla_constants", [P, TOK + GLA_HEADS * P], F32, ph)
            g_ss = sb("gla_sumsq", [P, 8], F32, ph)
            g_junk = sb("gla_junk", [P, GLA_DV], F32, ph)
            chunk_keep = g_cst[:, 0:TOK]
            chunk_mask = g_cst[:, TOK:TOK + GLA_HEADS * P]
        with ExitStack() as ph:
            r_qk = sb("ret_qkT", [P, 2, KC, TOK], F32, ph)
            r_v = sb("ret_v", [P, TB, 2 * D], F32, ph)
            r_g = sb("ret_g", [P, TB, 2 * D], F32, ph)
            r_rot = sb("ret_rot", [P, 2, 2, 2, TOK], F32, ph)
            r_after = r_rot[:, :, :, :, :].rearrange("p a b c t -> p (a b c t)")
            r_s = r_after[:, 0:RET_HEADS * CAUSAL].rearrange("p (h c) -> p h c", h=RET_HEADS)
            r_gain = r_after[:, RET_HEADS * CAUSAL:RET_HEADS * CAUSAL + RET_DV]
            r_lo = sb("ret_out_lo", [P, 2 * KC, TOK], F32R, ph)
            r_hi2 = sb("ret_out_hi", [P, KC, TOK], F32R, ph)
            r_cst = sb("ret_constants", [P, 2 * TOK + RET_HEADS * CAUSAL], F32, ph)
            r_o = r_qk[:, :, :, :].rearrange("p a c t -> p a (c t)")
            cos, sin = r_cst[:, 0:TOK], r_cst[:, TOK:2 * TOK]
            decay = r_cst[:, 2 * TOK:].rearrange("p (h c) -> p h c", h=RET_HEADS)
        with ExitStack() as ph:
            a_q = sb("att_qT", [P, 2, 4, TOK], F32, ph)
            a_k = sb("att_kT", [P, 2, 4, TOK], F32, ph)
            a_v = sb("att_v", [P, 3, TB, HEADS * HEAD_DIM], F32, ph)
            a_ki = sb("att_kiT", [P, TOK], F32, ph)
            a_wf = sb("att_wi_fg", [P, TB, IDX_HEADS + HEADS], F32, ph)
            a_bf = sb("att_b_forget", [P, HEADS], F32, ph)
            a_lf = sb("att_log_f", [P, 3, TB, HEADS], F32, ph)
            a_cT = sb("att_cT", [HEADS, 2, TOK], F32, ph)
            a_cst = sb("att_constants", [P, 3, CAUSAL], F32, ph)
            a_sc = sb("att_score", [P, 2, CAUSAL], F32, ph)
            a_top = sb("att_top8", [P, 8], F32, ph)
            a_max = sb("att_max", [P, 2, TB, HEADS], F32, ph)
            a_sum = sb("att_sum", [P, TB, HEADS], F32, ph)
            a_p = sb("att_p", [P, HEADS, CAUSAL], F32, ph)
            a_pt = sb("att_pT", [P, HEADS, CAUSAL], F32, ph)
            causal, negdist, strict = (a_cst[:, i, :] for i in range(3))
            with ExitStack() as sub:
                a_tail = sb("att_w_small", [P, KC, P + IDX_HEADS + HEADS], F32, sub)
                a_qi = sb("att_qiT", [P, 8, TOK], F32, sub)
            a_oh = sb("att_out_hi", [P, 12, TOK], F32R, ph)
            a_ol = sb("att_out_lo", [P, 12, TOK], F32R, ph)
            relu = a_pt[:, :, :].rearrange("p h c -> p (h c)")[:, 0:2048].rearrange("p (b c) -> p b c", b=2)
            sig = a_p[:, :, :].rearrange("p h c -> p (h c)")[:, 0:2048].rearrange("p (b t c) -> p b t c", b=2, t=TB)
            upg = a_pt[:, :, :].rearrange("p h c -> p (h c)")[:, 0:2048].rearrange("p (b t c) -> p b t c", b=2, t=TB)
            merged = xn

        weight_loaded = [sem(f"weight_loaded{i}") for i in range(RING)]
        hi_split = sem("hi_split")
        lo_split = sem("lo_split")
        weights_used = sem("weights_used")
        pair_free = [sem("pair_free0"), sem("pair_free1")]
        x_loaded, consts_loaded = [sem("x_loaded0"), sem("x_loaded1")], sem("consts_loaded")
        acc_ready = sem("acc_ready")
        mean_ready = sem("mean_ready")
        var_ready, rstd_ready = sem("var_ready"), sem("rstd_ready")
        xn_ready, resid_ready = sem("xn_ready"), sem("resid_ready")
        rows_loaded = sem("rows_loaded")
        turned, turned_hi, operand_ready = sem("turned"), sem("turned_hi"), sem("operand_ready")
        silu_done, hid_done = sem("silu_done"), sem("hid_done")
        hid_turned, hid_hi_done, hid_ready = sem("hid_turned"), sem("hid_hi_done"), sem("hid_ready")
        dve_step, pool_step, act_step = sem("dve_step"), sem("pool_step"), sem("act_step")
        out_stored = sem("out_stored")
        gla_loaded, ret_loaded, att_loaded = sem("gla_loaded"), sem("ret_loaded"), sem("att_loaded")
        low_ready, low_copied, z_ready = sem("low_ready"), sem("low_copied"), sem("z_ready")
        naz_ready, ln1p_ready, cum_ready = sem("naz_ready"), sem("ln1p_ready"), sem("cum_ready")
        exp_ready, dec_ready = sem("exp_ready"), sem("dec_ready")
        kend_turned, kend_copied = sem("kend_turned"), sem("kend_copied")
        gs_ready, gs_masked = sem("gs_ready"), sem("gs_masked")
        upd_ready, state_ready, gla_o = sem("upd_ready"), sem("state_ready"), sem("gla_o")
        ss_ready, gate_ready, mixed = sem("ss_ready"), sem("gate_ready"), sem("mixed")
        rot_ready, rope_done = sem("rot_ready"), sem("rope_done")
        rs_ready, rs_decayed, ret_o = sem("rs_ready"), sem("rs_decayed"), sem("ret_o")
        unit_copied = sem("unit_copied")
        small_ready, small_copied = sem("small_ready"), sem("small_copied")
        dots_ready, relu_done, dots_used = sem("dots_ready"), sem("relu_done"), sem("dots_used")
        lf_exp, lf_ln, lf_ready, cum_f, cT_copied = sem("lf_exp"), sem("lf_ln"), sem("lf_ready"), sem("cum_f"), sem("cT_copied")
        lf_in = sem("lf_in")
        logits_ready, max_ready, exp_done, p_ready = sem("logits_ready"), sem("max_ready"), sem("exp_done"), sem("p_ready")
        p_turned, pt_act, pt_dve = sem("p_turned"), sem("pt_act"), sem("pt_dve")
        o_ready, o_hi_done, o_done = sem("o_ready"), sem("o_hi_done"), sem("o_done")
        sb_z, sb_ln, sb_l, sb_later, sb_t, sb_exp, sb_a = (
            sem(n) for n in ("sb_z", "sb_ln", "sb_l", "sb_later", "sb_t", "sb_exp", "sb_a"))
        sig_done, up_used, merged_ready = sem("sig_done"), sem("up_used"), sem("merged_ready")

        pairs = [work[:, 0:2, :], work[:, 2:4, :]]
        as_pair = lambda t: t.rearrange("p (a b) t -> p a (b t)", a=2)
        two = lambda t: t.rearrange("p (c t) -> p c t", c=2)
        slot_of = lambda n: n % RING

        order = ["ln1", "gla", "ln2", "ln3", "ln4", "ret", "ln5", "ln6", "mrg", "ln7"]
        turns, at = {"x": 0}, KC // 2
        for what in order:
            turns[what] = at
            at += KC if what == "ret" else KC // 2

        block = ctx.enter_context(nc.Block())

        @block.sync
        def _(sp):
            sp.dma_start(xn[:, 0, :], io["x"][0]).then_inc(x_loaded[0], 16)
            for n in range(RING):
                sp.dma_start(raw[:, n, :], io["weights"][n]).then_inc(weight_loaded[n], 16)
            rounds = (N_TILES - RING) // RING
            with sp.Fori(0, rounds) as i:
                for n in range(RING, 2 * RING):
                    src = io["weights"][bass.ds(sp.snap(i * RING + n), 1)].rearrange("a p n -> (a p) n")
                    sp.wait_ge(lo_split, i * RING + (n - RING + 1))
                    sp.dma_start(raw[:, n % RING, :], src).then_inc(weight_loaded[n % RING], 16)
            for n in range(RING * (rounds + 1), N_TILES):
                sp.wait_ge(lo_split, n - RING + 1)
                sp.dma_start(raw[:, n % RING, :], io["weights"][n]).then_inc(weight_loaded[n % RING], 16)
            for tb in range(TB):
                sp.wait_ge(xn_ready, 4 * 7 + 2 * tb + 2)
                sp.dma_start(io["out"][tb], xn[:, tb, :]).then_inc(out_stored, 16)
            sp.wait_ge(out_stored, 16 * TB)

        @block.gpsimd
        def _(pool):
            step = [0]

            def link(ins):
                step[0] += 1
                ins.then_inc(pool_step, 1)
                pool.wait_ge(pool_step, step[0])

            powers = [0]

            def inverse_root(out, var, scale, eps, n):
                powers[0] += 1
                pool.wait_ge(var_ready, powers[0])
                link(nc.gpsimd.tensor_scalar(out, var, scale, eps, ALU.mult, ALU.add))
                nc.gpsimd.tensor_tensor(out, out, minus_half[:, 0:n], ALU.pow).then_inc(rstd_ready, 1)

            link(nc.gpsimd.memset(minus_half[:, :], -0.5))

            def load_rows(ln):
                for j in range(2):
                    pool.dma_start(ln_rows[:, j, :], io["ln_rows"][2 * (ln - 1) + j:2 * (ln - 1) + j + 1, :]
                                   .to_broadcast([P, D])).then_inc(rows_loaded, 16)

            def residual(tb, alpha):
                nc.gpsimd.tensor_scalar(resid[:, tb, :], xn[:, tb, :], alpha, 0.0, ALU.mult, ALU.add).then_inc(resid_ready, 1)

            def layer_norm(ln):
                for tb in range(TB):
                    inverse_root(ln_rstd[:, tb:tb + 1], square_sum[:, tb:tb + 1], 1.0 / D, LN_EPS, 1)
                    if ln < 8:
                        pool.wait_ge(xn_ready, 4 * (ln - 1) + 2 * tb + 2)
                        residual(tb, ALPHA if ln < 6 else ALPHA_2)
                if ln < 8:
                    load_rows(ln + 1)

            load_rows(1)
            for tb in range(TB):
                pool.wait_ge(x_loaded[tb], 16)
                residual(tb, ALPHA)
            layer_norm(1)
            pool.wait_ge(gla_loaded, 16 * 5)
            pool.wait_ge(unit_copied, 1)
            for tb in range(TB):
                for h in range(GLA_HEADS):
                    cols = slice(h * GLA_DV, (h + 1) * GLA_DV)
                    last = nc.gpsimd.tensor_tensor(g_r[:, tb, cols], g_r[:, tb, cols], g_gain[:, :], ALU.mult)
            last.then_inc(gate_ready, 1)
            inverse_root(rstd[:, 0:8], g_ss[:, :], 1.0 / GLA_DV, NORM_EPS, 8)
            layer_norm(2)
            layer_norm(3)
            layer_norm(4)
            for u in range(4):
                for j in range(2):
                    pool.wait_ge(rot_ready, 2 * u + j + 1)
                    head = 2 * (u % 2) + j
                    qk = r_qk[:, u // 2, 2 * head:2 * head + 2, :]
                    by_cos, by_sin = r_rot[:, j, 0], r_rot[:, j, 1]
                    nc.gpsimd.tensor_tensor(qk[:, 0, :], by_cos[:, 0, :], by_sin[:, 1, :], ALU.subtract)
                    nc.gpsimd.tensor_tensor(qk[:, 1, :], by_sin[:, 0, :], by_cos[:, 1, :], ALU.add).then_inc(rope_done, 1)
            pool.wait_ge(ret_loaded, 32)
            pool.wait_ge(unit_copied, 2)
            for tb in range(TB):
                for h in range(RET_HEADS):
                    cols = slice(h * RET_DV, (h + 1) * RET_DV)
                    last = nc.gpsimd.tensor_tensor(r_g[:, tb, cols], r_g[:, tb, cols], r_gain, ALU.mult)
            last.then_inc(gate_ready, 1)
            for tb in range(TB):
                inverse_root(rstd[:, 4 * tb:4 * tb + 4], mv[:, 4 * tb:4 * tb + 4, 1], 1.0, NORM_EPS, 4)
            layer_norm(5)
            layer_norm(6)
            layer_norm(7)
            layer_norm(8)

        @block.scalar
        def _(act):
            step = [0]

            def link(ins):
                step[0] += 1
                ins.then_inc(act_step, 1)
                act.wait_ge(act_step, step[0])

            def split_hi(n, i=0):
                if n >= N_TILES:
                    return
                s = slot_of(n)
                act.wait_ge(weight_loaded[s], i * 16 + 16 * (n // RING + 1))
                if n >= RING:
                    act.wait_ge(weights_used, i * RING + (n - RING + 1))
                nc.scalar.activation(w_hi[:, s, :], raw[:, s, :], ACT.Copy).then_inc(hi_split, 1)

            def turn_hi(what, hi, first=0):
                base = turns[what] + first
                for b in range(KC // 2):
                    act.wait_ge(turned, base + b + 1)
                    nc.scalar.activation(hi[:, 2 * b:2 * b + 2, :].rearrange("p c t -> p (c t)"), work[:, b, :],
                                         ACT.Copy).then_inc(turned_hi, 1)

            def rows_hi(what, tb):
                for b in range(2):
                    act.wait_ge(turned, turns[what] + 2 * tb + b + 1)
                    nc.scalar.activation(x_hi[:, 4 * b:4 * b + 4, tb * P:(tb + 1) * P],
                                         acc[:, 2 * tb + b, :].rearrange("p (c t) -> p c t", c=4),
                                         ACT.Copy).then_inc(turned_hi, 1)

            def layer_norm(ln, end):
                for tb in range(TB):
                    act.wait_ge(mean_ready, 2 * (ln - 1) + tb + 1)
                    link(nc.scalar.activation(squares[:, :], xn[:, tb, :], ACT.Square, bias=minus_mean[:, tb:tb + 1],
                                              accum_out=square_sum[:, tb:tb + 1]))
                    act.sem_inc(var_ready, 1)
                    if ln == 8:
                        continue
                    if tb == 0:
                        split_hi(end + 1)
                    rows_hi(f"ln{ln}", tb)
                    if tb == 0:
                        split_hi(end + 2)

            def ffn(n0, f):
                j0 = f * FFN_STEPS

                def silu(n, gate, i=0):
                    act.wait_ge(weights_used, i * 12 + n + 2)
                    nc.scalar.activation(silu_g[:, :, :], gate, ACT.Silu).then_inc(silu_done, 1)

                def hidden_hi(j, slot, src, i=0):
                    nc.scalar.activation(hid_hi[:, 2 * slot:2 * slot + 2, :], src, ACT.Copy).then_inc(hid_hi_done, 1)

                split_hi(n0 + 3)
                silu(n0, pairs[0][:, :, 0:TOK])
                split_hi(n0 + 4)
                act.wait_ge(hid_turned, f + 1)
                hidden_hi(j0, 0, two(acc[:, 0, :]))

                def step(j, n, ahead, gate_up, i=0):
                    split_hi(ahead, 4 * i)
                    silu(n, two(gate_up[:, 0, :]), i)
                    split_hi(ahead + 1, 4 * i)
                    act.wait_ge(hid_done, i * 4 + j0 + j + 1)
                    hidden_hi(j0 + j, j % 4, hid[:, 0:2, :], i)

                step(1, n0 + 2, n0 + 5, pairs[1])
                step(2, n0 + 4, n0 + 7, pairs[0])
                split_hi(n0 + 9)
                with act.Fori(0, 2) as i:
                    for j in range(3, 7):
                        step(j, n0 + 3 * j - 2, n0 + 3 * j + 1, pairs[1], i)
                        split_hi(n0 + 3 * j + 3, 4 * i)

            def unit(n, u, out, func=ACT.Copy, scale=1.0):
                split_hi(n + 3)
                act.wait_ge(weights_used, n + 2)
                src = pairs[u % 2]
                ins = nc.scalar.activation(out, src, func, scale=scale)
                ins.then_inc(pair_free[u % 2], 1)
                split_hi(n + 4)

            act.dma_start(cst[:, :, :], io["constants"]).then_inc(consts_loaded, 16)
            act.dma_start(xn[:, 1, :], io["x"][1]).then_inc(x_loaded[1], 16)
            rows_hi("x", 0)
            split_hi(0)
            split_hi(1)
            rows_hi("x", 1)
            split_hi(2)
            ffn(N_FFN0, 0)
            layer_norm(1, N_GLA)

            for dst, name in ((g_tail, "gla_w_low"), (g_wg, "gla_w_gate"), (g_bg, "gla_b_gate"),
                              (g_cst, "gla_constants")):
                act.dma_start(dst[tuple([slice(None)] * len(dst.shape))], io[name]).then_inc(gla_loaded, 16)
            act.dma_start(g_gain[:, :], io["gla_gain"].to_broadcast([P, GLA_DV])).then_inc(gla_loaded, 16)
            n = N_GLA
            unit(n, 0, g_v[:, :, 0:512])
            act.wait_ge(low_ready, 1)
            nc.scalar.activation(g_low[:, :], acc[0:GLA_RANK, 0, 0:TOK], ACT.Copy).then_inc(low_copied, 1)
            flat = lambda t: t.rearrange("p h t -> p (h t)")
            unit(n + 2, 1, as_pair(g_qT[:, :, :]), scale=GLA_DK ** -0.5)
            act.wait_ge(naz_ready, 1)
            link(nc.scalar.activation(g_t[:, :, :], g_t[:, :, :], ACT.Exp))
            nc.scalar.activation(g_t[:, :, :], g_t[:, :, :], ACT.Ln, bias=1.0).then_inc(ln1p_ready, 1)
            unit(n + 4, 2, as_pair(g_kT[:, :, :]))
            act.wait_ge(cum_ready, 1)
            nc.scalar.activation(g_up[:, :, :], g_cum[:, :, :], ACT.Exp, scale=1.0 / GLA_TAU)
            nc.scalar.activation(g_dn[:, :, :], g_cum[:, :, :], ACT.Exp, scale=-1.0 / GLA_TAU)
            nc.scalar.activation(g_end[:, :, :], g_end[:, :, :], ACT.Exp, scale=1.0 / GLA_TAU).then_inc(exp_ready, 1)
            unit(n + 6, 3, g_v[:, :, 512:1024])
            for tb in range(TB):
                act.wait_ge(kend_turned, tb + 1)
                nc.scalar.activation(g_kend[:, tb, :], acc[:, 3 * tb, :], ACT.Copy).then_inc(kend_copied, 1)
            unit(n + 8, 4, g_r[:, :, 0:512], ACT.Silu)
            unit(n + 10, 5, g_r[:, :, 512:1024], ACT.Silu)
            act.wait_ge(pair_free[1], 3)
            act.sem_inc(unit_copied, 1)
            for tb in range(TB):
                act.wait_ge(gla_o, tb + 1)
                for h in range(GLA_HEADS):
                    src = acc[:, 2 * tb + h // 2, (h % 2) * GLA_DV:(h % 2 + 1) * GLA_DV]
                    link(nc.scalar.activation(g_junk[:, :], src, ACT.Square,
                                              accum_out=g_ss[:, 4 * tb + h:4 * tb + h + 1]))
            act.sem_inc(var_ready, 1)
            turn_hi("gla", x_hi)
            for j in range(2):
                split_hi(N_GLA_OUT + j + 3)
            layer_norm(2, N_FFN1)
            ffn(N_FFN1, 1)
            layer_norm(3, N_FFN2)
            ffn(N_FFN2, 2)
            layer_norm(4, N_RET)

            act.dma_start(r_cst[:, :], io["ret_constants"]).then_inc(ret_loaded, 16)
            n = N_RET
            unit(n, 0, r_v[:, :, 0:512])
            for u in range(1, 5):
                n += 2
                split_hi(n + 3)
                split_hi(n + 4)
            n += 2
            act.wait_ge(rope_done, 8)
            act.dma_start(r_gain, io["ret_gain"].to_broadcast([P, RET_DV])).then_inc(ret_loaded, 16)
            for u in range(5, 8):
                unit(n, u, r_v[:, :, (u - 4) * 512:(u - 3) * 512])
                n += 2
            for u in range(8, 12):
                unit(n, u, r_g[:, :, (u - 8) * 512:(u - 7) * 512], ACT.Silu)
                n += 2
            act.wait_ge(pair_free[1], 9)
            act.sem_inc(unit_copied, 1)
            turn_hi("ret", x_hi)
            turn_hi("ret", r_hi2, KC // 2)
            for j in range(6):
                split_hi(N_RET_OUT + j + 3)
            layer_norm(5, N_FFN3)
            ffn(N_FFN3, 3)
            layer_norm(6, N_SEC)

            act.dma_start(a_tail[:, :, :], io["att_w_small"]).then_inc(att_loaded, 16)
            act.dma_start(a_cst[:, :, :], io["att_constants"]).then_inc(att_loaded, 16)
            act.dma_start(a_bf[:, :], io["b_forget"].to_broadcast([P, HEADS])).then_inc(att_loaded, 16)
            n = N_SEC
            unit(n, 0, a_v[:, 0])
            unit(n + 2, 1, as_pair(a_qi[:, 0:4, :]))
            unit(n + 4, 2, as_pair(a_qi[:, 4:8, :]))
            act.wait_ge(small_ready, 1)
            nc.scalar.activation(a_ki[:, :], acc[:, 0, 0:TOK], ACT.Copy)
            nc.scalar.activation(a_wf[:, :, :], acc[:, 1, 0:64].rearrange("p (t c) -> p t c", t=TB)[:, :, 0:24],
                                 ACT.Copy).then_inc(small_copied, 1)
            unit(n + 6, 3, as_pair(a_q[:, 0]), scale=HEAD_DIM ** -0.5)
            unit(n + 8, 4, as_pair(a_k[:, 0]))
            act.wait_ge(lf_in, 1)
            link(nc.scalar.activation(a_lf[:, 1], a_lf[:, 1], ACT.Exp))
            nc.scalar.activation(a_lf[:, 1], a_lf[:, 1], ACT.Ln, bias=1.0).then_inc(lf_ln, 1)
            for p in range(6):
                act.wait_ge(dots_ready, p + 1)
                if p >= 2:
                    act.wait_ge(dots_used, p - 1)
                nc.scalar.activation(relu[:, p % 2, :].rearrange("p (b c) -> p b c", b=2),
                                     acc[:, 2 * (p % 2):2 * (p % 2) + 2, :], ACT.Relu).then_inc(relu_done, 1)
            unit(n + 10, 5, as_pair(a_q[:, 1]), scale=HEAD_DIM ** -0.5)
            act.wait_ge(cum_f, 1)
            nc.scalar.activation(a_cT[:, 0, :], acc[0:HEADS, 0, 0:TOK], ACT.Copy)
            nc.scalar.activation(a_cT[:, 1, :], acc[0:HEADS, 0, 0:TOK], ACT.Copy, scale=-1.0).then_inc(cT_copied, 1)
            unit(n + 12, 6, as_pair(a_k[:, 1]))
            unit(n + 14, 7, a_v[:, 1])

            def softmax_exp(br):
                for g, (tb, heads) in enumerate(((1, range(0, 4)), (1, range(4, 8)), (0, range(8)))):
                    act.wait_ge(max_ready, 3 * br + g + 1)
                    cols = slice(P, CAUSAL) if tb else slice(0, P)
                    for h in heads:
                        ins = nc.scalar.activation(a_p[:, h, cols], a_p[:, h, cols], ACT.Exp,
                                                   bias=a_max[:, 1, tb, h:h + 1],
                                                   accum_out=a_sum[:, tb, h:h + 1])
                    ins.then_inc(exp_done, 1)

            def pt_copy(br):
                for h in range(0, HEADS, 2):
                    act.wait_ge(p_turned, 8 * br + h + 1)
                    nc.scalar.activation(a_pt[:, h, :], acc[:, h % 4, 0:CAUSAL], ACT.Copy).then_inc(pt_act, 1)

            def out_hi(br):
                act.wait_ge(o_ready, br + 1)
                nc.scalar.activation(a_oh[:, 4 * br:4 * br + 4, :].rearrange("p (a b) t -> p a (b t)", a=2),
                                     acc[:, 0:2, :], ACT.Copy).then_inc(o_hi_done, 1)

            softmax_exp(0)
            unit(n + 16, 8, as_pair(a_q[:, 0]), scale=HEAD_DIM ** -0.5)
            pt_copy(0)
            out_hi(0)
            unit(n + 18, 9, as_pair(a_k[:, 0]))
            softmax_exp(1)
            unit(n + 20, 10, a_v[:, 2])
            pt_copy(1)
            out_hi(1)
            for r in range(2):
                rows = slice(4 * r, 4 * r + 4)
                act.wait_ge(sb_z, r + 1)
                link(nc.scalar.activation(a_pt[:, rows, :], acc[:, 0:4, 0:CAUSAL], ACT.Abs))
                link(nc.scalar.activation(a_pt[:, rows, :], a_pt[:, rows, :], ACT.Exp, scale=-1.0))
                nc.scalar.activation(a_pt[:, rows, :], a_pt[:, rows, :], ACT.Ln, bias=1.0).then_inc(sb_ln, 1)
                act.wait_ge(sb_t, r + 1)
                nc.scalar.activation(a_p[:, rows, :], a_p[:, rows, :], ACT.Exp).then_inc(sb_exp, 1)
            out_hi(2)

            with act.Fori(0, 2) as half:
                for b in range(3):
                    m = N_MERGE + 3 * b
                    split_hi(m + 3, 3 * half)
                    act.wait_ge(weights_used, half * 9 + m + 2)
                    if b == 2:
                        act.wait_ge(up_used, half * 3 + 1)
                    nc.scalar.activation(sig[:, b % 2, :, :], pairs[(b + 1) % 2], ACT.Sigmoid).then_inc(sig_done, 1)
                    split_hi(m + 4, 3 * half)
                    split_hi(m + 5, 3 * half)
            turn_hi("mrg", x_hi)
            for j in range(2):
                split_hi(N_SEC_OUT + j + 3)
            layer_norm(7, N_FF2)

            j0 = 4 * FFN_STEPS

            def relu_up(n, up, i=0):
                act.wait_ge(weights_used, i * 12 + n + 2)
                nc.scalar.activation(as_pair(hid[:, :, :]), up, ACT.Relu).then_inc(silu_done, 1)

            def hidden2_hi(slot, src):
                nc.scalar.activation(hid_hi[:, 4 * slot:4 * slot + 4, :].rearrange("p (a b) t -> p a (b t)", a=2), src,
                                     ACT.Copy).then_inc(hid_hi_done, 1)

            def ff2_step(s, i=0):
                n = N_FF2 + 4 * s
                if s > 1:
                    split_hi(n, 4 * i)
                split_hi(n + 1, 4 * i)
                act.wait_ge(hid_ready, i * 3 + j0 + s)
                relu_up(n - 2, pairs[0], i)
                split_hi(n + 2, 4 * i)
                act.wait_ge(hid_done, i * 3 + j0 + s + 1)
                hidden2_hi(s % 3, as_pair(hid[:, :, :]))
                split_hi(n + 3, 4 * i)

            split_hi(N_FF2 + 3)
            relu_up(N_FF2, pairs[1])
            split_hi(N_FF2 + 4)
            act.wait_ge(hid_turned, 5)
            hidden2_hi(0, acc[:, 0:2, :])
            ff2_step(1)
            with act.Fori(0, 2) as i:
                for s in range(2, 5):
                    ff2_step(s, i)
            layer_norm(8, N_TILES)

        @block.vector
        def _(dve):
            step = [0]

            def mark(ins):
                step[0] += 1
                ins.then_inc(dve_step, 1)
                return step[0]

            def link(ins):
                dve.wait_ge(dve_step, mark(ins))

            def split_lo(n, i=0):
                if n >= N_TILES:
                    return
                s = slot_of(n)
                dve.wait_ge(hi_split, i * RING + (n + 1))
                nc.vector.tensor_tensor(w_lo[:, s, :], raw[:, s, :], w_hi[:, s, :].bitcast(F32),
                                        ALU.subtract).then_inc(lo_split, 1)

            def turn_lo(what, hi, lo, first=0):
                base = turns[what] + first
                for b in range(KC // 2):
                    dve.wait_ge(turned_hi, base + b + 1)
                    pair = lambda t: t[:, 2 * b:2 * b + 2, :].rearrange("p c t -> p (c t)")
                    nc.vector.tensor_tensor(pair(lo), work[:, b, :], pair(hi).bitcast(F32),
                                            ALU.subtract).then_inc(operand_ready, 1)

            def rows_lo(what, tb):
                for b in range(2):
                    dve.wait_ge(turned_hi, turns[what] + 2 * tb + b + 1)
                    part = lambda t: t[:, 4 * b:4 * b + 4, tb * P:(tb + 1) * P]
                    nc.vector.tensor_tensor(part(x_lo), acc[:, 2 * tb + b, :].rearrange("p (c t) -> p c t", c=4),
                                            part(x_hi).bitcast(F32), ALU.subtract).then_inc(operand_ready, 1)

            def layer_norm(ln, end, scale):
                dve.wait_ge(rows_loaded, 32 * ln)
                for tb in range(TB):
                    if tb == 0:
                        dve.wait_ge(acc_ready, ln)
                    else:
                        dve.wait_ge(weights_used, end)
                    dve.wait_ge(resid_ready, 2 * (ln - 1) + tb + 1)
                    link(nc.vector.scalar_tensor_tensor(
                        out=xn[:, tb, :], in0=acc[:, 2 * tb:2 * tb + 2, :].rearrange("p a b -> p (a b)"), scalar=scale,
                        in1=resid[:, tb, :], op0=ALU.mult, op1=ALU.add, accum_out=row_sum[:, tb:tb + 1]))
                    nc.vector.tensor_scalar(minus_mean[:, tb:tb + 1], row_sum[:, tb:tb + 1], -1.0 / D, None,
                                            ALU.mult).then_inc(mean_ready, 1)
                    dve.wait_ge(mean_ready, 2 * (ln - 1) + tb + 1)
                    link(nc.vector.scalar_tensor_tensor(
                        out=resid[:, tb, :], in0=xn[:, tb, :], scalar=minus_mean[:, tb:tb + 1], in1=ln_rows[:, 0, :],
                        op0=ALU.add, op1=ALU.mult))
                    count[0] += 1
                    dve.wait_ge(rstd_ready, count[0])
                    for b in range(2):
                        cols = slice(b * NCOL, (b + 1) * NCOL)
                        nc.vector.scalar_tensor_tensor(
                            out=xn[:, tb, cols], in0=resid[:, tb, cols], scalar=ln_rstd[:, tb:tb + 1],
                            in1=ln_rows[:, 1, cols], op0=ALU.mult, op1=ALU.add).then_inc(xn_ready, 1)
                    if ln < 8:
                        if tb == 0:
                            split_lo(end + 1)
                        rows_lo(f"ln{ln}", tb)
                        if tb == 1:
                            split_lo(end + 2)

            count = [0]

            def ffn(n0, f):
                j0 = f * FFN_STEPS

                def hidden(j, up, i=0):
                    dve.wait_ge(silu_done, i * 4 + j + 1)
                    nc.vector.tensor_tensor(hid[:, 0:2, :], silu_g[:, :, :], up, ALU.mult).then_inc(hid_done, 1)

                def hidden_lo(j, slot, src, i=0):
                    dve.wait_ge(hid_hi_done, i * 4 + j + 1)
                    nc.vector.tensor_tensor(hid_lo[:, 2 * slot:2 * slot + 2, :], src,
                                            hid_hi[:, 2 * slot:2 * slot + 2, :].bitcast(F32),
                                            ALU.subtract).then_inc(hid_ready, 1)

                split_lo(n0 + 3)
                hidden(j0, pairs[0][:, :, TOK:2 * TOK])
                split_lo(n0 + 4)
                hidden_lo(j0, 0, two(acc[:, 0, :]))

                def step(j, ahead, gate_up, i=0):
                    split_lo(ahead, 4 * i)
                    dve.wait_ge(hid_ready, i * 4 + j0 + j)
                    hidden(j0 + j, two(gate_up[:, 1, :]), i)
                    split_lo(ahead + 1, 4 * i)
                    hidden_lo(j0 + j, j % 4, hid[:, 0:2, :], i)

                step(1, n0 + 5, pairs[1])
                step(2, n0 + 7, pairs[0])
                split_lo(n0 + 9)
                with dve.Fori(0, 2) as i:
                    for j in range(3, 7):
                        step(j, n0 + 3 * j + 1, pairs[1], i)
                        split_lo(n0 + 3 * j + 3, 4 * i)

            rows_lo("x", 0)
            split_lo(0)
            split_lo(1)
            rows_lo("x", 1)
            split_lo(2)
            ffn(N_FFN0, 0)
            layer_norm(1, N_GLA, 0.5)

            n = N_GLA
            dve.wait_ge(gla_loaded, 16 * 5)
            link(nc.vector.memset(g_s[:, :, :, :], 0.0))
            for j in range(3, 7):
                split_lo(n + j)
            dve.wait_ge(z_ready, 1)
            for h in range(GLA_HEADS):
                last = nc.vector.tensor_scalar(g_z[:, h, :], acc[:, 1 + h // 2, (h % 2) * TOK:(h % 2 + 1) * TOK],
                                               g_bg[:, h:h + 1], None, ALU.add)
            link(last)
            nc.vector.scalar_tensor_tensor(out=g_t[:, :, :], in0=g_z[:, :, :], scalar=-1.0, in1=g_z[:, :, :],
                                           op0=ALU.mult, op1=ALU.min).then_inc(naz_ready, 1)
            split_lo(n + 7)
            dve.wait_ge(ln1p_ready, 1)
            link(nc.vector.scalar_tensor_tensor(out=g_z[:, :, :], in0=g_z[:, :, :], scalar=0.0, in1=g_t[:, :, :],
                                                op0=ALU.min, op1=ALU.subtract))
            for h in range(GLA_HEADS):
                last = nc.vector.tensor_tensor_scan(g_cum[:, h, :], chunk_keep, g_z[:, h, :], 0.0, ALU.mult, ALU.add)
            link(last)
            cum_c = g_cum[:, :, :].rearrange("p h (c t) -> p (h c) t", t=CHUNK)
            nc.vector.tensor_tensor(g_end[:, :, :].rearrange("p h (c t) -> p (h c) t", t=CHUNK),
                                    cum_c[:, :, CHUNK - 1:CHUNK].to_broadcast([P, 16, CHUNK]), cum_c,
                                    ALU.subtract).then_inc(cum_ready, 1)
            split_lo(n + 8)
            dve.wait_ge(exp_ready, 1)
            nc.vector.tensor_tensor(g_qT[:, :, :], g_qT[:, :, :], g_up[:, :, :], ALU.mult)
            nc.vector.tensor_tensor(g_end[:, :, :], g_kT[:, :, :], g_end[:, :, :], ALU.mult)
            nc.vector.tensor_tensor(g_dn[:, :, :], g_kT[:, :, :], g_dn[:, :, :], ALU.mult).then_inc(dec_ready, 1)
            for j in range(9, 12):
                split_lo(n + j)
                if j == 10:
                    for tb in range(TB):
                        dve.wait_ge(gs_ready, tb + 1)
                        nc.vector.copy_predicated(g_s[:, tb].rearrange("p h i -> p (h i)"), chunk_mask.bitcast(U32),
                                                  acc[:, 1 + tb, :]).then_inc(gs_masked, 1)
            for j in range(12, 15):
                split_lo(n + j)
            for c in range(3):
                dve.wait_ge(upd_ready, c + 1)
                src = pairs[c % 2].rearrange("p a (b v) -> p (a b) v", b=2)
                if c == 0:
                    link(nc.vector.tensor_copy(g_state[:, 0], src))
                else:
                    for h in range(GLA_HEADS):
                        end = c * CHUNK + CHUNK - 1
                        last = nc.vector.scalar_tensor_tensor(out=g_state[:, c, h, :], in0=g_state[:, c - 1, h, :],
                                                              scalar=g_up[:, h, end:end + 1], in1=src[:, h, :],
                                                              op0=ALU.mult, op1=ALU.add)
                    link(last)
                dve.sem_inc(state_ready, 1)
            count[0] += 1
            dve.wait_ge(rstd_ready, count[0])
            dve.wait_ge(gate_ready, 1)
            for tb in range(TB):
                for h in range(GLA_HEADS):
                    cols = slice(h * GLA_DV, (h + 1) * GLA_DV)
                    last = nc.vector.scalar_tensor_tensor(
                        out=g_v[:, tb, cols], in0=acc[:, 2 * tb + h // 2, (h % 2) * GLA_DV:(h % 2 + 1) * GLA_DV],
                        scalar=rstd[:, 4 * tb + h:4 * tb + h + 1], in1=g_r[:, tb, cols], op0=ALU.mult, op1=ALU.mult)
                last.then_inc(mixed, 1)
            turn_lo("gla", x_hi, x_lo)
            for j in range(2):
                split_lo(N_GLA_OUT + j + 3)
            layer_norm(2, N_FFN1, 1.0)
            ffn(N_FFN1, 1)
            layer_norm(3, N_FFN2, 0.5)
            ffn(N_FFN2, 2)
            layer_norm(4, N_RET, 0.5)

            n = N_RET
            split_lo(n + 3)
            split_lo(n + 4)
            dve.wait_ge(ret_loaded, 16)
            for u in range(4):
                n += 2
                split_lo(n + 3)
                dve.wait_ge(weights_used, n + 2)
                for j in range(2):
                    if u:
                        dve.wait_ge(rope_done, 2 * (u - 1) + j + 1)
                    src = pairs[(u + 1) % 2][:, j, :].rearrange("p (b t) -> p b t", b=2)
                    nc.vector.tensor_tensor(r_rot[:, j, 0], src, cos.rearrange("p (b t) -> p b t", b=1)
                                            .to_broadcast([P, 2, TOK]), ALU.mult)
                    last = nc.vector.tensor_tensor(r_rot[:, j, 1], src, sin.rearrange("p (b t) -> p b t", b=1)
                                                   .to_broadcast([P, 2, TOK]), ALU.mult)
                    last.then_inc(rot_ready, 1)
                dve.wait_ge(rot_ready, 2 * u + 2)
                dve.sem_inc(pair_free[(u + 1) % 2], 1)
                split_lo(n + 4)
            for u in range(5, 12):
                n += 2
                split_lo(n + 3)
                split_lo(n + 4)
                if u == 5:
                    for h in range(RET_HEADS):
                        dve.wait_ge(rs_ready, h + 1)
                        nc.vector.tensor_tensor(r_s[:, h, :], acc[:, h, 0:CAUSAL], decay[:, h, :],
                                                ALU.mult).then_inc(rs_decayed, 1)
            for tb in range(TB):
                dve.wait_ge(ret_o, tb + 1)
                o = work if tb == 0 else acc
                for h in range(RET_HEADS):
                    last = nc.vector.bn_stats(stats[:, 4 * tb + h, :], o[:, h, :])
                link(last)
                for h in range(RET_HEADS):
                    last = nc.vector.bn_aggr(mv[:, 4 * tb + h, :], stats[:, 4 * tb + h, :])
                last.then_inc(var_ready, 1)
            dve.wait_ge(gate_ready, 2)
            for tb in range(TB):
                o = work if tb == 0 else acc
                count[0] += 1
                dve.wait_ge(rstd_ready, count[0])
                for h in range(RET_HEADS):
                    i = 4 * tb + h
                    cols = slice(h * RET_DV, (h + 1) * RET_DV)
                    last = nc.vector.tensor_scalar(r_o[:, tb, cols], o[:, h, :], mv[:, i, 0:1], rstd[:, i:i + 1],
                                                   ALU.subtract, ALU.mult)
                link(last)
                nc.vector.tensor_tensor(r_o[:, tb, :], r_o[:, tb, :], r_g[:, tb, :], ALU.mult).then_inc(mixed, 1)
            turn_lo("ret", x_hi, r_lo[:, 0:KC, :])
            turn_lo("ret", r_hi2, r_lo[:, KC:2 * KC, :], KC // 2)
            for j in range(6):
                split_lo(N_RET_OUT + j + 3)
            layer_norm(5, N_FFN3, 1.0)
            ffn(N_FFN3, 3)
            layer_norm(6, N_SEC, 0.5)

            n = N_SEC
            dve.wait_ge(att_loaded, 48)
            for j in range(3, 13):
                split_lo(n + j)
            dve.wait_ge(small_copied, 1)
            link(nc.vector.tensor_tensor(a_lf[:, 0], a_wf[:, :, IDX_HEADS:],
                                         a_bf[:, :].rearrange("p (t h) -> p t h", t=1).to_broadcast([P, TB, HEADS]), ALU.add))
            nc.vector.scalar_tensor_tensor(out=a_lf[:, 1], in0=a_lf[:, 0], scalar=-1.0, in1=a_lf[:, 0],
                                           op0=ALU.mult, op1=ALU.min).then_inc(lf_in, 1)
            for p in range(6):
                dve.wait_ge(relu_done, p + 1)
                tb = 1 if p < 4 else 0
                width = TOK if tb else P
                per = NCOL // width
                cols = slice(P, CAUSAL) if tb else slice(0, P)
                for b in range(2):
                    for s in range(per):
                        h = (4 * p if tb else 8 * (p - 4)) + 2 * s + b
                        src = relu[:, p % 2, b * NCOL + s * width:b * NCOL + (s + 1) * width]
                        if h == 0:
                            link(nc.vector.tensor_scalar(a_sc[:, 0, cols], src, a_wf[:, tb, h:h + 1], None, ALU.mult))
                        else:
                            link(nc.vector.scalar_tensor_tensor(out=a_sc[:, 0, cols], in0=src, scalar=a_wf[:, tb, h:h + 1],
                                                                in1=a_sc[:, 0, cols], op0=ALU.mult, op1=ALU.add))
                dve.sem_inc(dots_used, 1)
                if p == 0:
                    dve.wait_ge(lf_ln, 1)
                    nc.vector.scalar_tensor_tensor(out=a_lf[:, 2], in0=a_lf[:, 0], scalar=0.0, in1=a_lf[:, 1],
                                                   op0=ALU.min, op1=ALU.subtract).then_inc(lf_ready, 1)
            link(nc.vector.tensor_tensor(a_sc[:, 0, :], a_sc[:, 0, :], causal, ALU.add))
            split_lo(n + 13)
            for tb, cols in ((1, slice(P, CAUSAL)), (0, slice(0, P))):
                for r in range(TOPK // 8):
                    link(nc.vector.max(out=a_top[:, :], in_=a_sc[:, 0, cols]))
                    link(nc.vector.match_replace(out=a_sc[:, 0, cols], in_to_replace=a_top[:, :],
                                                 in_values=a_sc[:, 0, cols], imm_value=TAKEN))
                    if r == 3:
                        split_lo(n + 14 + 2 * (1 - tb))
                split_lo(n + 15 + 2 * (1 - tb))
            link(nc.vector.tensor_scalar(a_sc[:, 0, :], a_sc[:, 0, :], TAKEN, NEG, ALU.not_equal, ALU.mult))
            link(nc.vector.tensor_tensor(a_sc[:, 0, :], a_sc[:, 0, :], causal, ALU.min))
            for j in range(18, 19):
                split_lo(n + j)

            groups = ((1, range(0, 4)), (1, range(4, 8)), (0, range(8)))

            def logits(br):
                for g, (tb, heads) in enumerate(groups):
                    dve.wait_ge(logits_ready, 3 * br + g + 1)
                    width = TOK if tb else P
                    cols = slice(P, CAUSAL) if tb else slice(0, P)
                    if br == 0:
                        for h in heads:
                            last = nc.vector.scalar_tensor_tensor(
                                out=a_p[:, h, cols], in0=negdist[:, cols], scalar=2.0 ** -(h + 1), in1=a_sc[:, 0, cols],
                                op0=ALU.mult, op1=ALU.add)
                        link(last)
                    for h in heads:
                        b, s = h % 2, (h - heads[0]) // 2
                        src = acc[:, 2 * (g % 2) + b, s * width:(s + 1) * width]
                        last = nc.vector.tensor_tensor_reduce(
                            out=a_p[:, h, cols], in0=src, in1=a_p[:, h, cols] if br == 0 else causal[:, cols],
                            scale=1.0, scalar=-3.4e38, op0=ALU.add, op1=ALU.max, accum_out=a_max[:, 0, tb, h:h + 1])
                    link(last)
                    nc.vector.tensor_scalar(a_max[:, 1, tb, heads[0]:heads[-1] + 1], a_max[:, 0, tb, heads[0]:heads[-1] + 1],
                                            -1.0, None, ALU.mult).then_inc(max_ready, 1)

            def normalise(br):
                for g, (tb, heads) in enumerate(groups):
                    dve.wait_ge(exp_done, 3 * br + g + 1)
                    cols = slice(P, CAUSAL) if tb else slice(0, P)
                    hs = slice(heads[0], heads[-1] + 1)
                    link(nc.vector.reciprocal(a_sum[:, tb, hs], a_sum[:, tb, hs]))
                    for h in heads:
                        last = nc.vector.tensor_scalar(a_p[:, h, cols], a_p[:, h, cols], a_sum[:, tb, h:h + 1], None, ALU.mult)
                    last.then_inc(p_ready, 1)

            def pt_copy(br):
                for h in range(1, HEADS, 2):
                    dve.wait_ge(p_turned, 8 * br + h + 1)
                    nc.vector.tensor_copy(a_pt[:, h, :], acc[:, h % 4, 0:CAUSAL]).then_inc(pt_dve, 1)

            def out_lo(br):
                dve.wait_ge(o_hi_done, br + 1)
                nc.vector.tensor_tensor(a_ol[:, 4 * br:4 * br + 4, :].rearrange("p (a b) t -> p a (b t)", a=2),
                                        acc[:, 0:2, :],
                                        a_oh[:, 4 * br:4 * br + 4, :].rearrange("p (a b) t -> p a (b t)", a=2).bitcast(F32),
                                        ALU.subtract).then_inc(o_done, 1)

            logits(0)
            normalise(0)
            split_lo(n + 19)
            split_lo(n + 20)
            pt_copy(0)
            out_lo(0)
            split_lo(n + 21)
            split_lo(n + 22)
            logits(1)
            normalise(1)
            split_lo(n + 23)
            split_lo(n + 24)
            pt_copy(1)
            out_lo(1)
            for r in range(2):
                rows = slice(4 * r, 4 * r + 4)
                z = acc[:, 0:4, 0:CAUSAL]
                dve.wait_ge(sb_ln, r + 1)
                link(nc.vector.scalar_tensor_tensor(out=a_p[:, rows, :], in0=z, scalar=0.0, in1=a_pt[:, rows, :],
                                                    op0=ALU.min, op1=ALU.subtract))
                link(nc.vector.tensor_tensor(a_pt[:, rows, :], a_p[:, rows, :], z, ALU.subtract))
                mask = strict.rearrange("p (h c) -> p h c", h=1).to_broadcast([P, 4, CAUSAL])
                nc.vector.tensor_tensor(a_pt[:, rows, :], a_pt[:, rows, :], mask, ALU.mult).then_inc(sb_l, 1)
                dve.wait_ge(sb_later, r + 1)
                nc.vector.tensor_tensor(a_p[:, rows, :], a_p[:, rows, :], z, ALU.add).then_inc(sb_t, 1)
                dve.wait_ge(sb_exp, r + 1)
                nc.vector.tensor_tensor(a_p[:, rows, :], a_p[:, rows, :], mask, ALU.mult).then_inc(sb_a, 1)
            out_lo(2)

            dve.wait_ge(resid_ready, 14)
            with dve.Fori(0, 2) as half:
                for b in range(3):
                    m = N_MERGE + 3 * b
                    split_lo(m + 3, 3 * half)
                    split_lo(m + 4, 3 * half)
                    dve.wait_ge(sig_done, half * 3 + b + 1)
                    dve.wait_ge(weights_used, half * 9 + m + 3)
                    dst = merged[:, :, bass.ds(half * NCOL, NCOL)]
                    up = acc[:, 2 * (b % 2):2 * (b % 2) + 2, :]
                    nc.vector.tensor_tensor(dst if b == 0 else upg[:, b % 2], sig[:, b % 2], up, ALU.mult).then_inc(up_used, 1)
                    if b:
                        dve.wait_ge(up_used, half * 3 + b + 1)
                        if b == 2:
                            dve.wait_ge(merged_ready, half * 2 + 1)
                        nc.vector.tensor_tensor(dst, dst, upg[:, b % 2], ALU.add).then_inc(merged_ready, 1)
                    split_lo(m + 5, 3 * half)
            turn_lo("mrg", x_hi, x_lo)
            for j in range(2):
                split_lo(N_SEC_OUT + j + 3)
            layer_norm(7, N_FF2, 1.0)

            j0 = 4 * FFN_STEPS

            def square(j, up, i=0):
                dve.wait_ge(silu_done, i * 3 + j + 1)
                nc.vector.tensor_tensor(as_pair(hid[:, :, :]), as_pair(hid[:, :, :]), up, ALU.mult).then_inc(hid_done, 1)

            def hidden2_lo(j, slot, src, i=0):
                dve.wait_ge(hid_hi_done, i * 3 + j + 1)
                part = lambda t: as_pair(t[:, 4 * slot:4 * slot + 4, :])
                nc.vector.tensor_tensor(part(hid_lo), src, part(hid_hi).bitcast(F32), ALU.subtract).then_inc(hid_ready, 1)

            def ff2_step(s, i=0):
                n = N_FF2 + 4 * s
                if s > 1:
                    split_lo(n, 4 * i)
                split_lo(n + 1, 4 * i)
                square(j0 + s, pairs[0], i)
                split_lo(n + 2, 4 * i)
                hidden2_lo(j0 + s, s % 3, as_pair(hid[:, :, :]), i)
                split_lo(n + 3, 4 * i)

            split_lo(N_FF2 + 3)
            square(j0, pairs[1])
            split_lo(N_FF2 + 4)
            hidden2_lo(j0, 0, acc[:, 0:2, :])
            ff2_step(1)
            with dve.Fori(0, 2) as i:
                for s in range(2, 5):
                    ff2_step(s, i)
            layer_norm(8, N_TILES, 1.0)

        @block.tensor
        def _(pe):
            mm = nc.tensor.matmul

            def three(out, a_hi, a_lo, b_hi, b_lo, start, stop):
                mm(out, a_hi, b_hi, start=start, stop=False, skip_group_check=True)
                mm(out, a_hi, b_lo, start=False, stop=False, skip_group_check=True)
                return mm(out, a_lo, b_hi, start=False, stop=stop, skip_group_check=True)

            def turn(what, src, ready, values, c0=0):
                for tb in range(TB):
                    pe.wait_ge(ready, values[tb])
                    for c in range(KC):
                        at = (c % 2) * TOK + tb * P
                        ins = nc.tensor.transpose(work[:, c // 2, at:at + P], src[:, tb, (c0 + c) * P:(c0 + c + 1) * P],
                                                  ident)
                        if tb == TB - 1 and c % 2:
                            ins.then_inc(turned, 1)

            def first_unit(n, out, what, ready, count):
                for tb in range(TB):
                    for b in range(2):
                        pe.wait_ge(ready[tb], count + (0 if what == "x" else 2 * tb + b + 1))
                        for j in range(4):
                            c = 4 * b + j
                            ins = nc.tensor.transpose(acc[:, 2 * tb + b, j * P:(j + 1) * P], xn[:, tb, c * P:(c + 1) * P], ident)
                        ins.then_inc(turned, 1)
                    t = slice(tb * P, (tb + 1) * P)
                    for s in range(2):
                        slot = slot_of(n + s)
                        pe.wait_ge(lo_split, n + s + 1)
                        pe.wait_ge(operand_ready, turns[what] + 2 * tb + s + 1)
                        for k in range(4):
                            c = 4 * s + k
                            cols = slice(k * NCOL, (k + 1) * NCOL)
                            last = three(out[:, tb, :], x_hi[:, c, t], x_lo[:, c, t], w_hi[:, slot, cols], w_lo[:, slot, cols],
                                         c == 0, c == KC - 1)
                        if tb == TB - 1:
                            last.then_inc(weights_used, 1)

            def normed_unit(n, out, ln):
                first_unit(n, out, f"ln{ln}", [xn_ready] * TB, 4 * (ln - 1))

            def tokens_unit(n, out, i=0):
                for s in range(2):
                    slot = slot_of(n + s)
                    pe.wait_ge(lo_split, i + (n + s + 1))
                    for k in range(4):
                        c = 4 * s + k
                        cols = slice(k * NCOL, (k + 1) * NCOL)
                        for tb in range(TB):
                            t = slice(tb * P, (tb + 1) * P)
                            last = three(out[:, tb, :], x_hi[:, c, t], x_lo[:, c, t], w_hi[:, slot, cols], w_lo[:, slot, cols],
                                         c == 0, c == KC - 1)
                    last.then_inc(weights_used, 1)

            def features_unit(n, out, i=0, between=None):
                for s in range(2):
                    slot = slot_of(n + s)
                    pe.wait_ge(lo_split, i + (n + s + 1))
                    if s and between:
                        between()
                    for k in range(4):
                        c = 4 * s + k
                        for b in range(4):
                            cols = slice(k * NCOL + b * P, k * NCOL + (b + 1) * P)
                            last = three(out[:, b // 2, (b % 2) * TOK:(b % 2 + 1) * TOK], w_hi[:, slot, cols], w_lo[:, slot, cols],
                                         x_hi[:, c, :], x_lo[:, c, :], c == 0 and b % 2 == 0, c == KC - 1)
                    last.then_inc(weights_used, 1)

            def down(n, h_hi, h_lo, chunks, first, final, i=0, ready=None):
                slot = slot_of(n)
                pe.wait_ge(lo_split, i + (n + 1))
                for k, c in enumerate(chunks):
                    if ready is not None:
                        pe.wait_ge(operand_ready, ready + c // 2 + 1)
                    for tb in range(TB):
                        t = slice(tb * P, (tb + 1) * P)
                        for half in range(2):
                            cols = slice(k * D + half * NCOL, k * D + (half + 1) * NCOL)
                            last = three(acc[:, 2 * tb + half, :], h_hi[:, c, t], h_lo[:, c, t], w_hi[:, slot, cols],
                                         w_lo[:, slot, cols], first and k == 0, final and k == len(chunks) - 1)
                last.then_inc(weights_used, 1)

            def last_pair(n, ready, values, chunks):
                for tb in range(TB):
                    t = slice(tb * P, (tb + 1) * P)
                    for s in range(2):
                        slot = slot_of(n + s)
                        pe.wait_ge(lo_split, n + s + 1)
                        pe.wait_ge(ready, values[s])
                        for k in range(2):
                            h_hi, h_lo, c = chunks[2 * s + k]
                            for half in range(2):
                                cols = slice(k * D + half * NCOL, k * D + (half + 1) * NCOL)
                                last = three(acc[:, 2 * tb + half, :], h_hi[:, c, t], h_lo[:, c, t], w_hi[:, slot, cols],
                                             w_lo[:, slot, cols], False, s == 1 and k == 1)
                        if tb == TB - 1:
                            last.then_inc(weights_used, 1)
                    if tb == 0:
                        last.then_inc(acc_ready, 1)

            def turn_hidden(j, cols):
                pe.wait_ge(hid_done, j + 1)
                src = hid[:, :, :].rearrange("p c t -> p (c t)")
                for c in range(cols // P):
                    for tb in range(TB):
                        at = (c % 2) * TOK + tb * P
                        ins = nc.tensor.transpose(acc[:, c // 2, at:at + P], src[:, tb * cols + c * P:tb * cols + (c + 1) * P], ident)
                ins.then_inc(hid_turned, 1)

            def hidden_chunks(slots, each):
                return [(hid_hi, hid_lo, each * s + k) for s in slots for k in range(each)]

            def ffn(n0, f):
                j0 = f * FFN_STEPS
                features_unit(n0 + 2, pairs[1], between=lambda: turn_hidden(j0, 2 * P))
                features_unit(n0 + 4, pairs[0])
                pe.wait_ge(hid_ready, j0 + 1)
                down(n0 + 6, hid_hi, hid_lo, range(2), True, False)
                with pe.Fori(0, 2) as i:
                    for j in range(3, 7):
                        pe.wait_ge(hid_done, i * 4 + j0 + j)
                        features_unit(n0 + 3 * j - 2, pairs[1], i=12 * i)
                        pe.wait_ge(hid_ready, i * 4 + j0 + j - 1)
                        at = 2 * ((j - 2) % 4)
                        down(n0 + 3 * j, hid_hi, hid_lo, range(at, at + 2), False, False, 12 * i)
                last_pair(n0 + FFN_TILES - 2, hid_ready, [j0 + FFN_STEPS - 1, j0 + FFN_STEPS], hidden_chunks((1, 2), 2))

            pe.wait_ge(consts_loaded, 16)
            first_unit(N_FFN0, pairs[0], "x", x_loaded, 16)
            ffn(N_FFN0, 0)

            n = N_GLA
            normed_unit(n, pairs[0], 1)
            pe.wait_ge(gla_loaded, 16 * 5)
            for c in range(KC):
                for part in (x_hi, x_lo):
                    last = mm(acc[0:GLA_RANK, 0, 0:TOK], g_tail[:, c, :], part[:, c, :].bitcast(F32),
                              start=(c == 0 and part is x_hi), stop=(c == KC - 1 and part is x_lo))
            last.then_inc(low_ready, 1)
            features_unit(n + 2, pairs[1])
            pe.wait_ge(low_copied, 1)
            for h in range(GLA_HEADS):
                last = mm(acc[:, 1 + h // 2, (h % 2) * TOK:(h % 2 + 1) * TOK], g_wg[:, h * GLA_DK:(h + 1) * GLA_DK],
                          g_low[:, :], start=(h % 2 == 0), stop=True, skip_group_check=True)
            last.then_inc(z_ready, 1)
            for u, kind in ((2, features_unit), (3, tokens_unit)):
                pe.wait_ge(pair_free[u % 2], u // 2)
                kind(n + 2 * u, pairs[u % 2])
            pe.wait_ge(dec_ready, 1)
            for tb in range(TB):
                for h in range(GLA_HEADS):
                    last = nc.tensor.transpose(acc[:, 3 * tb, h * P:(h + 1) * P], g_end[:, h, tb * P:(tb + 1) * P], ident)
                last.then_inc(kend_turned, 1)
            for tb in range(TB):
                for h in range(GLA_HEADS):
                    t = slice(tb * P, (tb + 1) * P)
                    last = mm(acc[:, 1 + tb, h * P:(h + 1) * P], g_dn[:, h, t], g_qT[:, h, t],
                              start=(h == 0), stop=True, skip_group_check=True)
                last.then_inc(gs_ready, 1)
            for u in range(4, 6):
                pe.wait_ge(pair_free[u % 2], u // 2)
                tokens_unit(n + 2 * u, pairs[u % 2])
            pe.wait_ge(kend_copied, TB)
            pe.wait_ge(gs_masked, TB)

            def update(c):
                rows, tb = slice((c % 2) * CHUNK, (c % 2 + 1) * CHUNK), c // 2
                for h in range(GLA_HEADS):
                    last = mm(pairs[c % 2][:, h // 2, (h % 2) * GLA_DV:(h % 2 + 1) * GLA_DV],
                              g_kend[rows, tb, h * GLA_DK:(h + 1) * GLA_DK], g_v[rows, tb, h * GLA_DV:(h + 1) * GLA_DV],
                              start=(h % 2 == 0), stop=True, skip_group_check=True)
                last.then_inc(upd_ready, 1)

            def gla_out(tb, h):
                return acc[:, 2 * tb + h // 2, (h % 2) * GLA_DV:(h % 2 + 1) * GLA_DV]

            def from_state(c):
                rows, tb = slice((c % 2) * CHUNK, (c % 2 + 1) * CHUNK), c // 2
                pe.wait_ge(state_ready, c)
                for h in range(GLA_HEADS):
                    last = mm(gla_out(tb, h)[rows], g_qT[:, h, c * CHUNK:(c + 1) * CHUNK], g_state[:, c - 1, h, :],
                              start=False, stop=True, skip_group_check=True)
                return last

            for c in range(2):
                pe.wait_ge(pair_free[c], 3)
                update(c)
            for tb in range(TB):
                for h in range(GLA_HEADS):
                    mm(gla_out(tb, h), g_s[:, tb, h, :], g_v[:, tb, h * GLA_DV:(h + 1) * GLA_DV],
                       start=(h % 2 == 0), stop=False, skip_group_check=True)
            from_state(1).then_inc(gla_o, 1)
            update(2)
            from_state(2)
            from_state(3).then_inc(gla_o, 1)
            turn("gla", g_v, mixed, [1, 2])
            for j in range(2):
                down(N_GLA_OUT + j, x_hi, x_lo, range(2 * j, 2 * j + 2), j == 0, False, ready=turns["gla"])
            last_pair(N_GLA_OUT + 2, operand_ready, [turns["gla"] + 3, turns["gla"] + 4],
                      [(x_hi, x_lo, c) for c in range(4, 8)])
            normed_unit(N_FFN1, pairs[0], 2)
            ffn(N_FFN1, 1)
            normed_unit(N_FFN2, pairs[0], 3)
            ffn(N_FFN2, 2)

            n = N_RET
            free = [3, 3]
            normed_unit(n, pairs[0], 4)
            for u in range(1, RET_UNITS):
                if u >= 2:
                    free[u % 2] += 1
                    pe.wait_ge(pair_free[u % 2], free[u % 2])
                (features_unit if u < 5 else tokens_unit)(n + 2 * u, pairs[u % 2])
                if u == 5:
                    pe.wait_ge(rope_done, 8)
                    for h in range(RET_HEADS):
                        for kb, cols in ((0, slice(0, TOK)), (1, slice(TOK, CAUSAL))):
                            for c in range(2):
                                last = mm(acc[:, h, cols], r_qk[:, 1, 2 * h + c, kb * P:(kb + 1) * P],
                                          r_qk[:, 0, 2 * h + c, kb * P:TOK], start=(c == 0), stop=(c == 1))
                        last.then_inc(rs_ready, 1)
            pe.wait_ge(rs_decayed, RET_HEADS)
            for u in range(2):
                pe.wait_ge(pair_free[u], free[u] + 1)
            for tb in range(TB):
                o = work if tb == 0 else acc
                for h in range(RET_HEADS):
                    for kb in range(tb + 1):
                        cols = slice(tb * P, (tb + 1) * P) if kb == 0 else slice(TOK, CAUSAL)
                        last = mm(o[:, h, :], r_s[:, h, cols], r_v[:, kb, h * RET_DV:(h + 1) * RET_DV],
                                  start=(kb == 0), stop=(kb == tb))
                last.then_inc(ret_o, 1)
            turn("ret", r_o, mixed, [3, 4])
            pe.wait_ge(operand_ready, turns["ret"] + KC // 2)
            turn("ret", r_o, mixed, [3, 4], KC)
            for j in range(6):
                hi, c = (x_hi, 2 * j) if j < 4 else (r_hi2, 2 * j - KC)
                lo = r_lo[:, 0:KC, :] if j < 4 else r_lo[:, KC:2 * KC, :]
                down(N_RET_OUT + j, hi, lo, range(c, c + 2), j == 0, False, ready=turns["ret"] + (0 if j < 4 else KC // 2))
            last_pair(N_RET_OUT + 6, operand_ready, [turns["ret"] + KC - 1, turns["ret"] + KC],
                      [(r_hi2, r_lo[:, KC:2 * KC, :], c) for c in range(4, 8)])
            normed_unit(N_FFN3, pairs[0], 5)
            ffn(N_FFN3, 3)

            n = N_SEC
            free = [9, 9]

            def unit(u, kind):
                if u >= 2:
                    free[u % 2] += 1
                    pe.wait_ge(pair_free[u % 2], free[u % 2])
                kind(n + 2 * u, pairs[u % 2])

            normed_unit(n, pairs[0], 6)
            unit(1, features_unit)
            unit(2, features_unit)
            pe.wait_ge(att_loaded, 48)
            for c in range(KC):
                for part in (x_hi, x_lo):
                    mm(acc[:, 0, 0:TOK], a_tail[:, c, 0:P], part[:, c, :].bitcast(F32),
                       start=(c == 0 and part is x_hi), stop=(c == KC - 1 and part is x_lo))
            for tb in range(TB):
                for c in range(KC):
                    for part in (x_hi, x_lo):
                        last = mm(acc[:, 1, 32 * tb:32 * tb + 24], part[:, c, tb * P:(tb + 1) * P].bitcast(F32), a_tail[:, c, P:],
                                  start=(c == 0 and part is x_hi), stop=(c == KC - 1 and part is x_lo))
            last.then_inc(small_ready, 1)
            unit(3, features_unit)
            unit(4, features_unit)
            pe.wait_ge(small_copied, 1)
            pe.wait_ge(pair_free[1], free[1])
            for p in range(6):
                if p >= 2:
                    pe.wait_ge(relu_done, p - 1)
                tb = 1 if p < 4 else 0
                width = TOK if tb else P
                per = NCOL // width
                for s in range(per):
                    for b in range(2):
                        h = (4 * p if tb else 8 * (p - 4)) + 2 * s + b
                        rows = slice(HEAD_DIM * b, HEAD_DIM * (b + 1))
                        last = mm(acc[:, 2 * (p % 2) + b, s * width:(s + 1) * width], a_qi[rows, h // 2, tb * P:(tb + 1) * P],
                                  a_ki[rows, 0:width], start=(s == 0), stop=True, skip_group_check=True)
                last.then_inc(dots_ready, 1)
            unit(5, features_unit)
            pe.wait_ge(lf_ready, 1)
            pe.wait_ge(relu_done, 6)
            mm(acc[0:HEADS, 0, 0:P], a_lf[:, 2, 0, :], tri, start=True, stop=True, skip_group_check=True)
            mm(acc[0:HEADS, 0, P:TOK], a_lf[:, 2, 0, :], ones, start=False, stop=False, skip_group_check=True)
            mm(acc[0:HEADS, 0, P:TOK], a_lf[:, 2, 1, :], tri, start=False, stop=True, skip_group_check=True).then_inc(cum_f, 1)
            unit(6, features_unit)
            unit(7, tokens_unit)

            def logits(br, st):
                for g, (tb, heads) in enumerate(((1, range(0, 4)), (1, range(4, 8)), (0, range(8)))):
                    if g == 2:
                        pe.wait_ge(max_ready, 3 * br + 1)
                    width = TOK if tb else P
                    for h in heads:
                        b, s = h % 2, (h - heads[0]) // 2
                        rows = slice(HEAD_DIM * b, HEAD_DIM * (b + 1))
                        out = acc[:, 2 * (g % 2) + b, s * width:(s + 1) * width]
                        last = mm(out, a_q[rows, st, h // 2, tb * P:(tb + 1) * P], a_k[rows, st, h // 2, 0:width],
                                  start=(s == 0), stop=(br == 0), skip_group_check=True)
                    if br == 1:
                        for h in heads:
                            b, s = h % 2, (h - heads[0]) // 2
                            out = acc[:, 2 * (g % 2) + b, s * width:(s + 1) * width]
                            pick = ident[0:HEADS, h:h + 1]
                            mm(out, a_cT[:, 0, tb * P:(tb + 1) * P], pick.to_broadcast([HEADS, width]),
                               start=False, stop=False, skip_group_check=True)
                            last = mm(out, pick.to_broadcast([HEADS, P]), a_cT[:, 1, 0:width],
                                      start=False, stop=True, skip_group_check=True)
                    last.then_inc(logits_ready, 1)

            def turn_p(br):
                pe.wait_ge(p_ready, 3 * br + 3)
                for h in range(HEADS):
                    if h >= 4:
                        pe.wait_ge(pt_act if h % 2 == 0 else pt_dve, 4 * br + (h - 4) // 2 + 1)
                    nc.tensor.transpose(acc[:, h % 4, 0:P], a_p[:, h, 0:P], ident)
                    nc.tensor.transpose(acc[:, h % 4, P:TOK], a_p[:, h, P:TOK], ident)
                    nc.tensor.transpose(acc[:, h % 4, TOK:CAUSAL], a_p[:, h, TOK:CAUSAL], ident).then_inc(p_turned, 1)

            def values(br, pt):
                for h in range(HEADS):
                    rows = slice(HEAD_DIM * (h % 2), HEAD_DIM * (h % 2 + 1))
                    c = h // 2
                    out = acc[rows, c // 2, (c % 2) * TOK:(c % 2 + 1) * TOK]
                    cols = slice(h * HEAD_DIM, (h + 1) * HEAD_DIM)
                    mm(out, a_v[:, br, 0, cols], pt[:, h, 0:TOK], start=(c % 2 == 0), stop=False, skip_group_check=True)
                    last = mm(out[:, P:TOK], a_v[:, br, 1, cols], pt[:, h, TOK:CAUSAL], start=False, stop=True,
                              skip_group_check=True)
                last.then_inc(o_ready, 1)

            pe.wait_ge(cT_copied, 1)
            logits(0, 0)
            unit(8, features_unit)
            turn_p(0)
            pe.wait_ge(pt_act, 4)
            pe.wait_ge(pt_dve, 4)
            values(0, a_pt)
            unit(9, features_unit)
            pe.wait_ge(o_done, 1)
            logits(1, 1)
            unit(10, tokens_unit)
            turn_p(1)
            pe.wait_ge(pt_act, 8)
            pe.wait_ge(pt_dve, 8)
            values(1, a_pt)
            pe.wait_ge(o_done, 2)
            pe.wait_ge(pair_free[0], free[0] + 1)
            for r in range(2):
                if r:
                    pe.wait_ge(sb_t, r)
                for i in range(4):
                    h = 4 * r + i
                    rows = slice(HEAD_DIM * (h % 2), HEAD_DIM * (h % 2 + 1))
                    for kb, cols in ((0, slice(0, TOK)), (1, slice(TOK, CAUSAL))):
                        last = mm(acc[:, i, cols], a_k[rows, 0, h // 2, kb * P:(kb + 1) * P], a_q[rows, 0, h // 2, kb * P:TOK],
                                  start=True, stop=True, skip_group_check=True)
                last.then_inc(sb_z, 1)
                pe.wait_ge(sb_l, r + 1)
                for i in range(4):
                    h = 4 * r + i
                    mm(acc[:, i, 0:TOK], later_of, a_pt[:, h, 0:TOK], start=True, stop=False, skip_group_check=True)
                    mm(acc[:, i, P:TOK], ones, a_pt[:, h, TOK:CAUSAL], start=False, stop=False, skip_group_check=True)
                    last = mm(acc[:, i, TOK:CAUSAL], later_of, a_pt[:, h, TOK:CAUSAL], start=False, stop=True,
                              skip_group_check=True)
                last.then_inc(sb_later, 1)
            pe.wait_ge(sb_a, 2)
            values(2, a_p)
            pe.wait_ge(o_done, 3)
            for u in range(2):
                pe.wait_ge(pair_free[u], free[u] + (1 if u == 0 else 0))
            with pe.Fori(0, 2) as half:
                for b in range(3):
                    m = N_MERGE + 3 * b
                    if b == 2:
                        pe.wait_ge(sig_done, half * 3 + 1)
                    tokens_unit(m, pairs[(b + 1) % 2], i=9 * half)
                    slot = slot_of(m + 2)
                    pe.wait_ge(lo_split, half * 9 + (m + 3))
                    if b == 2:
                        pe.wait_ge(up_used, half * 3 + 1)
                    for k in range(4):
                        cols = slice(k * NCOL, (k + 1) * NCOL)
                        for tb in range(TB):
                            t = slice(tb * P, (tb + 1) * P)
                            last = three(acc[:, 2 * (b % 2) + tb, :], a_oh[:, 4 * b + k, t], a_ol[:, 4 * b + k, t],
                                         w_hi[:, slot, cols], w_lo[:, slot, cols], k == 0, k == 3)
                    last.then_inc(weights_used, 1)
                pe.wait_ge(up_used, half * 3 + 3)
            turn("mrg", merged, merged_ready, [4, 4])
            for j in range(2):
                down(N_SEC_OUT + j, x_hi, x_lo, range(2 * j, 2 * j + 2), j == 0, False, ready=turns["mrg"])
            last_pair(N_SEC_OUT + 2, operand_ready, [turns["mrg"] + 3, turns["mrg"] + 4],
                      [(x_hi, x_lo, c) for c in range(4, 8)])
            normed_unit(N_FF2, pairs[1], 7)

            j0 = 4 * FFN_STEPS

            def ff2_step(s, first=False, i=0):
                n = N_FF2 + 4 * s - 2
                if s > 1:
                    pe.wait_ge(hid_done, i * 3 + j0 + s)
                features_unit(n, pairs[0], i=12 * i, between=(lambda: turn_hidden(j0, 4 * P)) if s == 1 else None)
                pe.wait_ge(hid_ready, i * 3 + j0 + s)
                at = 4 * ((s - 1) % 3)
                for k in range(2):
                    down(n + 2 + k, hid_hi, hid_lo, range(at + 2 * k, at + 2 * k + 2), first and k == 0, False, 12 * i)

            ff2_step(1, first=True)
            with pe.Fori(0, 2) as i:
                for s in range(2, 5):
                    ff2_step(s, i=i)
            last_pair(N_TILES - 2, hid_ready, [j0 + FF2_STEPS] * 2, hidden_chunks((1,), 4))


def _column_tiles(w):
    return [w[r:r + 512].reshape(4, P, NCOL).transpose(1, 0, 2).reshape(P, TILE) for r in (0, 512)]


def _row_tiles(w):
    return [w[r:r + 256].reshape(2, P, D).transpose(1, 0, 2).reshape(P, TILE) for r in range(0, w.shape[0], 256)]


def _weight_stream(a):
    def units(w, columns):
        return [t for c in columns for t in _column_tiles(w[:, c:c + NCOL])]

    def ffn(i, j):
        w_in, down = a["ffn_w_in"][i, j], _row_tiles(a["ffn_w_out"][i, j])
        up = [_column_tiles(np.concatenate([w_in[:, 256 * s:256 * s + 256], w_in[:, D_FF + 256 * s:D_FF + 256 * s + 256]], 1))
              for s in range(FFN_STEPS)]
        tiles = up[0] + up[1]
        for s in range(2, FFN_STEPS):
            tiles += up[s] + [down[s - 2]]
        return tiles + down[-2:]

    tiles = ffn(0, 0)
    tiles += units(a["gla_w_in"][0], (D, 0, NCOL, D + NCOL, 2 * D, 2 * D + NCOL)) + _row_tiles(a["gla_w_out"][0])
    tiles += ffn(0, 1) + ffn(1, 0)
    tiles += units(a["ret_w_in"][0], [2 * D, *range(0, 2 * D, NCOL), *range(2 * D + NCOL, 6 * D, NCOL)]) + _row_tiles(a["ret_w_out"][0])
    tiles += ffn(1, 1)
    w = a["w_in_2"][0]
    at = dict(zip("qa ka va qi ki wi qf kf vf fg qs ks vs gates".split(),
                  np.cumsum([0, 512, 512, 512, 1024, 64, 16, 512, 512, 512, 8, 512, 512, 512])))
    tiles += units(w, [at["va"], at["qi"], at["qi"] + NCOL] + [at[s] for s in "qa ka qf kf vf qs ks vs".split()])
    for half in range(2):
        for b in range(3):
            tiles += units(w, [at["gates"] + b * D + half * NCOL])
            tiles += _column_tiles(np.concatenate([a["w_branch_2"][0, b][:, half * NCOL:(half + 1) * NCOL]] * 2))[:1]
    tiles += _row_tiles(a["w_out_2"][0])
    up = [_column_tiles(a["w_ff1_2"][0][:, 512 * s:512 * s + 512]) for s in range(FF2_STEPS)]
    down = _row_tiles(a["w_ff2_2"][0])
    tiles += up[0]
    for s in range(1, FF2_STEPS):
        tiles += up[s] + down[2 * s - 2:2 * s]
    tiles += down[-2:]
    small = np.concatenate([w[:, at["ki"]:at["ki"] + 64]] * 2 + [w[:, at["wi"]:at["wi"] + 16], w[:, at["fg"]:at["fg"] + 8]], 1)
    return np.stack(tiles), small


def _constants():
    f = np.float32
    i = np.arange(P)
    square = np.stack([np.eye(P), i[:, None] <= i[None, :], i[:, None] > i[None, :], np.ones((P, P))], 1).astype(f)
    t = np.arange(TOK)
    keep = np.broadcast_to(t % CHUNK != 0, (P, TOK))
    same = (i[:, None] // CHUNK == i[None, :] // CHUNK) & (i[:, None] <= i[None, :])
    gla = np.concatenate([keep] + [same] * GLA_HEADS, 1).astype(f)
    inv = (np.float32(10000.0) ** (-np.arange(0, RET_DK, 2, dtype=f) / f(RET_DK))).astype(f)
    angle = (t.astype(f)[None, :] * inv[:, None]).astype(np.float64)
    log_g = np.log(1.0 - 2.0 ** (-5.0 - np.arange(RET_HEADS)))
    decays = []
    for h in range(RET_HEADS):
        gap = t[None, :] - t[:, None]
        d = np.where(gap >= 0, np.exp(np.maximum(gap, 0) * log_g[h]), 0.0) * RET_DK ** -0.5
        decays += [d[0:P, :], d[P:, P:]]
    ret = np.concatenate([np.cos(angle), np.sin(angle)] + decays, 1).astype(f)
    gap = np.concatenate([i[:, None] - i[None, :], P + i[:, None] - t[None, :]], 1)
    before = np.concatenate([i[:, None] < t[None, :], i[:, None] < i[None, :]], 1)
    att = np.stack([np.where(gap >= 0, 0.0, NEG), -gap, before], 1).astype(f)
    return square, gla, ret, att


def kernel(**inputs):
    import concourse.bacc as _bacc
    from concourse.bass_utils import run_bass_kernel_spmd as _run

    a = {k: np.asarray(v) for k, v in inputs.items()}
    weights, small = _weight_stream(a)
    square, gla, ret, att = _constants()
    gains = [a["ln_g"][i, j] for i in range(2) for j in range(3)] + [a["ln1_g_2"][0], a["ln2_g_2"][0]]
    shifts = [a["ln_b"][i, j] for i in range(2) for j in range(3)] + [a["ln1_b_2"][0], a["ln2_b_2"][0]]
    by_chunk = lambda w: w.reshape(KC, P, -1).transpose(1, 0, 2)
    arrays = {
        "weights": weights,
        "x": a["x"][0].reshape(TB, P, D),
        "constants": square,
        "ln_rows": np.stack([r for g, b in zip(gains, shifts) for r in (g, b)]),
        "gla_w_low": by_chunk(a["gla_w_in"][0][:, 3072:]),
        "gla_w_gate": a["gla_w_gate"][0],
        "gla_b_gate": a["gla_b_gate"][0].reshape(GLA_HEADS, P).T,
        "gla_constants": gla,
        "gla_gain": a["gla_norm_g"],
        "ret_constants": ret,
        "ret_gain": a["ret_norm_g"],
        "att_w_small": by_chunk(small),
        "att_constants": att,
        "b_forget": a["b_forget_2"],
    }
    nc = _bacc.Bacc("TRN2", target_bir_lowering=False, num_devices=1)
    io, data = {}, {}
    for name, v in arrays.items():
        data[f"in_{name}"] = np.ascontiguousarray(v)
        io[name] = nc.dram_tensor(f"in_{name}", v.shape, F32, kind="ExternalInput").ap()
    io["out"] = nc.dram_tensor("out_0", (TB, P, D), F32, kind="ExternalOutput").ap()
    build(nc, io)
    r = _run(nc, [data], core_ids=[0])
    return r.results[0]["out_0"].reshape(1, TOK, D)
```

```python
from contextlib import ExitStack

import concourse.bass as bass
import numpy as np
from concourse import mybir

F32 = mybir.dt.float32
F32R = mybir.dt.float32r
U32 = mybir.dt.uint32
ALU = mybir.AluOpType
ACT = mybir.ActivationFunctionType
AX_X = mybir.AxisListType.X

P = 128
D = 1024
TOK = 256
TB = TOK // P
KC = D // P
NCOL = 512
TILE = 2048
POOL_COLS = 768
RING = 3

D_FF = 2816
FFN_STEPS = D_FF // 256
GLA_HEADS, GLA_DK, GLA_DV, GLA_RANK, GLA_TAU = 4, 128, 256, 16, 16.0
CHUNK = 64
RET_HEADS, RET_DK, RET_DV = 4, 256, 512
HEADS, HEAD_DIM = 8, 64
IDX_HEADS = 16
TOPK = 64
FF2 = 4096
FF2_STEPS = FF2 // 512
ALPHA = 4.0 ** 0.25
ALPHA_2 = 2.0 ** 0.25
LN_EPS, NORM_EPS = 1e-5, 1e-6
NEG = -3.0e38
TAKEN = -3.4e38
CAUSAL = P + TOK

FFN_TILES = 3 * FFN_STEPS
GLA_UNITS, RET_UNITS, SEC_UNITS = 6, 12, 11
N_FFN0 = 0
N_GLA = N_FFN0 + FFN_TILES
N_GLA_OUT = N_GLA + 2 * GLA_UNITS
N_FFN1 = N_GLA_OUT + 4
N_FFN2 = N_FFN1 + FFN_TILES
N_RET = N_FFN2 + FFN_TILES
N_RET_OUT = N_RET + 2 * RET_UNITS
N_FFN3 = N_RET_OUT + 8
N_SEC = N_FFN3 + FFN_TILES
N_MERGE = N_SEC + 2 * SEC_UNITS
N_SEC_OUT = N_MERGE + 18
N_FF2 = N_SEC_OUT + 4
N_TILES = N_FF2 + 4 * FF2_STEPS
LAYER_STARTS = (N_FFN0, N_GLA, N_FFN1, N_FFN2, N_RET, N_FFN3, N_SEC, N_FF2, N_TILES)


def build(nc, io):
    ctx = ExitStack()
    with ctx:
        def sb(name, shape, dt=F32, where=ctx):
            return where.enter_context(nc.sbuf_tensor(name, shape, dt))

        def sem(name):
            return ctx.enter_context(nc.semaphore(name))

        raw = sb("weights_raw", [P, RING, TILE])
        w_hi = sb("weights_hi", [P, RING, TILE], F32R)
        w_lo = sb("weights_lo", [P, RING, TILE], F32R)
        x_hi = sb("operand_hi", [P, KC, TOK], F32R)
        x_lo = sb("operand_lo", [P, KC, TOK], F32R)
        xn = sb("normalised", [P, TB, D])
        resid = sb("residual", [P, TB, D])
        ln_rows = sb("ln_rows", [P, 2, D])
        cst = sb("constants", [P, 4, P])
        ident, tri, later_of, ones = (cst[:, i, :] for i in range(4))
        squares = sb("squares", [P, D])
        row_sum = sb("row_sum", [P, 2 * TB])
        minus_mean = sb("minus_mean", [P, TB])
        scaled_mean = sb("scaled_mean", [P, TB])
        variance = sb("variance", [P, TB])
        ln_rstd = sb("ln_rstd", [P, TB])
        stats = sb("stats", [P, 8, 6])
        mv = sb("mean_var", [P, 8, 2])
        rstd = sb("rstd", [P, 8])
        minus_half = sb("minus_half", [P, 8])
        bank = ctx.enter_context(nc.psum_tensor("psum", [P, 8, NCOL], F32))
        acc = bank[:, 0:4, :]
        work = bank[:, 4:8, :]

        as_pair = lambda t: t.rearrange("p (a b) t -> p a (b t)", a=2)
        two = lambda t: t.rearrange("p (c t) -> p c t", c=2)

        with ExitStack() as ph:
            silu_g = sb("silu_gate", [P, 2, TOK], F32, ph)
            hid = sb("hidden", [P, 4, TOK], F32, ph)
            hid_hi = sb("hidden_hi", [P, 12, TOK], F32R, ph)
            hid_lo = sb("hidden_lo", [P, 12, TOK], F32R, ph)
        with ExitStack() as ph:
            g_qT = sb("gla_qT", [P, GLA_HEADS, TOK], F32, ph)
            g_kT = sb("gla_kT", [P, GLA_HEADS, TOK], F32, ph)
            g_v = sb("gla_v", [P, TB, D], F32, ph)
            g_r = sb("gla_r", [P, TB, D], F32, ph)
            g_z = sb("gla_z", [P, GLA_HEADS, TOK], F32, ph)
            g_t = sb("gla_t", [P, GLA_HEADS, TOK], F32, ph)
            g_cum = sb("gla_cum", [P, GLA_HEADS, TOK], F32, ph)
            g_up = sb("gla_exp_cum", [P, GLA_HEADS, TOK], F32, ph)
            g_dn = sb("gla_exp_minus_cum", [P, GLA_HEADS, TOK], F32, ph)
            g_end = sb("gla_exp_to_end", [P, GLA_HEADS, TOK], F32, ph)
            g_kend = sb("gla_k_end", [P, TB, GLA_HEADS * GLA_DK], F32, ph)
            g_s = sb("gla_scores", [P, TB, GLA_HEADS, P], F32, ph)
            g_state = sb("gla_state", [P, 3, GLA_HEADS, GLA_DV], F32, ph)
            g_low = sb("gla_low", [GLA_RANK, TOK], F32, ph)
            g_tail = sb("gla_w_low", [P, KC, P], F32, ph)
            g_tail_hi = sb("gla_w_low_hi", [P, KC, P], F32R, ph)
            g_tail_lo = sb("gla_w_low_lo", [P, KC, P], F32R, ph)
            g_wg = sb("gla_w_gate", [GLA_RANK, GLA_HEADS * GLA_DK], F32, ph)
            g_bg = sb("gla_b_gate", [P, GLA_HEADS], F32, ph)
            g_gain = sb("gla_gain", [P, GLA_DV], F32, ph)
            g_cst = sb("gla_constants", [P, TOK + GLA_HEADS * P], F32, ph)
            g_ss = sb("gla_sumsq", [P, 8], F32, ph)
            g_junk = sb("gla_junk", [P, GLA_DV], F32, ph)
            chunk_keep = g_cst[:, 0:TOK]
            chunk_mask = g_cst[:, TOK:TOK + GLA_HEADS * P]
        with ExitStack() as ph:
            r_qk = sb("ret_qkT", [P, 2, KC, TOK], F32, ph)
            r_v = sb("ret_v", [P, TB, 2 * D], F32, ph)
            r_g = sb("ret_g", [P, TB, 2 * D], F32, ph)
            r_rot = sb("ret_rot", [P, 2, 2, 2, TOK], F32, ph)
            r_after = r_rot[:, :, :, :, :].rearrange("p a b c t -> p (a b c t)")
            r_s = r_after[:, 0:RET_HEADS * CAUSAL].rearrange("p (h c) -> p h c", h=RET_HEADS)
            r_gain = r_after[:, RET_HEADS * CAUSAL:RET_HEADS * CAUSAL + RET_DV]
            r_lo = sb("ret_out_lo", [P, 2 * KC, TOK], F32R, ph)
            r_hi2 = sb("ret_out_hi", [P, KC, TOK], F32R, ph)
            r_cst = sb("ret_constants", [P, 2 * TOK + RET_HEADS * CAUSAL], F32, ph)
            r_o = r_qk[:, :, :, :].rearrange("p a c t -> p a (c t)")
            cos, sin = r_cst[:, 0:TOK], r_cst[:, TOK:2 * TOK]
            decay = r_cst[:, 2 * TOK:].rearrange("p (h c) -> p h c", h=RET_HEADS)
        with ExitStack() as ph:
            a_q = sb("att_qT", [P, 2, 4, TOK], F32, ph)
            a_k = sb("att_kT", [P, 2, 4, TOK], F32, ph)
            a_v = sb("att_v", [P, 3, TB, HEADS * HEAD_DIM], F32, ph)
            a_ki = sb("att_kiT", [P, TOK], F32, ph)
            a_wf = sb("att_wi_fg", [P, TB, IDX_HEADS + HEADS], F32, ph)
            a_lf = sb("att_log_f", [P, 3, TB, HEADS], F32, ph)
            a_cT = sb("att_minus_cT", [HEADS, TOK], F32, ph)
            a_c = sb("att_c", [P, TB, HEADS], F32, ph)
            a_cst = sb("att_constants", [P, 3, CAUSAL], F32, ph)
            a_bf = sb("att_b_forget", [P, HEADS], F32, ph)
            a_sc = sb("att_score", [P, 2, CAUSAL], F32, ph)
            a_top = sb("att_top8", [P, 8], F32, ph)
            a_max = sb("att_max", [P, 2, TB, HEADS], F32, ph)
            a_sum = sb("att_sum", [P, TB, HEADS], F32, ph)
            a_p = sb("att_p", [P, HEADS, CAUSAL], F32, ph)
            a_pt = sb("att_pT", [P, HEADS, CAUSAL], F32, ph)
            causal, negdist, strict = (a_cst[:, i, :] for i in range(3))
            with ExitStack() as sub:
                a_tail = sb("att_w_small", [P, KC, P], F32, sub)
                a_tail_hi = sb("att_w_small_hi", [P, KC, P], F32R, sub)
                a_tail_lo = sb("att_w_small_lo", [P, KC, P], F32R, sub)
                a_qi = sb("att_qiT", [P, 8, TOK], F32, sub)
            a_oh = sb("att_out_hi", [P, 12, TOK], F32R, ph)
            a_ol = sb("att_out_lo", [P, 12, TOK], F32R, ph)
            relu = a_pt[:, :, :].rearrange("p h c -> p (h c)")[:, 0:2048].rearrange("p (b c) -> p b c", b=2)
            sig = [as_pair(a_q[:, 1]), as_pair(a_k[:, 1]), squares[:, :].rearrange("p (t c) -> p t c", t=TB), a_v[:, 0]]
            gated = a_v[:, 1]
            merged = xn

        weight_loaded = [sem(f"weight_loaded{i}") for i in range(RING)]
        hi_split = sem("hi_split")
        piece_hi = sem("piece_hi")
        piece_split = sem("piece_split")
        lo_split = sem("lo_split")
        weights_used = sem("weights_used")
        pair_free = [sem("pair_free0"), sem("pair_free1")]
        x_loaded, ident_loaded = [sem("x_loaded0"), sem("x_loaded1")], sem("ident_loaded")
        consts_loaded = sem("consts_loaded")
        acc_ready = sem("acc_ready")
        mean_ready = sem("mean_ready")
        var_ready, rstd_ready = sem("var_ready"), sem("rstd_ready")
        xn_ready, resid_ready = sem("xn_ready"), sem("resid_ready")
        rows_loaded = sem("rows_loaded")
        turned, turned_hi, operand_ready = sem("turned"), sem("turned_hi"), sem("operand_ready")
        silu_done, hid_done = sem("silu_done"), sem("hid_done")
        hid_turned, hid_hi_done, hid_ready = sem("hid_turned"), sem("hid_hi_done"), sem("hid_ready")
        dve_step, pool_step, act_step = sem("dve_step"), sem("pool_step"), sem("act_step")
        out_stored = sem("out_stored")
        gla_loaded, ret_loaded, att_loaded = sem("gla_loaded"), sem("ret_loaded"), sem("att_loaded")
        low_ready, low_copied, z_ready = sem("low_ready"), sem("low_copied"), sem("z_ready")
        naz_ready, ln1p_ready, cum_ready = sem("naz_ready"), sem("ln1p_ready"), sem("cum_ready")
        exp_ready, dec_ready = sem("exp_ready"), sem("dec_ready")
        kend_turned, kend_copied = sem("kend_turned"), sem("kend_copied")
        gs_ready, gs_masked = sem("gs_ready"), sem("gs_masked")
        upd_ready, state_ready, gla_o = sem("upd_ready"), sem("state_ready"), sem("gla_o")
        ss_ready, gate_ready, mixed = sem("ss_ready"), sem("gate_ready"), sem("mixed")
        rot_ready, rope_done = sem("rot_ready"), sem("rope_done")
        rs_ready, rs_decayed = sem("rs_ready"), sem("rs_decayed")
        ret_o, ret_normed = sem("ret_o"), sem("ret_normed")
        unit_copied = sem("unit_copied")
        small_ready, small_copied = sem("small_ready"), sem("small_copied")
        small_turned, wf_copied, ki_doubled = sem("small_turned"), sem("wf_copied"), sem("ki_doubled")
        tail_hi_done, tail_ready = sem("tail_hi_done"), sem("tail_ready")
        dots_ready, relu_done, dots_used = sem("dots_ready"), sem("relu_done"), sem("dots_used")
        lf_exp, lf_ln, lf_ready, cum_f, cT_copied = sem("lf_exp"), sem("lf_ln"), sem("lf_ready"), sem("cum_f"), sem("cT_copied")
        lf_in = sem("lf_in")
        logits_ready, max_ready, exp_done = sem("logits_ready"), sem("max_ready"), sem("exp_done")
        weight_ready, p_ready = sem("weight_ready"), sem("p_ready")
        p_turned, pt_act, pt_dve = sem("p_turned"), sem("pt_act"), sem("pt_dve")
        o_ready, o_hi_done, o_done = sem("o_ready"), sem("o_hi_done"), sem("o_done")
        sb_z, sb_ln, sb_l, sb_later, sb_t, sb_exp, sb_a = (
            sem(n) for n in ("sb_z", "sb_ln", "sb_l", "sb_later", "sb_t", "sb_exp", "sb_a"))
        sig_done, up_used, merged_ready = sem("sig_done"), sem("up_used"), sem("merged_ready")

        pairs = [work[:, 0:2, :], work[:, 2:4, :]]
        quarter_pair = [pairs[0], pairs[0], pairs[1], pairs[0]]
        ret_hi = lambda c: r_hi2[:, c:c + 2, :] if c < KC else x_hi[:, c - KC:c - KC + 2, :]
        block_acc = lambda tb: acc[:, 2 * tb:2 * tb + 2, :]
        slot_of = lambda n: n % RING

        order = ["ln1", "gla", "ln2", "ln3", "ln4", "ret", "ln5", "ln6", "mrg", "ln7"]
        turns, at = {"x": 0}, KC // 2
        for what in order:
            turns[what] = at
            at += KC if what == "ret" else KC // 2

        dot_passes = ((1, 0), (1, 4), (0, 0), (1, 8), (1, 12), (0, 8))
        groups = ((1, range(0, 4)), (1, range(4, 8)), (0, range(8)))
        block_cols = lambda tb: slice(P, CAUSAL) if tb else slice(0, P)
        merge = [("gate", 0, 0), ("gate", 0, 1), ("gate", 0, 2), ("up", 0, 0), ("up", 0, 1),
                 ("gate", 1, 0), ("gate", 1, 1), ("gate", 1, 2), ("up", 1, 0), ("up", 1, 1), ("up", 0, 2), ("up", 1, 2)]
        merge_tile = [N_MERGE + sum(2 if m[0] == "gate" else 1 for m in merge[:j]) for j in range(len(merge))]
        sig_of = lambda half, b: sig[3 if (half, b) == (1, 2) else b]

        pair_count = lambda u: 9 + u // 2 + 1

        block = ctx.enter_context(nc.Block())

        @block.sync
        def _(sp):
            sp.dma_start(xn[:, 0, :], io["x"][0]).then_inc(x_loaded[0], 16)
            for n in range(RING):
                if n == 2:
                    sp.dma_start(xn[:, 1, :], io["x"][1]).then_inc(x_loaded[1], 16)
                sp.dma_start(raw[:, n, :], io["weights"][n]).then_inc(weight_loaded[n], 16)
            rounds = (N_TILES - RING) // RING
            with sp.Fori(0, rounds) as i:
                for n in range(RING, 2 * RING):
                    src = io["weights"][bass.ds(sp.snap(i * RING + n), 1)].rearrange("a p n -> (a p) n")
                    sp.wait_ge(lo_split, i * RING + (n - RING + 1))
                    sp.dma_start(raw[:, n % RING, :], src).then_inc(weight_loaded[n % RING], 16)
            for n in range(RING * (rounds + 1), N_TILES):
                sp.wait_ge(lo_split, n - RING + 1)
                sp.dma_start(raw[:, n % RING, :], io["weights"][n]).then_inc(weight_loaded[n % RING], 16)
            for tb in range(TB):
                for b in range(2):
                    cols = slice(b * NCOL, (b + 1) * NCOL)
                    sp.wait_ge(xn_ready, 4 * 7 + 2 * tb + b + 1)
                    sp.dma_start(io["out"][tb][:, cols], xn[:, tb, cols]).then_inc(out_stored, 16)
            sp.wait_ge(out_stored, 16 * 2 * TB)

        @block.gpsimd
        def _(pool):
            step = [0]

            def link(ins):
                step[0] += 1
                ins.then_inc(pool_step, 1)
                pool.wait_ge(pool_step, step[0])

            powers = [0]

            def inverse_root(out, var, scale, eps, n):
                powers[0] += 1
                pool.wait_ge(var_ready, powers[0])
                link(nc.gpsimd.tensor_scalar(out, var, scale, eps, ALU.mult, ALU.add))
                nc.gpsimd.tensor_tensor(out, out, minus_half[:, 0:n], ALU.pow).then_inc(rstd_ready, 1)

            link(nc.gpsimd.memset(minus_half[:, :], -0.5))

            def split_lo_piece(n, ln):
                s = slot_of(n)
                pool.wait_ge(piece_hi, ln)
                nc.gpsimd.tensor_tensor(w_lo[:, s, 0:POOL_COLS], raw[:, s, 0:POOL_COLS], w_hi[:, s, 0:POOL_COLS].bitcast(F32),
                                        ALU.subtract).then_inc(piece_split, 1)

            def load_rows(ln):
                for j in range(2):
                    pool.dma_start(ln_rows[:, j, :], io["ln_rows"][2 * (ln - 1) + j:2 * (ln - 1) + j + 1, :]
                                   .to_broadcast([P, D])).then_inc(rows_loaded, 16)

            def residual(tb, alpha):
                nc.gpsimd.tensor_scalar(resid[:, tb, :], xn[:, tb, :], alpha, 0.0, ALU.mult, ALU.add).then_inc(resid_ready, 1)

            def layer_norm(ln):
                for tb in range(TB):
                    inverse_root(ln_rstd[:, tb:tb + 1], variance[:, tb:tb + 1], 1.0, LN_EPS, 1)
                    if ln < 8 and tb == 0:
                        split_lo_piece(LAYER_STARTS[ln] + 1, ln)
                    if ln < 8:
                        pool.wait_ge(xn_ready, 4 * (ln - 1) + 2 * tb + 2)
                        residual(tb, ALPHA if ln < 6 else ALPHA_2)
                if ln < 8:
                    load_rows(ln + 1)

            for tb in range(TB):
                pool.wait_ge(x_loaded[tb], 16)
                residual(tb, ALPHA)
            load_rows(1)
            pool.dma_start(cst[:, 1:, :], io["constants"][:, 1:, :]).then_inc(consts_loaded, 16)
            layer_norm(1)
            pool.wait_ge(gla_loaded, 16 * 5)

            def gate_gain(tb, heads):
                for h in heads:
                    cols = slice(h * GLA_DV, (h + 1) * GLA_DV)
                    last = nc.gpsimd.tensor_tensor(g_r[:, tb, cols], g_r[:, tb, cols], g_gain[:, :], ALU.mult)
                last.then_inc(gate_ready, 1)

            pool.wait_ge(unit_copied, 1)
            for tb in range(TB):
                gate_gain(tb, (0, 1))
            inverse_root(rstd[:, 0:4], g_ss[:, 0:4], 1.0 / GLA_DV, NORM_EPS, 4)
            pool.wait_ge(unit_copied, 2)
            for tb in range(TB):
                gate_gain(tb, (2, 3))
            inverse_root(rstd[:, 4:8], g_ss[:, 4:8], 1.0 / GLA_DV, NORM_EPS, 4)
            layer_norm(2)
            layer_norm(3)
            layer_norm(4)
            for u in range(4):
                for j in range(2):
                    pool.wait_ge(rot_ready, 2 * u + j + 1)
                    head = 2 * (u % 2) + j
                    qk = r_qk[:, u // 2, 2 * head:2 * head + 2, :]
                    by_cos, by_sin = r_rot[:, j, 0], r_rot[:, j, 1]
                    nc.gpsimd.tensor_tensor(qk[:, 0, :], by_cos[:, 0, :], by_sin[:, 1, :], ALU.subtract)
                    nc.gpsimd.tensor_tensor(qk[:, 1, :], by_sin[:, 0, :], by_cos[:, 1, :], ALU.add).then_inc(rope_done, 1)
            pool.wait_ge(ret_loaded, 32)

            def head_gain(h):
                pool.wait_ge(unit_copied, 3 + h)
                for tb in range(TB):
                    cols = slice(h * RET_DV, (h + 1) * RET_DV)
                    last = nc.gpsimd.tensor_tensor(r_g[:, tb, cols], r_g[:, tb, cols], r_gain, ALU.mult)
                last.then_inc(gate_ready, 1)

            head_gain(0)
            inverse_root(rstd[:, 0:4], mv[:, 0:4, 1], 1.0, NORM_EPS, 4)
            head_gain(1)
            inverse_root(rstd[:, 4:8], mv[:, 4:8, 1], 1.0, NORM_EPS, 4)
            head_gain(2)
            head_gain(3)
            layer_norm(5)
            layer_norm(6)
            for br in range(2):
                for g, (tb, heads) in enumerate(groups):
                    pool.wait_ge(weight_ready, 3 * br + g + 1)
                    for h in heads:
                        p = a_p[:, h, block_cols(tb)]
                        last = nc.gpsimd.tensor_scalar(p, p, a_sum[:, tb, h:h + 1], 0.0, ALU.mult, ALU.add)
                    last.then_inc(p_ready, 1)
            layer_norm(7)
            layer_norm(8)

        @block.scalar
        def _(act):
            step = [0]

            def link(ins):
                step[0] += 1
                ins.then_inc(act_step, 1)
                act.wait_ge(act_step, step[0])

            def split_hi(n, i=0, first_piece=False):
                if n >= N_TILES:
                    return
                s = slot_of(n)
                act.wait_ge(weight_loaded[s], i * 16 + 16 * (n // RING + 1))
                if n >= RING:
                    act.wait_ge(weights_used, i * RING + (n - RING + 1))
                if first_piece:
                    nc.scalar.activation(w_hi[:, s, 0:POOL_COLS], raw[:, s, 0:POOL_COLS], ACT.Copy).then_inc(piece_hi, 1)
                whole = slice(POOL_COLS if first_piece else 0, 2 * D)
                nc.scalar.activation(w_hi[:, s, whole], raw[:, s, whole], ACT.Copy).then_inc(hi_split, 1)

            def turn_hi(what, hi, banks, swap=0):
                for b in banks:
                    act.wait_ge(turned, turns[what] + b + 1)
                    nc.scalar.activation(hi[:, 2 * b:2 * b + 2, :].rearrange("p c t -> p (c t)"), work[:, (b + swap) % 4, :],
                                         ACT.Copy).then_inc(turned_hi, 1)

            def rows_hi(what, tb, banks):
                for b in range(2):
                    act.wait_ge(turned, turns[what] + 2 * tb + b + 1)
                    nc.scalar.activation(x_hi[:, 4 * b:4 * b + 4, tb * P:(tb + 1) * P],
                                         banks[:, b, :].rearrange("p (c t) -> p c t", c=4),
                                         ACT.Copy).then_inc(turned_hi, 1)

            def layer_norm(ln, end):
                for tb in range(TB):
                    act.wait_ge(mean_ready, 2 * (ln - 1) + tb + 1)
                    link(nc.scalar.activation(squares[:, :], xn[:, tb, :], ACT.Square, bias=scaled_mean[:, tb:tb + 1],
                                              scale=D ** -0.5, accum_out=variance[:, tb:tb + 1]))
                    act.sem_inc(var_ready, 1)
                    if ln == 8:
                        continue
                    if tb == 0 and ln != 2:
                        split_hi(end)
                    if tb == 0 and ln == 2:
                        split_hi(end + 1, first_piece=True)
                    if tb == 1:
                        split_hi(end + 2)
                    rows_hi(f"ln{ln}", tb, block_acc(tb))
                    if tb == 0 and ln != 2:
                        split_hi(end + 1, first_piece=True)

            def ffn(n0, f):
                j0 = f * FFN_STEPS

                def silu(n, gate, i=0):
                    act.wait_ge(weights_used, i * 9 + n + 2)
                    nc.scalar.activation(silu_g[:, :, :], gate, ACT.Silu).then_inc(silu_done, 1)

                def hidden_hi(j, slot, src, i=0):
                    nc.scalar.activation(hid_hi[:, 2 * slot:2 * slot + 2, :], src, ACT.Copy).then_inc(hid_hi_done, 1)

                split_hi(n0 + 3)
                silu(n0, pairs[0][:, :, 0:TOK])
                split_hi(n0 + 4)
                act.wait_ge(hid_turned, f + 1)
                hidden_hi(j0, 0, two(acc[:, 0, :]))

                def step(j, n, ahead, gate_up, i=0):
                    if j > 2:
                        split_hi(ahead - 1, 3 * i)
                    split_hi(ahead, 3 * i)
                    silu(n, two(gate_up[:, 0, :]), i)
                    split_hi(ahead + 1, 3 * i)
                    act.wait_ge(hid_done, i * 3 + j0 + j + 1)
                    hidden_hi(j0 + j, j % 3, hid[:, 0:2, :], i)

                step(1, n0 + 2, n0 + 5, pairs[1])
                step(2, n0 + 4, n0 + 7, pairs[0])
                for j in range(3, 5):
                    step(j, n0 + 3 * j - 2, n0 + 3 * j + 1, pairs[1])
                with act.Fori(0, 2) as i:
                    for j in range(5, 8):
                        step(j, n0 + 3 * j - 2, n0 + 3 * j + 1, pairs[1], i)

            def unit(n, u, out, func=ACT.Copy, scale=1.0):
                split_hi(n + 3)
                act.wait_ge(weights_used, n + 2)
                src = pairs[u % 2]
                ins = nc.scalar.activation(out, src, func, scale=scale)
                ins.then_inc(pair_free[u % 2], 1)
                split_hi(n + 4)

            act.dma_start(ident, io["constants"][:, 0, :]).then_inc(ident_loaded, 16)
            rows_hi("x", 0, block_acc(0))
            split_hi(0)
            split_hi(1)
            rows_hi("x", 1, block_acc(1))
            split_hi(2)
            ffn(N_FFN0, 0)
            for dst, name in ((g_tail, "gla_w_low"), (g_wg, "gla_w_gate"), (g_bg, "gla_b_gate"),
                              (g_cst, "gla_constants")):
                act.dma_start(dst[tuple([slice(None)] * len(dst.shape))], io[name]).then_inc(gla_loaded, 16)
            act.dma_start(g_gain[:, :], io["gla_gain"].to_broadcast([P, GLA_DV])).then_inc(gla_loaded, 16)
            layer_norm(1, N_GLA)

            n = N_GLA
            act.wait_ge(gla_loaded, 16 * 5)
            nc.scalar.activation(g_tail_hi[:, :, :], g_tail[:, :, :], ACT.Copy).then_inc(tail_hi_done, 1)
            unit(n, 0, g_v[:, :, 0:512])
            act.wait_ge(low_ready, 1)
            nc.scalar.activation(g_low[:, :], acc[0:GLA_RANK, 0, 0:TOK], ACT.Copy).then_inc(low_copied, 1)
            flat = lambda t: t.rearrange("p h t -> p (h t)")
            unit(n + 2, 1, g_v[:, :, 512:1024])
            act.wait_ge(naz_ready, 1)
            link(nc.scalar.activation(g_t[:, :, :], g_t[:, :, :], ACT.Exp))
            nc.scalar.activation(g_t[:, :, :], g_t[:, :, :], ACT.Ln, bias=1.0).then_inc(ln1p_ready, 1)
            unit(n + 4, 2, as_pair(g_qT[:, :, :]), scale=GLA_DK ** -0.5)
            act.wait_ge(cum_ready, 1)
            nc.scalar.activation(g_up[:, :, :], g_cum[:, :, :], ACT.Exp, scale=1.0 / GLA_TAU)
            nc.scalar.activation(g_dn[:, :, :], g_cum[:, :, :], ACT.Exp, scale=-1.0 / GLA_TAU)
            nc.scalar.activation(g_end[:, :, :], g_end[:, :, :], ACT.Exp, scale=1.0 / GLA_TAU).then_inc(exp_ready, 1)
            unit(n + 6, 3, as_pair(g_kT[:, :, :]))
            split_hi(n + 11)
            for tb in range(TB):
                act.wait_ge(kend_turned, tb + 1)
                nc.scalar.activation(g_kend[:, tb, :], acc[:, 3 * tb, :], ACT.Copy).then_inc(kend_copied, 1)

            def gate_copied(u):
                act.wait_ge(pair_free[u % 2], u // 2 + 1)
                act.sem_inc(unit_copied, 1)

            def square_sums(tb):
                act.wait_ge(gla_o, tb + 1)
                for h in range(GLA_HEADS):
                    src = acc[:, 2 * tb + h // 2, (h % 2) * GLA_DV:(h % 2 + 1) * GLA_DV]
                    link(nc.scalar.activation(g_junk[:, :], src, ACT.Square,
                                              accum_out=g_ss[:, 4 * tb + h:4 * tb + h + 1]))
                act.sem_inc(var_ready, 1)

            act.wait_ge(weights_used, n + 10)
            nc.scalar.activation(g_r[:, :, 0:512], pairs[0], ACT.Silu).then_inc(pair_free[0], 1)
            gate_copied(4)
            split_hi(n + 12)
            split_hi(n + 13)
            square_sums(0)
            act.wait_ge(weights_used, n + 12)
            nc.scalar.activation(g_r[:, :, 512:1024], pairs[1], ACT.Silu).then_inc(pair_free[1], 1)
            gate_copied(5)
            split_hi(n + 14)
            rows_hi("gla", 0, pairs[1])
            square_sums(1)
            rows_hi("gla", 1, pairs[0])
            for j in range(2):
                split_hi(N_GLA_OUT + j + 3)
            layer_norm(2, N_FFN1)
            ffn(N_FFN1, 1)
            layer_norm(3, N_FFN2)
            ffn(N_FFN2, 2)
            act.dma_start(r_cst[:, :], io["ret_constants"]).then_inc(ret_loaded, 16)
            layer_norm(4, N_RET)

            n = N_RET
            unit(n, 0, r_v[:, :, 0:512])
            for u in range(1, 5):
                n += 2
                split_hi(n + 3)
                split_hi(n + 4)
            n += 2
            act.wait_ge(rope_done, 8)
            act.dma_start(r_gain, io["ret_gain"].to_broadcast([P, RET_DV])).then_inc(ret_loaded, 16)
            for u in range(5, 8):
                unit(n, u, r_v[:, :, (u - 4) * 512:(u - 3) * 512])
                n += 2

            def quarter_hi(h):
                for b in range(2):
                    act.wait_ge(turned, turns["ret"] + 2 * h + b + 1)
                    nc.scalar.activation(ret_hi(4 * h + 2 * b).rearrange("p c t -> p (c t)"), quarter_pair[h][:, b, :],
                                         ACT.Copy).then_inc(turned_hi, 1)

            for u in range(8, 12):
                split_hi(n + 3)
                if u == 11:
                    quarter_hi(0)
                act.wait_ge(weights_used, n + 2)
                nc.scalar.activation(r_g[:, :, (u - 8) * 512:(u - 7) * 512], pairs[u % 2], ACT.Silu).then_inc(pair_free[u % 2], 1)
                act.wait_ge(pair_free[u % 2], 3 + u // 2 + 1)
                act.sem_inc(unit_copied, 1)
                split_hi(n + 4)
                n += 2
            for h in range(1, RET_HEADS):
                quarter_hi(h)
                split_hi(N_RET_OUT + 2 + h)
            for j in range(6, 8):
                split_hi(N_RET_OUT + j)
            layer_norm(5, N_FFN3)
            ffn(N_FFN3, 3)
            act.dma_start(a_tail[:, :, :], io["att_w_small"]).then_inc(att_loaded, 16)
            act.dma_start(a_cst[:, :, :], io["att_constants"]).then_inc(att_loaded, 16)
            act.dma_start(a_bf[:, :], io["b_forget"].to_broadcast([P, HEADS])).then_inc(att_loaded, 16)
            layer_norm(6, N_SEC)

            n = N_SEC

            def part(u, out, scale=1.0, mid=None):
                split_hi(n + 2 * u + 3)
                if mid:
                    mid()
                act.wait_ge(weights_used, n + 2 * u + 2)
                nc.scalar.activation(out, pairs[u % 2], ACT.Copy, scale=scale).then_inc(pair_free[u % 2], 1)

            def relu_dots(p):
                act.wait_ge(dots_ready, p + 1)
                if p >= 2:
                    act.wait_ge(dots_used, p - 1)
                nc.scalar.activation(relu[:, p % 2, :].rearrange("p (b c) -> p b c", b=2),
                                     acc[:, 2 * (p % 2):2 * (p % 2) + 2, :], ACT.Relu).then_inc(relu_done, 1)

            def copy_sums():
                act.wait_ge(cum_f, 1)
                nc.scalar.activation(a_c[:, :, :], acc[:, 1, 0:TB * HEADS].rearrange("p (t h) -> p t h", t=TB), ACT.Copy)
                nc.scalar.activation(a_cT[:, :], acc[0:HEADS, 0, 0:TOK], ACT.Copy, scale=-1.0).then_inc(cT_copied, 1)

            def softmax_exp(br, g):
                tb, heads = groups[g]
                act.wait_ge(max_ready, 3 * br + g + 1)
                for h in heads:
                    ins = nc.scalar.activation(a_p[:, h, block_cols(tb)], a_p[:, h, block_cols(tb)], ACT.Exp,
                                               bias=a_max[:, 1, tb, h:h + 1], accum_out=a_sum[:, tb, h:h + 1])
                ins.then_inc(exp_done, 1)

            def pt_copy(br, heads):
                for h in heads:
                    act.wait_ge(p_turned, 8 * br + h + 1)
                    nc.scalar.activation(a_pt[:, h, :], acc[:, h % 4, 0:CAUSAL], ACT.Copy).then_inc(pt_act, 1)

            def out_hi(br):
                act.wait_ge(o_ready, br + 1)
                nc.scalar.activation(as_pair(a_oh[:, 4 * br:4 * br + 4, :]), acc[:, 0:2, :], ACT.Copy).then_inc(o_hi_done, 1)

            def stick_ln(r):
                rows = slice(4 * r, 4 * r + 4)
                act.wait_ge(sb_z, r + 1)
                link(nc.scalar.activation(a_pt[:, rows, :], acc[:, 0:4, 0:CAUSAL], ACT.Abs))
                link(nc.scalar.activation(a_pt[:, rows, :], a_pt[:, rows, :], ACT.Exp, scale=-1.0))
                nc.scalar.activation(a_pt[:, rows, :], a_pt[:, rows, :], ACT.Ln, bias=1.0).then_inc(sb_ln, 1)

            def stick_exp(r):
                rows = slice(4 * r, 4 * r + 4)
                act.wait_ge(sb_t, r + 1)
                nc.scalar.activation(a_p[:, rows, :], a_p[:, rows, :], ACT.Exp).then_inc(sb_exp, 1)

            def gate(j):
                kind, half, b = merge[j]
                act.wait_ge(weights_used, merge_tile[j] + 2)
                if half and b < 2:
                    act.wait_ge(up_used, b + 1)
                u = SEC_UNITS + j
                ins = nc.scalar.activation(sig_of(half, b), pairs[u % 2], ACT.Sigmoid)
                ins.then_inc(pair_free[u % 2], 1)
                act.wait_ge(pair_free[u % 2], pair_count(u))
                act.sem_inc(sig_done, 1)

            act.wait_ge(att_loaded, 48)
            nc.scalar.activation(a_tail_hi[:, :, :], a_tail[:, :, :], ACT.Copy).then_inc(tail_hi_done, 1)
            part(0, a_v[:, 0])
            split_hi(n + 4)
            act.wait_ge(small_ready, 1)
            rows = HEAD_DIM + IDX_HEADS + HEADS
            nc.scalar.activation(a_ki[0:rows, :], acc[0:rows, 0, 0:TOK], ACT.Copy).then_inc(small_copied, 1)

            def copy_small():
                act.wait_ge(small_turned, 1)
                nc.scalar.activation(a_wf[:, :, :], acc[:, 1, 0:64].rearrange("p (t c) -> p t c", t=TB)[:, :, 0:24],
                                     ACT.Copy).then_inc(wf_copied, 1)
                act.dma_start(a_ki[HEAD_DIM:2 * HEAD_DIM, :], a_ki[0:HEAD_DIM, :]).then_inc(ki_doubled, 16)

            part(1, as_pair(a_qi[:, 0:4, :]), mid=copy_small)
            split_hi(n + 6)
            act.wait_ge(lf_in, 1)
            link(nc.scalar.activation(a_lf[:, 1], a_lf[:, 1], ACT.Exp))
            nc.scalar.activation(a_lf[:, 1], a_lf[:, 1], ACT.Ln, bias=1.0).then_inc(lf_ln, 1)
            part(2, as_pair(a_qi[:, 4:8, :]), mid=lambda: (relu_dots(0), relu_dots(1)))
            split_hi(n + 8)
            relu_dots(2)
            part(3, as_pair(a_q[:, 0]), HEAD_DIM ** -0.5, mid=lambda: (relu_dots(3), relu_dots(4)))
            split_hi(n + 10)
            relu_dots(5)
            part(4, as_pair(a_k[:, 0]), mid=copy_sums)
            split_hi(n + 12)
            part(5, as_pair(a_q[:, 1]), HEAD_DIM ** -0.5)
            split_hi(n + 14)
            part(6, as_pair(a_k[:, 1]))
            split_hi(n + 16)
            softmax_exp(0, 0)
            part(7, a_v[:, 1], mid=lambda: softmax_exp(0, 1))
            split_hi(n + 18)
            softmax_exp(0, 2)
            part(8, as_pair(a_q[:, 0]), HEAD_DIM ** -0.5)
            split_hi(n + 20)
            pt_copy(0, (0, 2))
            part(9, as_pair(a_k[:, 0]), mid=lambda: pt_copy(0, (4, 6)))
            split_hi(n + 22)
            out_hi(0)
            part(10, a_v[:, 2], mid=lambda: softmax_exp(1, 0))
            split_hi(n + 24)
            softmax_exp(1, 1)
            softmax_exp(1, 2)
            split_hi(n + 25)
            gate(0)
            split_hi(n + 26)
            split_hi(n + 27)
            pt_copy(1, (0, 2))
            gate(1)
            split_hi(n + 28)
            pt_copy(1, (4, 6))
            split_hi(n + 29)
            out_hi(1)
            gate(2)
            split_hi(n + 30)
            stick_ln(0)
            for j in range(31, 34):
                split_hi(n + j)
            gate(5)
            split_hi(n + 34)
            stick_exp(0)
            stick_ln(1)
            split_hi(n + 35)
            gate(6)
            split_hi(n + 36)
            split_hi(n + 37)
            stick_exp(1)
            gate(7)
            split_hi(n + 38)
            split_hi(n + 39)
            out_hi(2)
            split_hi(n + 40)
            split_hi(n + 41)
            turn_hi("mrg", x_hi, range(2), swap=2)
            split_hi(n + 42)
            turn_hi("mrg", x_hi, range(2, 4), swap=2)
            split_hi(N_SEC_OUT + 3)
            layer_norm(7, N_FF2)

            j0 = 4 * FFN_STEPS

            def relu_up(n, up, i=0):
                act.wait_ge(weights_used, i * 12 + n + 2)
                nc.scalar.activation(as_pair(hid[:, :, :]), up, ACT.Relu).then_inc(silu_done, 1)

            def hidden2_hi(slot, src):
                nc.scalar.activation(hid_hi[:, 4 * slot:4 * slot + 4, :].rearrange("p (a b) t -> p a (b t)", a=2), src,
                                     ACT.Copy).then_inc(hid_hi_done, 1)

            def ff2_step(s, i=0):
                n = N_FF2 + 4 * s
                if s > 1:
                    split_hi(n, 4 * i)
                split_hi(n + 1, 4 * i)
                act.wait_ge(hid_ready, i * 3 + j0 + s)
                relu_up(n - 2, pairs[0], i)
                split_hi(n + 2, 4 * i)
                act.wait_ge(hid_done, i * 3 + j0 + s + 1)
                hidden2_hi(s % 3, as_pair(hid[:, :, :]))
                split_hi(n + 3, 4 * i)

            split_hi(N_FF2 + 3)
            relu_up(N_FF2, pairs[1])
            split_hi(N_FF2 + 4)
            act.wait_ge(hid_turned, 5)
            hidden2_hi(0, acc[:, 0:2, :])
            ff2_step(1)
            with act.Fori(0, 2) as i:
                for s in range(2, 5):
                    ff2_step(s, i)
            layer_norm(8, N_TILES)

        @block.vector
        def _(dve):
            step = [0]

            def mark(ins):
                step[0] += 1
                ins.then_inc(dve_step, 1)
                return step[0]

            def link(ins):
                dve.wait_ge(dve_step, mark(ins))

            def split_lo(n, i=0):
                if n >= N_TILES:
                    return
                s = slot_of(n)
                dve.wait_ge(hi_split, i * RING + (n + 1))
                nc.vector.tensor_tensor(w_lo[:, s, :], raw[:, s, :], w_hi[:, s, :].bitcast(F32),
                                        ALU.subtract).then_inc(lo_split, 1)

            def turn_lo(what, hi, lo, banks, swap=0):
                for b in banks:
                    dve.wait_ge(turned_hi, turns[what] + b + 1)
                    pair = lambda t: t[:, 2 * b:2 * b + 2, :].rearrange("p c t -> p (c t)")
                    nc.vector.tensor_tensor(pair(lo), work[:, (b + swap) % 4, :], pair(hi).bitcast(F32),
                                            ALU.subtract).then_inc(operand_ready, 1)

            def rows_lo(what, tb, banks):
                for b in range(2):
                    dve.wait_ge(turned_hi, turns[what] + 2 * tb + b + 1)
                    part = lambda t: t[:, 4 * b:4 * b + 4, tb * P:(tb + 1) * P]
                    nc.vector.tensor_tensor(part(x_lo), banks[:, b, :].rearrange("p (c t) -> p c t", c=4),
                                            part(x_hi).bitcast(F32), ALU.subtract).then_inc(operand_ready, 1)

            def layer_norm(ln, end, scale):
                dve.wait_ge(rows_loaded, 32 * ln)
                for tb in range(TB):
                    dve.wait_ge(resid_ready, 2 * (ln - 1) + tb + 1)
                    for b in range(2):
                        cols = slice(b * NCOL, (b + 1) * NCOL)
                        if (tb, b) == (1, 1):
                            dve.wait_ge(weights_used, end)
                        else:
                            dve.wait_ge(acc_ready, 3 * (ln - 1) + 2 * tb + b + 1)
                        evacuated = nc.vector.scalar_tensor_tensor(
                            out=xn[:, tb, cols], in0=acc[:, 2 * tb + b, :], scalar=scale, in1=resid[:, tb, cols],
                            op0=ALU.mult, op1=ALU.add, accum_out=row_sum[:, 2 * tb + b:2 * tb + b + 1])
                    link(evacuated)
                    sums = [row_sum[:, 2 * tb + b:2 * tb + b + 1] for b in range(2)]
                    nc.vector.tensor_scalar(scaled_mean[:, tb:tb + 1], sums[0], sums[1], -D ** -1.5,
                                            ALU.add, ALU.mult).then_inc(mean_ready, 1)
                    link(nc.vector.tensor_scalar(minus_mean[:, tb:tb + 1], sums[0], sums[1], -1.0 / D, ALU.add, ALU.mult))
                    if ln < 8 and tb == 1:
                        s = slot_of(end + 1)
                        dve.wait_ge(hi_split, end + 2)
                        dve.wait_ge(piece_split, ln)
                        nc.vector.tensor_tensor(w_lo[:, s, POOL_COLS:], raw[:, s, POOL_COLS:], w_hi[:, s, POOL_COLS:].bitcast(F32),
                                                ALU.subtract).then_inc(lo_split, 1)
                    halves = [slice(b * NCOL, (b + 1) * NCOL) for b in range(2)]

                    def centre(cols):
                        link(nc.vector.scalar_tensor_tensor(
                            out=resid[:, tb, cols], in0=xn[:, tb, cols], scalar=minus_mean[:, tb:tb + 1],
                            in1=ln_rows[:, 0, cols], op0=ALU.add, op1=ALU.mult))

                    apart = ln < 8 and tb == 1
                    centre(halves[0] if apart else slice(0, D))
                    count[0] += 1
                    dve.wait_ge(rstd_ready, count[0])
                    for b in range(2):
                        if apart and b == 1:
                            centre(halves[1])
                        nc.vector.scalar_tensor_tensor(
                            out=xn[:, tb, halves[b]], in0=resid[:, tb, halves[b]], scalar=ln_rstd[:, tb:tb + 1],
                            in1=ln_rows[:, 1, halves[b]], op0=ALU.mult, op1=ALU.add).then_inc(xn_ready, 1)
                    if ln < 8:
                        if tb == 0 and ln != 2:
                            split_lo(end)
                        rows_lo(f"ln{ln}", tb, block_acc(tb))
                        if tb == 1:
                            split_lo(end + 2)

            count = [0]

            def ffn(n0, f):
                j0 = f * FFN_STEPS

                def hidden(j, up, i=0):
                    dve.wait_ge(silu_done, i * 3 + j + 1)
                    nc.vector.tensor_tensor(hid[:, 0:2, :], silu_g[:, :, :], up, ALU.mult).then_inc(hid_done, 1)

                def hidden_lo(j, slot, src, i=0):
                    dve.wait_ge(hid_hi_done, i * 3 + j + 1)
                    nc.vector.tensor_tensor(hid_lo[:, 2 * slot:2 * slot + 2, :], src,
                                            hid_hi[:, 2 * slot:2 * slot + 2, :].bitcast(F32),
                                            ALU.subtract).then_inc(hid_ready, 1)

                split_lo(n0 + 3)
                hidden(j0, pairs[0][:, :, TOK:2 * TOK])
                split_lo(n0 + 4)
                hidden_lo(j0, 0, two(acc[:, 0, :]))

                def step(j, ahead, gate_up, i=0):
                    if j > 2:
                        split_lo(ahead - 1, 3 * i)
                    split_lo(ahead, 3 * i)
                    dve.wait_ge(hid_ready, i * 3 + j0 + j)
                    hidden(j0 + j, two(gate_up[:, 1, :]), i)
                    split_lo(ahead + 1, 3 * i)
                    hidden_lo(j0 + j, j % 3, hid[:, 0:2, :], i)

                step(1, n0 + 5, pairs[1])
                step(2, n0 + 7, pairs[0])
                for j in range(3, 5):
                    step(j, n0 + 3 * j + 1, pairs[1])
                with dve.Fori(0, 2) as i:
                    for j in range(5, 8):
                        step(j, n0 + 3 * j + 1, pairs[1], i)

            rows_lo("x", 0, block_acc(0))
            split_lo(0)
            split_lo(1)
            rows_lo("x", 1, block_acc(1))
            split_lo(2)
            ffn(N_FFN0, 0)
            layer_norm(1, N_GLA, 0.5)

            n = N_GLA

            def tail_lo(lo, whole, hi, count):
                dve.wait_ge(tail_hi_done, count)
                nc.vector.tensor_tensor(lo[:, :, :], whole[:, :, :], hi[:, :, :].bitcast(F32), ALU.subtract).then_inc(tail_ready, 1)

            dve.wait_ge(gla_loaded, 16 * 5)
            tail_lo(g_tail_lo, g_tail, g_tail_hi, 1)
            split_lo(n + 3)
            split_lo(n + 4)
            link(nc.vector.memset(g_s[:, :, :, :], 0.0))
            split_lo(n + 5)
            dve.wait_ge(z_ready, 1)
            for h in range(GLA_HEADS):
                last = nc.vector.tensor_scalar(g_z[:, h, :], acc[:, 1 + h // 2, (h % 2) * TOK:(h % 2 + 1) * TOK],
                                               g_bg[:, h:h + 1], None, ALU.add)
            link(last)
            nc.vector.scalar_tensor_tensor(out=g_t[:, :, :], in0=g_z[:, :, :], scalar=-1.0, in1=g_z[:, :, :],
                                           op0=ALU.mult, op1=ALU.min).then_inc(naz_ready, 1)
            split_lo(n + 6)
            dve.wait_ge(ln1p_ready, 1)
            link(nc.vector.scalar_tensor_tensor(out=g_z[:, :, :], in0=g_z[:, :, :], scalar=0.0, in1=g_t[:, :, :],
                                                op0=ALU.min, op1=ALU.subtract))
            for h in range(GLA_HEADS):
                last = nc.vector.tensor_tensor_scan(g_cum[:, h, :], chunk_keep, g_z[:, h, :], 0.0, ALU.mult, ALU.add)
            link(last)
            cum_c = g_cum[:, :, :].rearrange("p h (c t) -> p (h c) t", t=CHUNK)
            nc.vector.tensor_tensor(g_end[:, :, :].rearrange("p h (c t) -> p (h c) t", t=CHUNK),
                                    cum_c[:, :, CHUNK - 1:CHUNK].to_broadcast([P, 16, CHUNK]), cum_c,
                                    ALU.subtract).then_inc(cum_ready, 1)
            for j in range(7, 10):
                split_lo(n + j)
            dve.wait_ge(exp_ready, 1)
            for pair in pair_free:
                dve.wait_ge(pair, 2)
            nc.vector.tensor_tensor(g_qT[:, :, :], g_qT[:, :, :], g_up[:, :, :], ALU.mult)
            nc.vector.tensor_tensor(g_end[:, :, :], g_kT[:, :, :], g_end[:, :, :], ALU.mult)
            nc.vector.tensor_tensor(g_dn[:, :, :], g_kT[:, :, :], g_dn[:, :, :], ALU.mult).then_inc(dec_ready, 1)
            split_lo(n + 10)
            split_lo(n + 11)
            for tb in range(TB):
                dve.wait_ge(gs_ready, tb + 1)
                nc.vector.copy_predicated(g_s[:, tb].rearrange("p h i -> p (h i)"), chunk_mask.bitcast(U32),
                                          acc[:, 1 + tb, :]).then_inc(gs_masked, 1)
            split_lo(n + 12)

            def state(c):
                dve.wait_ge(upd_ready, c + 1)
                src = (block_acc(1) if c == 0 else pairs[0]).rearrange("p a (b v) -> p (a b) v", b=2)
                if c == 0:
                    nc.vector.tensor_copy(g_state[:, 0], src).then_inc(state_ready, 1)
                    return
                dve.wait_ge(state_ready, c)
                for h in range(GLA_HEADS):
                    end = c * CHUNK + CHUNK - 1
                    last = nc.vector.scalar_tensor_tensor(out=g_state[:, c, h, :], in0=g_state[:, c - 1, h, :],
                                                          scalar=g_up[:, h, end:end + 1], in1=src[:, h, :],
                                                          op0=ALU.mult, op1=ALU.add)
                last.then_inc(state_ready, 1)

            def gated_output(tb):
                count[0] += 1
                dve.wait_ge(rstd_ready, count[0])
                dve.wait_ge(gate_ready, TB + tb + 1)
                for h in range(GLA_HEADS):
                    cols = slice(h * GLA_DV, (h + 1) * GLA_DV)
                    last = nc.vector.scalar_tensor_tensor(
                        out=g_v[:, tb, cols], in0=acc[:, 2 * tb + h // 2, (h % 2) * GLA_DV:(h % 2 + 1) * GLA_DV],
                        scalar=rstd[:, 4 * tb + h:4 * tb + h + 1], in1=g_r[:, tb, cols], op0=ALU.mult, op1=ALU.mult)
                last.then_inc(mixed, 1)

            state(0)
            split_lo(n + 13)
            state(1)
            gated_output(0)
            state(2)
            rows_lo("gla", 0, pairs[1])
            split_lo(n + 14)
            gated_output(1)
            rows_lo("gla", 1, pairs[0])
            for j in range(2):
                split_lo(N_GLA_OUT + j + 3)
            layer_norm(2, N_FFN1, 1.0)
            ffn(N_FFN1, 1)
            layer_norm(3, N_FFN2, 0.5)
            ffn(N_FFN2, 2)
            layer_norm(4, N_RET, 0.5)

            n = N_RET
            split_lo(n + 3)
            split_lo(n + 4)
            dve.wait_ge(ret_loaded, 16)
            for u in range(4):
                n += 2
                split_lo(n + 3)
                dve.wait_ge(weights_used, n + 2)
                for j in range(2):
                    if u:
                        dve.wait_ge(rope_done, 2 * (u - 1) + j + 1)
                    src = pairs[(u + 1) % 2][:, j, :].rearrange("p (b t) -> p b t", b=2)
                    nc.vector.tensor_tensor(r_rot[:, j, 0], src, cos.rearrange("p (b t) -> p b t", b=1)
                                            .to_broadcast([P, 2, TOK]), ALU.mult)
                    last = nc.vector.tensor_tensor(r_rot[:, j, 1], src, sin.rearrange("p (b t) -> p b t", b=1)
                                                   .to_broadcast([P, 2, TOK]), ALU.mult)
                    last.then_inc(rot_ready, 1)
                dve.wait_ge(rot_ready, 2 * u + 2)
                dve.sem_inc(pair_free[(u + 1) % 2], 1)
                split_lo(n + 4)
            for u in range(5, 8):
                n += 2
                split_lo(n + 3)
                split_lo(n + 4)
                if u == 5:
                    for h in range(RET_HEADS):
                        dve.wait_ge(rs_ready, h + 1)
                        nc.vector.tensor_tensor(r_s[:, h, :], acc[:, h, 0:CAUSAL], decay[:, h, :],
                                                ALU.mult).then_inc(rs_decayed, 1)
            n = N_RET_OUT

            def output_moments(tb):
                dve.wait_ge(ret_o, tb + 1)
                for h in range(RET_HEADS):
                    last = nc.vector.bn_stats(stats[:, 4 * tb + h, :], acc[:, h, :])
                link(last)
                for h in range(RET_HEADS):
                    last = nc.vector.bn_aggr(mv[:, 4 * tb + h, :], stats[:, 4 * tb + h, :])
                last.then_inc(var_ready, 1)

            def normed_output(tb):
                count[0] += 1
                dve.wait_ge(rstd_ready, count[0])
                for h in range(RET_HEADS):
                    i = 4 * tb + h
                    cols = slice(h * RET_DV, (h + 1) * RET_DV)
                    last = nc.vector.tensor_scalar(r_o[:, tb, cols], acc[:, h, :], mv[:, i, 0:1], rstd[:, i:i + 1],
                                                   ALU.subtract, ALU.mult)
                link(last)
                dve.sem_inc(ret_normed, 1)

            def gated_head(h):
                dve.wait_ge(gate_ready, 2 * TB + h + 1)
                cols = slice(h * RET_DV, (h + 1) * RET_DV)
                nc.vector.tensor_tensor(r_o[:, :, cols], r_o[:, :, cols], r_g[:, :, cols], ALU.mult).then_inc(mixed, 1)

            def quarter_lo(h):
                for b in range(2):
                    c = 4 * h + 2 * b
                    dve.wait_ge(turned_hi, turns["ret"] + 2 * h + b + 1)
                    flat = lambda t: t.rearrange("p c t -> p (c t)")
                    nc.vector.tensor_tensor(flat(r_lo[:, c:c + 2, :]), quarter_pair[h][:, b, :],
                                            flat(ret_hi(c)).bitcast(F32), ALU.subtract).then_inc(operand_ready, 1)

            split_lo(n - 5)
            output_moments(0)
            split_lo(n - 4)
            normed_output(0)
            split_lo(n - 3)
            split_lo(n - 2)
            output_moments(1)
            split_lo(n - 1)
            normed_output(1)
            gated_head(0)
            split_lo(n)
            gated_head(1)
            split_lo(n + 1)
            quarter_lo(0)
            gated_head(2)
            split_lo(n + 2)
            quarter_lo(1)
            gated_head(3)
            split_lo(n + 3)
            quarter_lo(2)
            split_lo(n + 4)
            quarter_lo(3)
            for j in range(5, 8):
                split_lo(n + j)
            layer_norm(5, N_FFN3, 1.0)
            ffn(N_FFN3, 3)
            layer_norm(6, N_SEC, 0.5)

            n = N_SEC
            dve.wait_ge(att_loaded, 48)

            def index_scores(p):
                dve.wait_ge(relu_done, p + 1)
                tb, first = dot_passes[p]
                width = TOK if tb else P
                per = NCOL // width
                score = a_sc[:, 0, block_cols(tb)]
                for b in range(2):
                    for i in range(per):
                        h = first + 2 * i + b
                        src = relu[:, p % 2, b * NCOL + i * width:b * NCOL + (i + 1) * width]
                        if h == 0:
                            link(nc.vector.tensor_scalar(score, src, a_wf[:, tb, h:h + 1], None, ALU.mult))
                        else:
                            link(nc.vector.scalar_tensor_tensor(out=score, in0=src, scalar=a_wf[:, tb, h:h + 1],
                                                                in1=score, op0=ALU.mult, op1=ALU.add))
                dve.sem_inc(dots_used, 1)

            def pick_largest(tb, rounds):
                score = a_sc[:, 0, block_cols(tb)]
                for _ in range(rounds):
                    link(nc.vector.max(out=a_top[:, :], in_=score))
                    link(nc.vector.match_replace(out=score, in_to_replace=a_top[:, :], in_values=score, imm_value=TAKEN))

            def logits(br, g):
                tb, heads = groups[g]
                cols, width = block_cols(tb), TOK if tb else P
                if br == 0:
                    for h in heads:
                        last = nc.vector.scalar_tensor_tensor(
                            out=a_p[:, h, cols], in0=negdist[:, cols], scalar=2.0 ** -(h + 1), in1=a_sc[:, 0, cols],
                            op0=ALU.mult, op1=ALU.add)
                    link(last)
                dve.wait_ge(logits_ready, 3 * br + g + 1)
                for h in heads:
                    b, i = h % 2, (h - heads[0]) // 2
                    src = acc[:, 2 * ((g + br) % 2) + b, i * width:(i + 1) * width]
                    last = nc.vector.tensor_tensor_reduce(
                        out=a_p[:, h, cols], in0=src, in1=a_p[:, h, cols] if br == 0 else causal[:, cols],
                        scale=1.0, scalar=-3.4e38, op0=ALU.add, op1=ALU.max, accum_out=a_max[:, 0, tb, h:h + 1])
                link(last)
                hs = slice(heads[0], heads[-1] + 1)
                if br == 0:
                    nc.vector.tensor_scalar(a_max[:, 1, tb, hs], a_max[:, 0, tb, hs], -1.0, None, ALU.mult).then_inc(max_ready, 1)
                    return
                dve.wait_ge(cT_copied, 1)
                link(nc.vector.tensor_tensor(a_max[:, 0, tb, hs], a_max[:, 0, tb, hs], a_c[:, tb, hs], ALU.add))
                nc.vector.tensor_tensor(a_max[:, 1, tb, hs], a_c[:, tb, hs], a_max[:, 0, tb, hs], ALU.subtract).then_inc(max_ready, 1)

            def inverse_sums(br, g):
                tb, heads = groups[g]
                dve.wait_ge(exp_done, 3 * br + g + 1)
                hs = slice(heads[0], heads[-1] + 1)
                nc.vector.reciprocal(a_sum[:, tb, hs], a_sum[:, tb, hs]).then_inc(weight_ready, 1)

            def pt_copy(br, heads):
                for h in heads:
                    dve.wait_ge(p_turned, 8 * br + h + 1)
                    nc.vector.tensor_copy(a_pt[:, h, :], acc[:, h % 4, 0:CAUSAL]).then_inc(pt_dve, 1)

            def out_lo(br):
                dve.wait_ge(o_hi_done, br + 1)
                part = lambda t: as_pair(t[:, 4 * br:4 * br + 4, :])
                nc.vector.tensor_tensor(part(a_ol), acc[:, 0:2, :], part(a_oh).bitcast(F32), ALU.subtract).then_inc(o_done, 1)

            strict4 = strict.rearrange("p (h c) -> p h c", h=1).to_broadcast([P, 4, CAUSAL])
            z = acc[:, 0:4, 0:CAUSAL]

            def stick_logs(r):
                rows = slice(4 * r, 4 * r + 4)
                dve.wait_ge(sb_ln, r + 1)
                link(nc.vector.scalar_tensor_tensor(out=a_p[:, rows, :], in0=z, scalar=0.0, in1=a_pt[:, rows, :],
                                                    op0=ALU.min, op1=ALU.subtract))
                link(nc.vector.tensor_tensor(a_pt[:, rows, :], a_p[:, rows, :], z, ALU.subtract))
                nc.vector.tensor_tensor(a_pt[:, rows, :], a_pt[:, rows, :], strict4, ALU.mult).then_inc(sb_l, 1)

            def stick_sum(r):
                dve.wait_ge(sb_later, r + 1)
                rows = slice(4 * r, 4 * r + 4)
                nc.vector.tensor_tensor(a_p[:, rows, :], a_p[:, rows, :], z, ALU.add).then_inc(sb_t, 1)

            def stick_mask(r):
                dve.wait_ge(sb_exp, r + 1)
                rows = slice(4 * r, 4 * r + 4)
                nc.vector.tensor_tensor(a_p[:, rows, :], a_p[:, rows, :], strict4, ALU.mult).then_inc(sb_a, 1)

            def gate_product(j):
                kind, half, b = merge[j]
                u = SEC_UNITS + j
                dve.wait_ge(weights_used, merge_tile[j] + 1)
                dve.wait_ge(sig_done, 1 + [m for m in merge if m[0] == "gate"].index(("gate", half, b)))
                dst = merged[:, :, half * NCOL:(half + 1) * NCOL]
                link(nc.vector.tensor_tensor(gated if b else dst, sig_of(half, b), pairs[u % 2], ALU.mult))
                dve.sem_inc(up_used, 1)
                dve.sem_inc(pair_free[u % 2], 1)
                if b:
                    link(nc.vector.tensor_tensor(dst, dst, gated, ALU.add))
                if b == 2:
                    dve.sem_inc(merged_ready, 1)

            tail_lo(a_tail_lo, a_tail, a_tail_hi, 2)
            for j in range(3, 6):
                split_lo(n + j)
            dve.wait_ge(wf_copied, 1)
            link(nc.vector.tensor_tensor(a_lf[:, 0], a_wf[:, :, IDX_HEADS:],
                                         a_bf[:, :].rearrange("p (t h) -> p t h", t=1).to_broadcast([P, TB, HEADS]), ALU.add))
            nc.vector.scalar_tensor_tensor(out=a_lf[:, 1], in0=a_lf[:, 0], scalar=-1.0, in1=a_lf[:, 0],
                                           op0=ALU.mult, op1=ALU.min).then_inc(lf_in, 1)
            split_lo(n + 6)
            dve.wait_ge(lf_ln, 1)
            nc.vector.scalar_tensor_tensor(out=a_lf[:, 2], in0=a_lf[:, 0], scalar=0.0, in1=a_lf[:, 1],
                                           op0=ALU.min, op1=ALU.subtract).then_inc(lf_ready, 1)
            split_lo(n + 7)
            index_scores(0)
            index_scores(1)
            split_lo(n + 8)
            index_scores(2)
            split_lo(n + 9)
            index_scores(3)
            index_scores(4)
            split_lo(n + 10)
            index_scores(5)
            link(nc.vector.tensor_tensor(a_sc[:, 0, :], a_sc[:, 0, :], causal, ALU.add))
            split_lo(n + 11)
            pick_largest(1, 4)
            split_lo(n + 12)
            pick_largest(1, 4)
            split_lo(n + 13)
            pick_largest(0, 4)
            split_lo(n + 14)
            pick_largest(0, 4)
            link(nc.vector.tensor_scalar(a_sc[:, 0, :], a_sc[:, 0, :], TAKEN, NEG, ALU.not_equal, ALU.mult))
            link(nc.vector.tensor_tensor(a_sc[:, 0, :], a_sc[:, 0, :], causal, ALU.min))
            split_lo(n + 15)
            logits(0, 0)
            split_lo(n + 16)
            logits(0, 1)
            inverse_sums(0, 0)
            split_lo(n + 17)
            logits(0, 2)
            inverse_sums(0, 1)
            split_lo(n + 18)
            inverse_sums(0, 2)
            split_lo(n + 19)
            split_lo(n + 20)
            pt_copy(0, (1, 3))
            split_lo(n + 21)
            pt_copy(0, (5, 7))
            split_lo(n + 22)
            out_lo(0)
            logits(1, 0)
            split_lo(n + 23)
            logits(1, 1)
            inverse_sums(1, 0)
            split_lo(n + 24)
            logits(1, 2)
            inverse_sums(1, 1)
            inverse_sums(1, 2)
            split_lo(n + 25)
            split_lo(n + 26)
            split_lo(n + 27)
            pt_copy(1, (1, 3))
            split_lo(n + 28)
            pt_copy(1, (5, 7))
            split_lo(n + 29)
            out_lo(1)
            split_lo(n + 30)
            dve.wait_ge(resid_ready, 14)
            gate_product(3)
            stick_logs(0)
            split_lo(n + 31)
            gate_product(4)
            for j in range(32, 34):
                split_lo(n + j)
            stick_sum(0)
            split_lo(n + 34)
            stick_mask(0)
            stick_logs(1)
            split_lo(n + 35)
            split_lo(n + 36)
            split_lo(n + 37)
            stick_sum(1)
            stick_mask(1)
            split_lo(n + 38)
            gate_product(8)
            split_lo(n + 39)
            out_lo(2)
            gate_product(9)
            split_lo(n + 40)
            gate_product(10)
            split_lo(n + 41)
            turn_lo("mrg", x_hi, x_lo, range(2), swap=2)
            gate_product(11)
            split_lo(n + 42)
            turn_lo("mrg", x_hi, x_lo, range(2, 4), swap=2)
            split_lo(N_SEC_OUT + 3)
            layer_norm(7, N_FF2, 1.0)

            j0 = 4 * FFN_STEPS

            def square(j, up, i=0):
                dve.wait_ge(silu_done, i * 3 + j + 1)
                nc.vector.tensor_tensor(as_pair(hid[:, :, :]), as_pair(hid[:, :, :]), up, ALU.mult).then_inc(hid_done, 1)

            def hidden2_lo(j, slot, src, i=0):
                dve.wait_ge(hid_hi_done, i * 3 + j + 1)
                part = lambda t: as_pair(t[:, 4 * slot:4 * slot + 4, :])
                nc.vector.tensor_tensor(part(hid_lo), src, part(hid_hi).bitcast(F32), ALU.subtract).then_inc(hid_ready, 1)

            def ff2_step(s, i=0):
                n = N_FF2 + 4 * s
                if s > 1:
                    split_lo(n, 4 * i)
                split_lo(n + 1, 4 * i)
                square(j0 + s, pairs[0], i)
                split_lo(n + 2, 4 * i)
                hidden2_lo(j0 + s, s % 3, as_pair(hid[:, :, :]), i)
                split_lo(n + 3, 4 * i)

            split_lo(N_FF2 + 3)
            square(j0, pairs[1])
            split_lo(N_FF2 + 4)
            hidden2_lo(j0, 0, acc[:, 0:2, :])
            ff2_step(1)
            with dve.Fori(0, 2) as i:
                for s in range(2, 5):
                    ff2_step(s, i)
            layer_norm(8, N_TILES, 1.0)

        @block.tensor
        def _(pe):
            mm = nc.tensor.matmul

            def three(out, a_hi, a_lo, b_hi, b_lo, start, stop, between=(None, None)):
                if between[0]:
                    between[0]()
                mm(out, a_hi, b_hi, start=start, stop=False, skip_group_check=True)
                if between[1]:
                    between[1]()
                mm(out, a_hi, b_lo, start=False, stop=False, skip_group_check=True)
                return mm(out, a_lo, b_hi, start=False, stop=stop, skip_group_check=True)

            def turn_rows(what, src, tb, banks, ready, value):
                def turn_bank(b):
                    pe.wait_ge(ready, value(b))
                    for j in range(4):
                        c = 4 * b + j
                        ins = nc.tensor.transpose(banks[:, b, j * P:(j + 1) * P], src[:, tb, c * P:(c + 1) * P], ident)
                    ins.then_inc(turned, 1)

                return (lambda: turn_bank(0)), (lambda: turn_bank(1))

            def turn_normed(ln, tb):
                return turn_rows(f"ln{ln}", xn, tb, block_acc(tb), xn_ready, lambda b: 4 * (ln - 1) + 2 * tb + b + 1)

            def first_unit(n, out, what, turn_second):
                inner = {(0, KC - 2): (turn_second[0], None), (0, KC - 1): (None, turn_second[1])}
                for tb in range(TB):
                    t = slice(tb * P, (tb + 1) * P)
                    for s in range(2):
                        slot = slot_of(n + s)
                        pe.wait_ge(lo_split, n + s + 1)
                        pe.wait_ge(operand_ready, turns[what] + 2 * tb + s + 1)
                        for k in range(4):
                            c = 4 * s + k
                            cols = slice(k * NCOL, (k + 1) * NCOL)
                            last = three(out[:, tb, :], x_hi[:, c, t], x_lo[:, c, t], w_hi[:, slot, cols], w_lo[:, slot, cols],
                                         c == 0, c == KC - 1, inner.get((tb, c), (None, None)))
                        if tb == TB - 1:
                            last.then_inc(weights_used, 1)

            def normed_unit(n, out, ln):
                first_unit(n, out, f"ln{ln}", turn_normed(ln, 1))

            def tokens_unit(n, out, i=0, between={}):
                for s in range(2):
                    slot = slot_of(n + s)
                    pe.wait_ge(lo_split, i + (n + s + 1))
                    for k in range(4):
                        c = 4 * s + k
                        if c in between:
                            between[c]()
                        cols = slice(k * NCOL, (k + 1) * NCOL)
                        for tb in range(TB):
                            t = slice(tb * P, (tb + 1) * P)
                            last = three(out[:, tb, :], x_hi[:, c, t], x_lo[:, c, t], w_hi[:, slot, cols], w_lo[:, slot, cols],
                                         c == 0, c == KC - 1)
                    last.then_inc(weights_used, 1)

            def features_unit(n, out, i=0, between={}):
                for s in range(2):
                    slot = slot_of(n + s)
                    pe.wait_ge(lo_split, i + (n + s + 1))
                    for k in range(4):
                        c = 4 * s + k
                        if c in between:
                            between[c]()
                        for b in range(4):
                            cols = slice(k * NCOL + b * P, k * NCOL + (b + 1) * P)
                            last = three(out[:, b // 2, (b % 2) * TOK:(b % 2 + 1) * TOK], w_hi[:, slot, cols], w_lo[:, slot, cols],
                                         x_hi[:, c, :], x_lo[:, c, :], c == 0 and b % 2 == 0, c == KC - 1)
                    last.then_inc(weights_used, 1)

            def down(n, h_hi, h_lo, chunks, first, final, i=0, ready=None):
                slot = slot_of(n)
                pe.wait_ge(lo_split, i + (n + 1))
                for k, c in enumerate(chunks):
                    if ready is not None:
                        pe.wait_ge(operand_ready, ready + c // 2 + 1)
                    for tb in range(TB):
                        t = slice(tb * P, (tb + 1) * P)
                        for half in range(2):
                            cols = slice(k * D + half * NCOL, k * D + (half + 1) * NCOL)
                            last = three(acc[:, 2 * tb + half, :], h_hi[:, c, t], h_lo[:, c, t], w_hi[:, slot, cols],
                                         w_lo[:, slot, cols], first and k == 0, final and k == len(chunks) - 1)
                last.then_inc(weights_used, 1)

            def block_product(n, ready, value, chunks, first=False, final=None, between=None):
                tiles = len(chunks) // 2
                for tb in range(TB):
                    t = slice(tb * P, (tb + 1) * P)
                    for s in range(tiles):
                        slot = slot_of(n + s)
                        pe.wait_ge(lo_split, n + s + 1)
                        pe.wait_ge(ready, value(tb, s))
                        order = [(k, half) for k in range(2) for half in range(2)]
                        if final is not None and s == tiles - 1:
                            order.sort(key=lambda at: at[1])
                        for k, half in order:
                            h_hi, h_lo, c = chunks[2 * s + k]
                            inner = (None, None)
                            if between and (tb, s, k, half) == (0, 1, 1, 0):
                                inner = between
                            if final is not None and final < 8 and (tb, s, k, half) == ((1, 1, 1, 1) if tiles == 2 else (1, 2, 0, 0)):
                                inner = turn_normed(final, 0)
                            cols = slice(k * D + half * NCOL, k * D + (half + 1) * NCOL)
                            last = three(acc[:, 2 * tb + half, :], h_hi[:, c, t], h_lo[:, c, t], w_hi[:, slot, cols],
                                         w_lo[:, slot, cols], first and s == 0 and k == 0,
                                         final is not None and s == tiles - 1 and k == 1, inner)
                            if final is not None and s == tiles - 1 and k == 1 and (tb, half) != (1, 1):
                                last.then_inc(acc_ready, 1)
                        if tb == TB - 1:
                            last.then_inc(weights_used, 1)

            def turn_hidden(j, cols):
                pe.wait_ge(hid_done, j + 1)
                src = hid[:, :, :].rearrange("p c t -> p (c t)")
                for c in range(cols // P):
                    for tb in range(TB):
                        at = (c % 2) * TOK + tb * P
                        ins = nc.tensor.transpose(acc[:, c // 2, at:at + P], src[:, tb * cols + c * P:tb * cols + (c + 1) * P], ident)
                ins.then_inc(hid_turned, 1)

            def hidden_chunks(slots, each):
                return [(hid_hi, hid_lo, each * s + k) for s in slots for k in range(each)]

            def ffn(n0, f):
                j0 = f * FFN_STEPS
                features_unit(n0 + 2, pairs[1], between={4: lambda: turn_hidden(j0, 2 * P)})
                features_unit(n0 + 4, pairs[0])

                def step(j, i=0):
                    pe.wait_ge(hid_ready, i * 3 + j0 + j + 1)
                    at = 2 * (j % 3)
                    down(n0 + 3 * j + 6, hid_hi, hid_lo, range(at, at + 2), j == 0, False, 9 * i)
                    pe.wait_ge(hid_done, i * 3 + j0 + j + 3)
                    features_unit(n0 + 3 * j + 7, pairs[1], i=9 * i)

                step(0)
                step(1)
                with pe.Fori(0, 2) as i:
                    for j in range(2, 5):
                        step(j, i)
                block_product(n0 + FFN_TILES - 3, hid_ready, lambda tb, s: j0 + FFN_STEPS - 2 + s, hidden_chunks((2, 0, 1), 2),
                              final=(1, 3, 4, 6)[f])

            pe.wait_ge(ident_loaded, 16)
            for turn_bank in turn_rows("x", xn, 0, block_acc(0), x_loaded[0], lambda b: 16):
                turn_bank()
            for _ in range(3):
                mm(work[:, 3, :], ident, xn[:, 0, 0:NCOL], start=True, stop=True)
            first_unit(N_FFN0, pairs[0], "x", turn_rows("x", xn, 1, block_acc(1), x_loaded[1], lambda b: 16))
            ffn(N_FFN0, 0)

            n = N_GLA
            normed_unit(n, pairs[0], 1)
            pe.wait_ge(tail_ready, 1)
            for c in range(KC):
                last = three(acc[:, 0, 0:TOK], g_tail_hi[:, c, :], g_tail_lo[:, c, :], x_hi[:, c, :], x_lo[:, c, :],
                             c == 0, c == KC - 1)
            last.then_inc(low_ready, 1)

            def gate_logits():
                pe.wait_ge(low_copied, 1)
                for h in range(GLA_HEADS):
                    last = mm(acc[:, 1 + h // 2, (h % 2) * TOK:(h % 2 + 1) * TOK], g_wg[:, h * GLA_DK:(h + 1) * GLA_DK],
                              g_low[:, :], start=(h % 2 == 0), stop=True, skip_group_check=True)
                last.then_inc(z_ready, 1)

            def chunk_scores():
                pe.wait_ge(dec_ready, 1)
                for tb in range(TB):
                    for h in range(GLA_HEADS):
                        last = nc.tensor.transpose(acc[:, 3 * tb, h * P:(h + 1) * P], g_end[:, h, tb * P:(tb + 1) * P], ident)
                    last.then_inc(kend_turned, 1)
                for tb in range(TB):
                    t = slice(tb * P, (tb + 1) * P)
                    for h in range(GLA_HEADS):
                        last = mm(acc[:, 1 + tb, h * P:(h + 1) * P], g_dn[:, h, t], g_qT[:, h, t],
                                  start=(h == 0), stop=True, skip_group_check=True)
                    last.then_inc(gs_ready, 1)

            def update(c, out):
                rows, tb = slice((c % 2) * CHUNK, (c % 2 + 1) * CHUNK), c // 2
                for h in range(GLA_HEADS):
                    last = mm(out[:, h // 2, (h % 2) * GLA_DV:(h % 2 + 1) * GLA_DV],
                              g_kend[rows, tb, h * GLA_DK:(h + 1) * GLA_DK], g_v[rows, tb, h * GLA_DV:(h + 1) * GLA_DV],
                              start=(h % 2 == 0), stop=True, skip_group_check=True)
                last.then_inc(upd_ready, 1)

            def gla_out(tb, h):
                return acc[:, 2 * tb + h // 2, (h % 2) * GLA_DV:(h % 2 + 1) * GLA_DV]

            def within_chunks(tb):
                for h in range(GLA_HEADS):
                    mm(gla_out(tb, h), g_s[:, tb, h, :], g_v[:, tb, h * GLA_DV:(h + 1) * GLA_DV],
                       start=(h % 2 == 0), stop=False, skip_group_check=True)

            def from_state(c):
                rows, tb = slice((c % 2) * CHUNK, (c % 2 + 1) * CHUNK), c // 2
                pe.wait_ge(state_ready, c)
                for h in range(GLA_HEADS):
                    last = mm(gla_out(tb, h)[rows], g_qT[:, h, c * CHUNK:(c + 1) * CHUNK], g_state[:, c - 1, h, :],
                              start=False, stop=True, skip_group_check=True)
                return last

            def second_chunk():
                pe.wait_ge(state_ready, 1)
                pe.wait_ge(pair_free[0], 3)
                update(1, pairs[0])
                from_state(1).then_inc(gla_o, 1)
                within_chunks(1)

            tokens_unit(n + 2, pairs[1], between={4: gate_logits})
            for u, between in ((2, {}), (3, {}), (4, {4: chunk_scores})):
                pe.wait_ge(pair_free[u % 2], u // 2)
                (features_unit if u < 4 else tokens_unit)(n + 2 * u, pairs[u % 2], between=between)
            pe.wait_ge(kend_copied, TB)
            pe.wait_ge(gs_masked, TB)
            update(0, block_acc(1))
            within_chunks(0)
            pe.wait_ge(pair_free[1], 2)
            tokens_unit(n + 10, pairs[1], between={4: second_chunk})
            from_state(2)
            update(2, pairs[0])
            for turn_bank in turn_rows("gla", g_v, 0, pairs[1], mixed, lambda b: 1):
                turn_bank()
            from_state(3).then_inc(gla_o, 1)
            block_product(N_GLA_OUT, operand_ready, lambda tb, s: turns["gla"] + 2 * tb + 1, [(x_hi, x_lo, c) for c in range(4)],
                         first=True, between=turn_rows("gla", g_v, 1, pairs[0], mixed, lambda b: 2))
            block_product(N_GLA_OUT + 2, operand_ready, lambda tb, s: turns["gla"] + 2 * tb + 2,
                         [(x_hi, x_lo, c) for c in range(4, 8)], final=2)
            normed_unit(N_FFN1, pairs[0], 2)
            ffn(N_FFN1, 1)
            normed_unit(N_FFN2, pairs[0], 3)
            ffn(N_FFN2, 2)

            n = N_RET
            normed_unit(n, pairs[0], 4)

            def head_scores():
                pe.wait_ge(rope_done, 8)
                for h in range(RET_HEADS):
                    for kb, cols in ((0, slice(0, TOK)), (1, slice(TOK, CAUSAL))):
                        for c in range(2):
                            last = mm(acc[:, h, cols], r_qk[:, 1, 2 * h + c, kb * P:(kb + 1) * P],
                                      r_qk[:, 0, 2 * h + c, kb * P:TOK], start=(c == 0), stop=(c == 1))
                    last.then_inc(rs_ready, 1)

            def head_outputs(tb):
                if tb == 0:
                    pe.wait_ge(rs_decayed, RET_HEADS)
                    pe.wait_ge(pair_free[1], 3 + 4)
                else:
                    pe.wait_ge(ret_normed, 1)
                for h in range(RET_HEADS):
                    for kb in range(tb + 1):
                        cols = slice(tb * P, (tb + 1) * P) if kb == 0 else slice(TOK, CAUSAL)
                        last = mm(acc[:, h, :], r_s[:, h, cols], r_v[:, kb, h * RET_DV:(h + 1) * RET_DV],
                                  start=(kb == 0), stop=(kb == tb))
                last.then_inc(ret_o, 1)

            def turn_quarter(h):
                pe.wait_ge(mixed, TB + h + 1)
                for c in range(4):
                    for tb in range(TB):
                        at = (c % 2) * TOK + tb * P
                        ins = nc.tensor.transpose(quarter_pair[h][:, c // 2, at:at + P],
                                                  r_o[:, tb, (4 * h + c) * P:(4 * h + c + 1) * P], ident)
                    if c % 2:
                        ins.then_inc(turned, 1)

            def first_quarter():
                pe.wait_ge(pair_free[0], 9)
                turn_quarter(0)

            between = {8: {4: lambda: head_outputs(0)}, 11: {4: first_quarter}}
            for u in range(1, RET_UNITS):
                if u >= 2:
                    pe.wait_ge(pair_free[u % 2], 3 + u // 2)
                if u == 10:
                    head_outputs(1)
                (features_unit if u < 5 else tokens_unit)(n + 2 * u, pairs[u % 2], between=between.get(u, {}))
                if u == 5:
                    head_scores()

            def ret_product(j):
                c = 2 * j
                at = c % KC
                down(N_RET_OUT + j, r_hi2 if c < KC else x_hi, r_lo[:, c - at:c - at + KC, :], range(at, at + 2), j == 0, False,
                     ready=turns["ret"] + (c - at) // 2)

            pe.wait_ge(operand_ready, turns["ret"] + 2)
            pe.wait_ge(ret_normed, 2)
            turn_quarter(1)
            ret_product(0)
            pe.wait_ge(pair_free[1], 9)
            turn_quarter(2)
            ret_product(1)
            pe.wait_ge(operand_ready, turns["ret"] + 4)
            turn_quarter(3)
            for j in range(2, 5):
                ret_product(j)
            block_product(N_RET_OUT + 5, operand_ready, lambda tb, s: turns["ret"] + 6 + s,
                          [(x_hi, r_lo[:, KC:2 * KC, :], c) for c in range(2, 8)], final=5)
            normed_unit(N_FFN3, pairs[0], 5)
            ffn(N_FFN3, 3)

            n = N_SEC

            def await_pair(u):
                if u >= 2:
                    pe.wait_ge(pair_free[u % 2], pair_count(u - 2))

            def unit(u, kind, **between):
                await_pair(u)
                kind(n + 2 * u, pairs[u % 2], **between)

            def small():
                pe.wait_ge(tail_ready, 2)
                for c in range(KC):
                    last = three(acc[:, 0, 0:TOK], a_tail_hi[:, c, :], a_tail_lo[:, c, :], x_hi[:, c, :], x_lo[:, c, :],
                                 c == 0, c == KC - 1)
                last.then_inc(small_ready, 1)

            def turn_small():
                pe.wait_ge(small_copied, 1)
                rows = slice(HEAD_DIM, HEAD_DIM + IDX_HEADS + HEADS)
                for tb in range(TB):
                    last = nc.tensor.transpose(acc[:, 1, 32 * tb:32 * tb + 24], a_ki[rows, tb * P:(tb + 1) * P], ident[rows, rows])
                last.then_inc(small_turned, 1)

            def dots(p):
                if p >= 2:
                    pe.wait_ge(relu_done, p - 1)
                tb, first = dot_passes[p]
                pe.wait_ge(pair_free[1 if first < 8 else 0], pair_count(1 if first < 8 else 2))
                width = TOK if tb else P
                for i in range(NCOL // width):
                    for b in range(2):
                        h = first + 2 * i + b
                        rows = slice(HEAD_DIM * b, HEAD_DIM * (b + 1))
                        last = mm(acc[:, 2 * (p % 2) + b, i * width:(i + 1) * width], a_qi[rows, h // 2, tb * P:(tb + 1) * P],
                                  a_ki[rows, 0:width], start=(i == 0), stop=True, skip_group_check=True)
                last.then_inc(dots_ready, 1)

            def forget_sums():
                pe.wait_ge(lf_ready, 1)
                pe.wait_ge(consts_loaded, 16)
                pe.wait_ge(relu_done, 5)
                mm(acc[:, 1, 0:HEADS], tri, a_lf[:, 2, 0, :], start=True, stop=True, skip_group_check=True)
                mm(acc[:, 1, HEADS:2 * HEADS], ones, a_lf[:, 2, 0, :], start=False, stop=False, skip_group_check=True)
                mm(acc[:, 1, HEADS:2 * HEADS], tri, a_lf[:, 2, 1, :], start=False, stop=True, skip_group_check=True)
                mm(acc[0:HEADS, 0, 0:P], a_lf[:, 2, 0, :], tri, start=True, stop=True, skip_group_check=True)
                mm(acc[0:HEADS, 0, P:TOK], a_lf[:, 2, 0, :], ones, start=False, stop=False, skip_group_check=True)
                mm(acc[0:HEADS, 0, P:TOK], a_lf[:, 2, 1, :], tri, start=False, stop=True, skip_group_check=True).then_inc(cum_f, 1)

            def key_sums(g):
                tb, heads = groups[g]
                width = TOK if tb else P
                for h in heads:
                    b, i = h % 2, (h - heads[0]) // 2
                    mm(acc[:, 2 * ((g + 1) % 2) + b, i * width:(i + 1) * width],
                       ident[0:HEADS, h:h + 1].to_broadcast([HEADS, P]), a_cT[:, 0:width],
                       start=(i == 0), stop=False, skip_group_check=True)

            def logits(br, g):
                tb, heads = groups[g]
                width = TOK if tb else P
                for h in heads:
                    b, i = h % 2, (h - heads[0]) // 2
                    rows = slice(HEAD_DIM * b, HEAD_DIM * (b + 1))
                    out = acc[:, 2 * ((g + br) % 2) + b, i * width:(i + 1) * width]
                    last = mm(out, a_q[rows, br, h // 2, tb * P:(tb + 1) * P], a_k[rows, br, h // 2, 0:width],
                              start=(br == 0 and i == 0), stop=True, skip_group_check=True)
                last.then_inc(logits_ready, 1)

            def turn_p(br, heads):
                pe.wait_ge(p_ready, 3 * br + 3)
                for h in heads:
                    if h >= 4:
                        pe.wait_ge(pt_act if h % 2 == 0 else pt_dve, 4 * br + (h - 4) // 2 + 1)
                    nc.tensor.transpose(acc[:, h % 4, 0:P], a_p[:, h, 0:P], ident)
                    nc.tensor.transpose(acc[:, h % 4, P:TOK], a_p[:, h, P:TOK], ident)
                    nc.tensor.transpose(acc[:, h % 4, TOK:CAUSAL], a_p[:, h, TOK:CAUSAL], ident).then_inc(p_turned, 1)

            def values(br, pt, heads):
                for h in heads:
                    rows = slice(HEAD_DIM * (h % 2), HEAD_DIM * (h % 2 + 1))
                    c = h // 2
                    out = acc[rows, c // 2, (c % 2) * TOK:(c % 2 + 1) * TOK]
                    cols = slice(h * HEAD_DIM, (h + 1) * HEAD_DIM)
                    mm(out, a_v[:, br, 0, cols], pt[:, h, 0:TOK], start=(c % 2 == 0), stop=False, skip_group_check=True)
                    last = mm(out[:, P:TOK], a_v[:, br, 1, cols], pt[:, h, TOK:CAUSAL], start=False, stop=True,
                              skip_group_check=True)
                if heads[-1] == HEADS - 1:
                    last.then_inc(o_ready, 1)

            def softmax_values(br, half):
                for copied in (pt_act, pt_dve):
                    pe.wait_ge(copied, 4 * br + 4)
                values(br, a_pt, range(4 * half, 4 * half + 4))

            def stick_logits(r):
                for i in range(4):
                    h = 4 * r + i
                    rows = slice(HEAD_DIM * (h % 2), HEAD_DIM * (h % 2 + 1))
                    for kb, cols in ((0, slice(0, TOK)), (1, slice(TOK, CAUSAL))):
                        last = mm(acc[:, i, cols], a_k[rows, 0, h // 2, kb * P:(kb + 1) * P], a_q[rows, 0, h // 2, kb * P:TOK],
                                  start=True, stop=True, skip_group_check=True)
                last.then_inc(sb_z, 1)

            def stick_later(r, half):
                pe.wait_ge(sb_l, r + 1)
                for i in range(2 * half, 2 * half + 2):
                    h = 4 * r + i
                    mm(acc[:, i, 0:TOK], later_of, a_pt[:, h, 0:TOK], start=True, stop=False, skip_group_check=True)
                    mm(acc[:, i, P:TOK], ones, a_pt[:, h, TOK:CAUSAL], start=False, stop=False, skip_group_check=True)
                    last = mm(acc[:, i, TOK:CAUSAL], later_of, a_pt[:, h, TOK:CAUSAL], start=False, stop=True,
                              skip_group_check=True)
                if half:
                    last.then_inc(sb_later, 1)

            def merge_unit(j, between={}):
                kind, half, b = merge[j]
                await_pair(SEC_UNITS + j)
                out = pairs[(SEC_UNITS + j) % 2]
                m = merge_tile[j]
                if kind == "gate":
                    tokens_unit(m, out, between=between)
                    return
                slot = slot_of(m)
                pe.wait_ge(lo_split, m + 1)
                for k in range(4):
                    if k in between:
                        between[k]()
                    cols = slice(k * NCOL, (k + 1) * NCOL)
                    for tb in range(TB):
                        t = slice(tb * P, (tb + 1) * P)
                        last = three(out[:, tb, :], a_oh[:, 4 * b + k, t], a_ol[:, 4 * b + k, t],
                                     w_hi[:, slot, cols], w_lo[:, slot, cols], k == 0, k == 3)
                last.then_inc(weights_used, 1)

            def turn_merged(half):
                pe.wait_ge(merged_ready, half + 1)
                for c in range(4 * half, 4 * half + 4):
                    for tb in range(TB):
                        at = (c % 2) * TOK + tb * P
                        ins = nc.tensor.transpose(work[:, (c // 2 + 2) % 4, at:at + P], merged[:, tb, c * P:(c + 1) * P], ident)
                    if c % 2:
                        ins.then_inc(turned, 1)

            normed_unit(n, pairs[0], 6)
            small()
            unit(1, features_unit, between={4: turn_small})
            pe.wait_ge(wf_copied, 1)
            pe.wait_ge(ki_doubled, 16)
            unit(2, features_unit, between={4: lambda: dots(0), 6: lambda: dots(1)})
            unit(3, features_unit, between={1: lambda: dots(2), 3: lambda: dots(3), 5: lambda: dots(4)})
            unit(4, features_unit, between={1: lambda: dots(5), 4: forget_sums})
            unit(5, features_unit)

            def first_logits():
                pe.wait_ge(cT_copied, 1)
                pe.wait_ge(relu_done, 6)
                logits(0, 0)

            def third_logits():
                pe.wait_ge(max_ready, 1)
                logits(0, 2)

            def second_sums():
                pe.wait_ge(o_done, 1)
                key_sums(1)

            def third_sums():
                pe.wait_ge(max_ready, 3 + 1)
                key_sums(2)

            unit(6, features_unit, between={4: first_logits, 6: lambda: logits(0, 1)})
            unit(7, tokens_unit, between={4: third_logits})
            unit(8, features_unit)
            turn_p(0, range(0, 4))
            unit(9, features_unit, between={4: lambda: turn_p(0, range(4, 8))})
            unit(10, tokens_unit, between={0: lambda: softmax_values(0, 0), 2: lambda: softmax_values(0, 1),
                                           3: lambda: key_sums(0), 4: lambda: logits(1, 0), 5: second_sums,
                                           6: lambda: logits(1, 1)})
            merge_unit(0, between={1: third_sums, 2: lambda: logits(1, 2)})
            merge_unit(1, between={4: lambda: turn_p(1, range(0, 4))})
            turn_p(1, range(4, 8))
            merge_unit(2, between={4: lambda: softmax_values(1, 0), 6: lambda: softmax_values(1, 1)})

            def next_stick(r):
                if r:
                    pe.wait_ge(sb_t, 1)
                else:
                    pe.wait_ge(o_done, 2)
                stick_logits(r)

            merge_unit(3, between={1: lambda: next_stick(0)})
            merge_unit(4)
            merge_unit(5, between={4: lambda: stick_later(0, 0), 6: lambda: stick_later(0, 1)})
            merge_unit(6, between={0: lambda: next_stick(1)})
            merge_unit(7, between={4: lambda: stick_later(1, 0), 6: lambda: stick_later(1, 1)})
            merge_unit(8)

            def stick_values(half):
                pe.wait_ge(sb_a, 2)
                values(2, a_p, range(4 * half, 4 * half + 4))

            merge_unit(9, between={0: lambda: stick_values(0), 2: lambda: stick_values(1)})
            pe.wait_ge(o_done, 3)
            merge_unit(10)
            merge_unit(11, between={3: lambda: turn_merged(0)})
            down(N_SEC_OUT, x_hi, x_lo, range(0, 2), True, False, ready=turns["mrg"])
            turn_merged(1)
            block_product(N_SEC_OUT + 1, operand_ready, lambda tb, s: turns["mrg"] + 2 + s,
                          [(x_hi, x_lo, c) for c in range(2, 8)], final=7)
            normed_unit(N_FF2, pairs[1], 7)

            j0 = 4 * FFN_STEPS

            def ff2_step(s, first=False, i=0):
                n = N_FF2 + 4 * s - 2
                if s > 1:
                    pe.wait_ge(hid_done, i * 3 + j0 + s)
                features_unit(n, pairs[0], i=12 * i, between={4: lambda: turn_hidden(j0, 4 * P)} if s == 1 else {})
                pe.wait_ge(hid_ready, i * 3 + j0 + s)
                at = 4 * ((s - 1) % 3)
                for k in range(2):
                    down(n + 2 + k, hid_hi, hid_lo, range(at + 2 * k, at + 2 * k + 2), first and k == 0, False, 12 * i)

            ff2_step(1, first=True)
            with pe.Fori(0, 2) as i:
                for s in range(2, 5):
                    ff2_step(s, i=i)
            block_product(N_TILES - 2, hid_ready, lambda tb, s: j0 + FF2_STEPS, hidden_chunks((1,), 4), final=8)


def _column_tiles(w):
    return [w[r:r + 512].reshape(4, P, NCOL).transpose(1, 0, 2).reshape(P, TILE) for r in (0, 512)]


def _row_tiles(w):
    return [w[r:r + 256].reshape(2, P, D).transpose(1, 0, 2).reshape(P, TILE) for r in range(0, w.shape[0], 256)]


def _weight_stream(a):
    def units(w, columns):
        return [t for c in columns for t in _column_tiles(w[:, c:c + NCOL])]

    def ffn(i, j):
        w_in, down = a["ffn_w_in"][i, j], _row_tiles(a["ffn_w_out"][i, j])
        up = [_column_tiles(np.concatenate([w_in[:, 256 * s:256 * s + 256], w_in[:, D_FF + 256 * s:D_FF + 256 * s + 256]], 1))
              for s in range(FFN_STEPS)]
        tiles = up[0] + up[1]
        for s in range(2, FFN_STEPS):
            tiles += up[s] + [down[s - 2]]
        return tiles + down[-2:]

    tiles = ffn(0, 0)
    tiles += units(a["gla_w_in"][0], (D, D + NCOL, 0, NCOL, 2 * D, 2 * D + NCOL)) + _row_tiles(a["gla_w_out"][0])
    tiles += ffn(0, 1) + ffn(1, 0)
    tiles += units(a["ret_w_in"][0], [2 * D, *range(0, 2 * D, NCOL), *range(2 * D + NCOL, 6 * D, NCOL)]) + _row_tiles(a["ret_w_out"][0])
    tiles += ffn(1, 1)
    w = a["w_in_2"][0]
    at = dict(zip("qa ka va qi ki wi qf kf vf fg qs ks vs gates".split(),
                  np.cumsum([0, 512, 512, 512, 1024, 64, 16, 512, 512, 512, 8, 512, 512, 512])))
    tiles += units(w, [at["va"], at["qi"], at["qi"] + NCOL] + [at[s] for s in "qa ka qf kf vf qs ks vs".split()])
    gate = lambda half, b: units(w, [at["gates"] + b * D + half * NCOL])
    branch = lambda half, b: _column_tiles(np.concatenate([a["w_branch_2"][0, b][:, half * NCOL:(half + 1) * NCOL]] * 2))[:1]
    tiles += gate(0, 0) + gate(0, 1) + gate(0, 2) + branch(0, 0) + branch(0, 1)
    tiles += gate(1, 0) + gate(1, 1) + gate(1, 2) + branch(1, 0) + branch(1, 1) + branch(0, 2) + branch(1, 2)
    tiles += _row_tiles(a["w_out_2"][0])
    up = [_column_tiles(a["w_ff1_2"][0][:, 512 * s:512 * s + 512]) for s in range(FF2_STEPS)]
    down = _row_tiles(a["w_ff2_2"][0])
    tiles += up[0]
    for s in range(1, FF2_STEPS):
        tiles += up[s] + down[2 * s - 2:2 * s]
    tiles += down[-2:]
    small = [w[:, at["ki"]:at["ki"] + HEAD_DIM], w[:, at["wi"]:at["wi"] + IDX_HEADS], w[:, at["fg"]:at["fg"] + HEADS]]
    small = np.concatenate(small + [np.zeros((D, P - HEAD_DIM - IDX_HEADS - HEADS), np.float32)], 1)
    return np.stack(tiles), small


def _constants():
    f = np.float32
    i = np.arange(P)
    square = np.stack([np.eye(P), i[:, None] <= i[None, :], i[:, None] > i[None, :], np.ones((P, P))], 1).astype(f)
    t = np.arange(TOK)
    keep = np.broadcast_to(t % CHUNK != 0, (P, TOK))
    same = (i[:, None] // CHUNK == i[None, :] // CHUNK) & (i[:, None] <= i[None, :])
    gla = np.concatenate([keep] + [same] * GLA_HEADS, 1).astype(f)
    inv = (np.float32(10000.0) ** (-np.arange(0, RET_DK, 2, dtype=f) / f(RET_DK))).astype(f)
    angle = (t.astype(f)[None, :] * inv[:, None]).astype(np.float64)
    log_g = np.log(1.0 - 2.0 ** (-5.0 - np.arange(RET_HEADS)))
    decays = []
    for h in range(RET_HEADS):
        gap = t[None, :] - t[:, None]
        d = np.where(gap >= 0, np.exp(np.maximum(gap, 0) * log_g[h]), 0.0) * RET_DK ** -0.5
        decays += [d[0:P, :], d[P:, P:]]
    ret = np.concatenate([np.cos(angle), np.sin(angle)] + decays, 1).astype(f)
    gap = np.concatenate([i[:, None] - i[None, :], P + i[:, None] - t[None, :]], 1)
    before = np.concatenate([i[:, None] < t[None, :], i[:, None] < i[None, :]], 1)
    att = np.stack([np.where(gap >= 0, 0.0, NEG), -gap, before], 1).astype(f)
    return square, gla, ret, att


def kernel(**inputs):
    import concourse.bacc as _bacc
    from concourse.bass_utils import run_bass_kernel_spmd as _run

    a = {k: np.asarray(v) for k, v in inputs.items()}
    weights, small = _weight_stream(a)
    square, gla, ret, att = _constants()
    gains = [a["ln_g"][i, j] for i in range(2) for j in range(3)] + [a["ln1_g_2"][0], a["ln2_g_2"][0]]
    shifts = [a["ln_b"][i, j] for i in range(2) for j in range(3)] + [a["ln1_b_2"][0], a["ln2_b_2"][0]]
    by_chunk = lambda w: w.reshape(KC, P, -1).transpose(1, 0, 2)
    arrays = {
        "weights": weights,
        "x": a["x"][0].reshape(TB, P, D),
        "constants": square,
        "ln_rows": np.stack([r for g, b in zip(gains, shifts) for r in (g, b)]),
        "gla_w_low": by_chunk(np.concatenate([a["gla_w_in"][0][:, 3 * D:]] * (P // GLA_RANK), 1)),
        "gla_w_gate": a["gla_w_gate"][0],
        "gla_b_gate": a["gla_b_gate"][0].reshape(GLA_HEADS, P).T,
        "gla_constants": gla,
        "gla_gain": a["gla_norm_g"],
        "ret_constants": ret,
        "ret_gain": a["ret_norm_g"],
        "att_w_small": by_chunk(small),
        "att_constants": att,
        "b_forget": a["b_forget_2"],
    }
    nc = _bacc.Bacc("TRN2", target_bir_lowering=False, num_devices=1)
    io, data = {}, {}
    for name, v in arrays.items():
        data[f"in_{name}"] = np.ascontiguousarray(v)
        io[name] = nc.dram_tensor(f"in_{name}", v.shape, F32, kind="ExternalInput").ap()
    io["out"] = nc.dram_tensor("out_0", (TB, P, D), F32, kind="ExternalOutput").ap()
    build(nc, io)
    r = _run(nc, [data], core_ids=[0])
    return r.results[0]["out_0"].reshape(1, TOK, D)
```
